# Optimizing a Trainium2 kernel written in Bass

```python
import math
import jax, jax.numpy as jnp
from jax import lax
import numpy as np
import jax
import jax.numpy as jnp

D_MODEL = 1024
BATCH = 1
SEQ = 512
DEPTH = 1

ROPE_THETA = 10000.0
NORM_EPS = 1e-6
Q_BLOCK = 128

DIFF_HEADS = 4
DIFF_HEAD_DIM = 64
DIFF_V_DIM = 2 * DIFF_HEAD_DIM
DIFF_WIDTH = DIFF_HEADS * DIFF_V_DIM
DIFF_QK_COLS = DIFF_HEADS * 2 * DIFF_HEAD_DIM

MLA_HEADS = 4
MLA_NOPE = 128
MLA_ROPE = 64
MLA_V = 128
MLA_Q_RANK = 384
MLA_KV_RANK = 256
MLA_WIDTH = MLA_HEADS * MLA_V

SPLIT_SIZES = (DIFF_QK_COLS, DIFF_QK_COLS, DIFF_WIDTH, DIFF_WIDTH,
               MLA_Q_RANK, MLA_KV_RANK, MLA_ROPE, MLA_WIDTH,
               D_MODEL, D_MODEL)
IN_COLS = sum(SPLIT_SIZES)


def rms_norm(x, gain):
    xf = x.astype(jnp.float32)
    y = xf * lax.rsqrt(jnp.mean(xf * xf, axis=-1, keepdims=True) + NORM_EPS)
    return (y * gain.astype(jnp.float32)).astype(x.dtype)

def rope_tables(positions, dim):
    inv_freq = ROPE_THETA ** (-jnp.arange(0, dim, 2, dtype=jnp.float32) / dim)
    ang = positions.astype(jnp.float32)[..., None] * inv_freq
    return jnp.cos(ang), jnp.sin(ang)

def apply_rope(x, cos, sin):
    b, s, half = cos.shape
    shape = (b,) + (1,) * (x.ndim - 3) + (s, half)
    c = cos.reshape(shape).astype(x.dtype)
    sn = sin.reshape(shape).astype(x.dtype)
    x1, x2 = x[..., :half], x[..., half:]
    return jnp.concatenate([x1 * c - x2 * sn, x2 * c + x1 * sn], axis=-1)

def causal_multimap_attention(q, k, v, map_weights, scale):
    b, h, m, s, dk = q.shape
    dv = v.shape[-1]
    nb = s // Q_BLOCK
    qb = jnp.moveaxis(q.reshape(b, h, m, nb, Q_BLOCK, dk), 3, 0)
    kpos = jnp.arange(s)
    w = map_weights.astype(jnp.float32)

    def one_block(args):
        q_blk, i = args
        qpos = i * Q_BLOCK + jnp.arange(Q_BLOCK)
        sc = jnp.einsum('bhmqd,bhmkd->bhmqk', q_blk, k).astype(jnp.float32) * scale
        sc = jnp.where(kpos[None, :] <= qpos[:, None], sc, -jnp.inf)
        p = jax.nn.softmax(sc, axis=-1)
        p = jnp.einsum('m,bhmqk->bhqk', w, p)
        return jnp.einsum('bhqk,bhkd->bhqd', p.astype(v.dtype), v)

    out = lax.map(one_block, (qb, jnp.arange(nb)))
    return jnp.moveaxis(out, 0, 2).reshape(b, h, s, dv)

def first_inputs(seed: int = 0) -> dict:
    key = jax.random.key(seed)
    ks = jax.random.split(key, 20)
    L = DEPTH
    nrm = lambda k, shape, fan: jax.random.normal(k, shape, jnp.float32) * fan ** -0.5
    gain = lambda k, n: 1.0 + 0.05 * jax.random.normal(k, (L, n), jnp.float32)
    x = jax.random.normal(ks[0], (BATCH, SEQ, D_MODEL), jnp.float32)
    positions = jnp.broadcast_to(jnp.arange(SEQ, dtype=jnp.int32), (BATCH, SEQ))
    return {
        "x": x,
        "positions": positions,
        "norm_in": gain(ks[1], D_MODEL),
        "w_in": nrm(ks[2], (L, D_MODEL, IN_COLS), D_MODEL),
        "diff_lambda_q1": 0.1 * jax.random.normal(ks[3], (L, DIFF_HEAD_DIM), jnp.float32),
        "diff_lambda_k1": 0.1 * jax.random.normal(ks[4], (L, DIFF_HEAD_DIM), jnp.float32),
        "diff_lambda_q2": 0.1 * jax.random.normal(ks[5], (L, DIFF_HEAD_DIM), jnp.float32),
        "diff_lambda_k2": 0.1 * jax.random.normal(ks[6], (L, DIFF_HEAD_DIM), jnp.float32),
        "diff_subln": gain(ks[7], DIFF_V_DIM),
        "mla_q_norm": gain(ks[8], MLA_Q_RANK),
        "w_uq": nrm(ks[9], (L, MLA_Q_RANK, MLA_HEADS * (MLA_NOPE + MLA_ROPE)), MLA_Q_RANK),
        "mla_kv_norm": gain(ks[10], MLA_KV_RANK),
        "w_ukv": nrm(ks[11], (L, MLA_KV_RANK, MLA_HEADS * (MLA_NOPE + MLA_V)), MLA_KV_RANK),
        "w_proj_diff": nrm(ks[12], (L, DIFF_WIDTH, D_MODEL), DIFF_WIDTH),
        "w_proj_mla": nrm(ks[13], (L, MLA_WIDTH, D_MODEL), MLA_WIDTH),
        "w_out": nrm(ks[14], (L, D_MODEL, D_MODEL), D_MODEL),
        "norm_final": 1.0 + 0.05 * jax.random.normal(ks[15], (D_MODEL,), jnp.float32),
    }

def first_block(x, positions, norm_in, w_in, diff_lambda_q1, diff_lambda_k1,
              diff_lambda_q2, diff_lambda_k2, diff_subln, mla_q_norm, w_uq,
              mla_kv_norm, w_ukv, w_proj_diff, w_proj_mla, w_out, norm_final):
    b, s, _ = x.shape
    cos_d, sin_d = rope_tables(positions, DIFF_HEAD_DIM)
    cos_m, sin_m = rope_tables(positions, MLA_ROPE)
    split_idx = list(np.cumsum(SPLIT_SIZES)[:-1])

    for layer in range(DEPTH):
        lambda_init = 0.8 - 0.6 * math.exp(-0.3 * layer)
        h = rms_norm(x, norm_in[layer])
        proj = h @ w_in[layer]
        (dq, dk, dv, dgate, cq, ckv, kr, mgate, g_diff, g_mla) = jnp.split(proj, split_idx, axis=-1)

        dq = dq.reshape(b, s, DIFF_HEADS, 2, DIFF_HEAD_DIM).transpose(0, 2, 3, 1, 4)
        dk = dk.reshape(b, s, DIFF_HEADS, 2, DIFF_HEAD_DIM).transpose(0, 2, 3, 1, 4)
        dv = dv.reshape(b, s, DIFF_HEADS, DIFF_V_DIM).transpose(0, 2, 1, 3)
        dq = apply_rope(dq, cos_d, sin_d)
        dk = apply_rope(dk, cos_d, sin_d)
        lam = (jnp.exp(jnp.sum(diff_lambda_q1[layer] * diff_lambda_k1[layer]))
               - jnp.exp(jnp.sum(diff_lambda_q2[layer] * diff_lambda_k2[layer]))
               + lambda_init)
        weights = jnp.stack([jnp.ones_like(lam), -lam])
        o_diff = causal_multimap_attention(dq, dk, dv, weights, DIFF_HEAD_DIM ** -0.5)
        o_diff = rms_norm(o_diff, diff_subln[layer]) * (1.0 - lambda_init)
        o_diff = o_diff.transpose(0, 2, 1, 3).reshape(b, s, DIFF_WIDTH)
        o_diff = o_diff * jax.nn.silu(dgate)

        cq = rms_norm(cq, mla_q_norm[layer])
        q = (cq @ w_uq[layer]).reshape(b, s, MLA_HEADS, MLA_NOPE + MLA_ROPE).transpose(0, 2, 1, 3)
        q_nope, q_rope = q[..., :MLA_NOPE], apply_rope(q[..., MLA_NOPE:], cos_m, sin_m)
        ckv = rms_norm(ckv, mla_kv_norm[layer])
        kv = (ckv @ w_ukv[layer]).reshape(b, s, MLA_HEADS, MLA_NOPE + MLA_V).transpose(0, 2, 1, 3)
        k_nope, mv = kv[..., :MLA_NOPE], kv[..., MLA_NOPE:]
        k_rope = apply_rope(kr[:, None], cos_m, sin_m)
        mq = jnp.concatenate([q_nope, q_rope], axis=-1)[:, :, None]
        mk = jnp.concatenate([k_nope, jnp.broadcast_to(k_rope, k_nope.shape[:-1] + (MLA_ROPE,))], axis=-1)[:, :, None]
        o_mla = causal_multimap_attention(mq, mk, mv, jnp.ones((1,), jnp.float32),
                                          (MLA_NOPE + MLA_ROPE) ** -0.5)
        o_mla = o_mla.transpose(0, 2, 1, 3).reshape(b, s, MLA_WIDTH)
        o_mla = o_mla * jax.nn.silu(mgate)

        merged = (jax.nn.sigmoid(g_diff) * (o_diff @ w_proj_diff[layer])
                  + jax.nn.sigmoid(g_mla) * (o_mla @ w_proj_mla[layer]))
        x = x + merged @ w_out[layer]

    return rms_norm(x, norm_final)


GRID_W = 64
CTX_LEN = 256
N_MIXERS = 2
N_HY_LAYERS = (DEPTH + N_MIXERS - 1) // N_MIXERS
N_ML_LAYERS = DEPTH // N_MIXERS
EPS = 1e-6
SHORT_W = 3

HY_EMB_BANDS = 16
HY_EMB_DIM = 1 + 2 * HY_EMB_BANDS
HY_FILTER_WIDTH = 64
HY_MAX_DECAY = math.log(1e-2) / 0.3
HY_MIN_DECAY = math.log(1e-2) / 1.5

ML_INNER = 2 * D_MODEL
ML_HEADS = 4
ML_HEAD_DIM = ML_INNER // ML_HEADS
ML_QKV_BLOCK = 4
ML_N_BLOCKS = ML_INNER // ML_QKV_BLOCK
ML_CHUNK = 128
ML_NORM_EPS = 1e-5

FFN_HIDDEN = 2816


def _f32(a):
    return a.astype(jnp.float32)

def rmsnorm(x, g):
    x32 = _f32(x)
    y = x32 * lax.rsqrt(jnp.mean(x32 * x32, axis=-1, keepdims=True) + EPS)
    return (y * _f32(g)).astype(x.dtype)

def modulate(h, shift, scale):
    return h * (1.0 + scale) + shift

def adaln_params(cond, w, b):
    mod = jax.nn.silu(cond) @ w + b
    return jnp.split(mod[..., None, :], 6, axis=-1)

def short_conv(x, w, b):
    xp = jnp.pad(x, ((0, 0), (1, 1), (0, 0)))
    return w[0] * xp[:, :-2] + w[1] * xp[:, 1:-1] + w[2] * xp[:, 2:] + b

def grid_dwconv(x, w, b, rows, cols):
    B, L, C = x.shape
    img = x.reshape(B, rows, cols, C)
    y = lax.conv_general_dilated(img, w.astype(x.dtype)[:, :, None, :], window_strides=(1, 1),
                                 padding='SAME', dimension_numbers=('NHWC', 'HWIO', 'NHWC'),
                                 feature_group_count=C)
    return y.reshape(B, L, C) + b

def conv_ffn(u, w_up, conv_w, conv_b, w_down, rows, cols):
    a, g = jnp.split(u @ w_up, 2, axis=-1)
    g = grid_dwconv(g, conv_w, conv_b, rows, cols)
    return (jax.nn.silu(g) * a) @ w_down

def hyena_filters(L, f_w1, f_b1, f_w2, f_b2, f_w3, f_b3, f_wout, freq):
    t = jnp.linspace(0.0, 1.0, L, dtype=jnp.float32)[:, None]
    w = 2.0 * math.pi * jnp.arange(L, dtype=jnp.float32)[:, None] / L
    bands = jnp.linspace(1e-4, HY_EMB_BANDS - 1, HY_EMB_BANDS, dtype=jnp.float32)[None, :]
    pos = jnp.concatenate([t, jnp.cos(bands * w), -jnp.sin(bands * w)], axis=-1)
    fr = _f32(freq)
    h = jnp.sin(fr * (pos @ _f32(f_w1) + _f32(f_b1)))
    h = jnp.sin(fr * (h @ _f32(f_w2) + _f32(f_b2)))
    h = jnp.sin(fr * (h @ _f32(f_w3) + _f32(f_b3)))
    h = (h @ _f32(f_wout)).reshape(L, 2, D_MODEL)
    deltas = jnp.linspace(HY_MIN_DECAY, HY_MAX_DECAY, D_MODEL, dtype=jnp.float32)
    h = h * jnp.exp(-t * jnp.abs(deltas))[:, None, :]
    kern = jnp.concatenate([h[:, 0], jnp.zeros((1, D_MODEL), jnp.float32), h[:0:-1, 1]], axis=0)
    return kern / jnp.sum(jnp.abs(kern), axis=0, keepdims=True)

def hyena_mix(u, p):
    (w_in, b_in, sc_w, sc_b, f_w1, f_b1, f_w2, f_b2, f_w3, f_b3, f_wout, freq,
     bias, w_out, b_out) = p
    L = u.shape[1]
    proj = short_conv(u @ w_in + b_in, sc_w, sc_b)
    x0, x1, v = jnp.split(proj, 3, axis=-1)
    kern = hyena_filters(L, f_w1, f_b1, f_w2, f_b2, f_w3, f_b3, f_wout, freq)
    z = _f32(x1 * v)
    y = jnp.fft.irfft(jnp.fft.rfft(z, n=2 * L, axis=1) * jnp.fft.rfft(kern, n=2 * L, axis=0)[None],
                      n=2 * L, axis=1)[:, :L]
    y = (y + z * _f32(bias)).astype(u.dtype)
    return (x0 * y) @ w_out + b_out

def headwise(a, w):
    B, L, _ = a.shape
    out = jnp.einsum('blnc,nce->blne', a.reshape(B, L, ML_N_BLOCKS, ML_QKV_BLOCK), w)
    return out.reshape(B, L, ML_INNER)

def to_heads(a):
    B, L, _ = a.shape
    return _f32(a).reshape(B, L, ML_HEADS, ML_HEAD_DIM).transpose(0, 2, 1, 3)

def mlstm_chunkwise(q, k, v, ig, lf, state):
    B, H, L, dh = q.shape
    nc = L // ML_CHUNK

    def chunks(a):
        return jnp.moveaxis(a.reshape(B, H, nc, ML_CHUNK, *a.shape[3:]), 2, 0)

    lower = jnp.tril(jnp.ones((ML_CHUNK, ML_CHUNK), dtype=bool))

    def step(carry, xs):
        C, n, m = carry
        qc, kc, vc, igc, lfc = xs
        b = jnp.cumsum(lfc, axis=-1)
        a_inter = b + m[..., None]
        d = jnp.where(lower, b[..., :, None] - b[..., None, :] + igc[..., None, :], -jnp.inf)
        m_row = jnp.maximum(a_inter, jnp.max(d, axis=-1))
        w_inter = jnp.exp(a_inter - m_row)
        s = jnp.einsum('bhid,bhjd->bhij', qc, kc) * jnp.exp(d - m_row[..., None])
        num = (w_inter[..., None] * jnp.einsum('bhed,bhid->bhie', C, qc)
               + jnp.einsum('bhij,bhje->bhie', s, vc))
        den = w_inter * jnp.einsum('bhd,bhid->bhi', n, qc) + jnp.sum(s, axis=-1)
        h = num / jnp.maximum(jnp.abs(den), jnp.exp(-m_row))[..., None]
        b_last = b[..., -1]
        e = b_last[..., None] - b + igc
        m_new = jnp.maximum(b_last + m, jnp.max(e, axis=-1))
        g_old = jnp.exp(b_last + m - m_new)
        w_new = jnp.exp(e - m_new[..., None])
        C_new = g_old[..., None, None] * C + jnp.einsum('bhje,bhjd->bhed', vc * w_new[..., None], kc)
        n_new = g_old[..., None] * n + jnp.einsum('bhj,bhjd->bhd', w_new, kc)
        return (C_new, n_new, m_new), h

    state, h = lax.scan(step, state, (chunks(q), chunks(k), chunks(v), chunks(ig), chunks(lf)))
    return jnp.moveaxis(h, 0, 2).reshape(B, H, L, dh), state

def mlstm_final_state(k, v, ig, lf):
    b = jnp.cumsum(lf, axis=-1)
    b_last = b[..., -1]
    e = b_last[..., None] - b + ig
    m = jnp.maximum(b_last, jnp.max(e, axis=-1))
    w = jnp.exp(e - m[..., None])
    return (jnp.einsum('bhje,bhjd->bhed', v * w[..., None], k),
            jnp.einsum('bhj,bhjd->bhd', w, k), m)

def mlstm_prep(u, w_in, conv_w, conv_b, wq, wk, wv, w_gate, b_gate):
    B, L, _ = u.shape
    xm, z = jnp.split(u @ w_in, 2, axis=-1)
    xc = jax.nn.silu(short_conv(xm, conv_w, conv_b))
    q = headwise(xc, wq)
    k = headwise(xc, wk)
    v = headwise(xm, wv)
    gates = (q @ w_gate[:ML_INNER] + k @ w_gate[ML_INNER:2 * ML_INNER]
             + v @ w_gate[2 * ML_INNER:] + b_gate)
    gates = jnp.transpose(_f32(gates).reshape(B, L, 2, 2, ML_HEADS), (2, 3, 0, 4, 1))
    ig = gates[:, 0]
    lf = jax.nn.log_sigmoid(gates[:, 1])
    return to_heads(q), to_heads(k) * (ML_HEAD_DIM ** -0.5), to_heads(v), ig, lf, xc, z

def mlstm_out(h, xc, z, norm_w, skip, w_down):
    B, H, L, dh = h.shape
    mu = jnp.mean(h, axis=-1, keepdims=True)
    var = jnp.mean(jnp.square(h - mu), axis=-1, keepdims=True)
    hn = ((h - mu) * lax.rsqrt(var + ML_NORM_EPS)).transpose(0, 2, 1, 3).reshape(B, L, H * dh)
    hs = (hn * _f32(norm_w)).astype(xc.dtype) + skip * xc
    return (hs * jax.nn.silu(z)) @ w_down

def mlstm_mix(u_lat, u_ctx, p, need_ctx):
    w_in, conv_w, conv_b, wq, wk, wv, w_gate, b_gate, norm_w, skip, w_down = p

    def prep(u):
        return mlstm_prep(u, w_in, conv_w, conv_b, wq, wk, wv, w_gate, b_gate)

    def flip(a):
        return jnp.flip(a, axis=2)

    q, k, v, ig, lf, xc, z = prep(u_lat)
    qc, kc, vc, igc, lfc, xcc, zc = prep(u_ctx)
    if need_ctx:
        B = u_ctx.shape[0]
        zero = (jnp.zeros((B, ML_HEADS, ML_HEAD_DIM, ML_HEAD_DIM), jnp.float32),
                jnp.zeros((B, ML_HEADS, ML_HEAD_DIM), jnp.float32),
                jnp.zeros((B, ML_HEADS), jnp.float32))
        hcf, st_f = mlstm_chunkwise(qc, kc, vc, igc[0], lfc[0], zero)
        hcb, st_b = mlstm_chunkwise(flip(qc), flip(kc), flip(vc), flip(igc[1]), flip(lfc[1]), zero)
        y_ctx = mlstm_out(hcf + flip(hcb), xcc, zc, norm_w, skip, w_down)
    else:
        st_f = mlstm_final_state(kc, vc, igc[0], lfc[0])
        st_b = mlstm_final_state(flip(kc), flip(vc), flip(igc[1]), flip(lfc[1]))
        y_ctx = None
    hf, _ = mlstm_chunkwise(q, k, v, ig[0], lf[0], st_f)
    hb, _ = mlstm_chunkwise(flip(q), flip(k), flip(v), flip(ig[1]), flip(lf[1]), st_b)
    y_lat = mlstm_out(hf + flip(hb), xc, z, norm_w, skip, w_down)
    return y_lat, y_ctx

def second_inputs(seed: int = 0) -> dict:
    key = jax.random.key(seed)
    keys = iter(jax.random.split(key, 48))

    def nrm(shape, scale):
        return jax.random.normal(next(keys), shape, dtype=jnp.float32) * scale

    D, NH, NM = D_MODEL, N_HY_LAYERS, N_ML_LAYERS
    fb = jnp.linspace(3.0, 6.0, ML_HEADS, dtype=jnp.float32)
    ml_b_gate = jnp.stack([nrm((NM, 2, ML_HEADS), 0.1), fb + nrm((NM, 2, ML_HEADS), 0.1)],
                          axis=2).reshape(NM, 4 * ML_HEADS)
    return {
        'x': nrm((BATCH, SEQ, D), 1.0),
        'c': nrm((BATCH, D), 1.0),
        'ctx': nrm((BATCH, CTX_LEN, D), 1.0),
        'c_ctx': nrm((D,), 1.0),
        'mod_w': nrm((DEPTH, D, 6 * D), 0.5 * D ** -0.5),
        'mod_b': nrm((DEPTH, 6 * D), 0.02),
        'norm_g': 1.0 + nrm((DEPTH, 2, D), 0.02),
        'final_g': 1.0 + nrm((D,), 0.02),
        'hy_w_in': nrm((NH, D, 3 * D), D ** -0.5),
        'hy_b_in': nrm((NH, 3 * D), 0.02),
        'hy_sc_w': nrm((NH, SHORT_W, 3 * D), SHORT_W ** -0.5),
        'hy_sc_b': nrm((NH, 3 * D), 0.02),
        'hy_f_w1': nrm((NH, HY_EMB_DIM, HY_FILTER_WIDTH), HY_EMB_DIM ** -0.5),
        'hy_f_b1': nrm((NH, HY_FILTER_WIDTH), 0.1),
        'hy_f_w2': nrm((NH, HY_FILTER_WIDTH, HY_FILTER_WIDTH), HY_FILTER_WIDTH ** -0.5),
        'hy_f_b2': nrm((NH, HY_FILTER_WIDTH), 0.1),
        'hy_f_w3': nrm((NH, HY_FILTER_WIDTH, HY_FILTER_WIDTH), HY_FILTER_WIDTH ** -0.5),
        'hy_f_b3': nrm((NH, HY_FILTER_WIDTH), 0.1),
        'hy_f_wout': nrm((NH, HY_FILTER_WIDTH, 2 * D), HY_FILTER_WIDTH ** -0.5),
        'hy_freq': 1.0 + nrm((NH, HY_FILTER_WIDTH), 0.1),
        'hy_bias': nrm((NH, D), 0.2),
        'hy_w_out': nrm((NH, D, D), D ** -0.5),
        'hy_b_out': nrm((NH, D), 0.02),
        'ml_w_in': nrm((NM, D, 2 * ML_INNER), D ** -0.5),
        'ml_conv_w': nrm((NM, SHORT_W, ML_INNER), SHORT_W ** -0.5),
        'ml_conv_b': nrm((NM, ML_INNER), 0.02),
        'ml_wq': nrm((NM, ML_N_BLOCKS, ML_QKV_BLOCK, ML_QKV_BLOCK), ML_QKV_BLOCK ** -0.5),
        'ml_wk': nrm((NM, ML_N_BLOCKS, ML_QKV_BLOCK, ML_QKV_BLOCK), ML_QKV_BLOCK ** -0.5),
        'ml_wv': nrm((NM, ML_N_BLOCKS, ML_QKV_BLOCK, ML_QKV_BLOCK), ML_QKV_BLOCK ** -0.5),
        'ml_w_gate': nrm((NM, 3 * ML_INNER, 4 * ML_HEADS), 0.1 * (3 * ML_INNER) ** -0.5),
        'ml_b_gate': ml_b_gate,
        'ml_norm_w': 1.0 + nrm((NM, ML_INNER), 0.02),
        'ml_skip': 1.0 + nrm((NM, ML_INNER), 0.02),
        'ml_w_down': nrm((NM, ML_INNER, D), ML_INNER ** -0.5),
        'ffn_w_up': nrm((DEPTH, D, 2 * FFN_HIDDEN), D ** -0.5),
        'ffn_conv_w': nrm((DEPTH, 3, 3, FFN_HIDDEN), 1.0 / 3.0),
        'ffn_conv_b': nrm((DEPTH, FFN_HIDDEN), 0.02),
        'ffn_w_down': nrm((DEPTH, FFN_HIDDEN, D), FFN_HIDDEN ** -0.5),
    }

def second_block(x, c, ctx, c_ctx, mod_w, mod_b, norm_g, final_g,
              hy_w_in, hy_b_in, hy_sc_w, hy_sc_b, hy_f_w1, hy_f_b1, hy_f_w2, hy_f_b2,
              hy_f_w3, hy_f_b3, hy_f_wout, hy_freq, hy_bias, hy_w_out, hy_b_out,
              ml_w_in, ml_conv_w, ml_conv_b, ml_wq, ml_wk, ml_wv, ml_w_gate, ml_b_gate,
              ml_norm_w, ml_skip, ml_w_down,
              ffn_w_up, ffn_conv_w, ffn_conv_b, ffn_w_down):
    rows = x.shape[1] // GRID_W
    ctx_len = ctx.shape[1]
    hy_params = (hy_w_in, hy_b_in, hy_sc_w, hy_sc_b, hy_f_w1, hy_f_b1, hy_f_w2, hy_f_b2,
                 hy_f_w3, hy_f_b3, hy_f_wout, hy_freq, hy_bias, hy_w_out, hy_b_out)
    ml_params = (ml_w_in, ml_conv_w, ml_conv_b, ml_wq, ml_wk, ml_wv, ml_w_gate, ml_b_gate,
                 ml_norm_w, ml_skip, ml_w_down)
    for i in range(DEPTH):
        last = i == DEPTH - 1
        sh1, sc1, g1, sh2, sc2, g2 = adaln_params(c, mod_w[i], mod_b[i])
        csh1, csc1, cg1, csh2, csc2, cg2 = adaln_params(c_ctx, mod_w[i], mod_b[i])
        h_lat = modulate(rmsnorm(x, norm_g[i, 0]), sh1, sc1)
        h_ctx = modulate(rmsnorm(ctx, norm_g[i, 0]), csh1, csc1)
        j = i // N_MIXERS
        if i % N_MIXERS == 0:
            p = tuple(a[j] for a in hy_params)
            y_lat = hyena_mix(h_lat, p)
            y_ctx = None if last else hyena_mix(h_ctx, p)
        else:
            p = tuple(a[j] for a in ml_params)
            y_lat, y_ctx = mlstm_mix(h_lat, h_ctx, p, not last)
        x = x + g1 * y_lat
        ffn_p = (ffn_w_up[i], ffn_conv_w[i], ffn_conv_b[i], ffn_w_down[i])
        x = x + g2 * conv_ffn(modulate(rmsnorm(x, norm_g[i, 1]), sh2, sc2), *ffn_p, rows, GRID_W)
        if not last:
            ctx = ctx + cg1 * y_ctx
            ctx = ctx + cg2 * conv_ffn(modulate(rmsnorm(ctx, norm_g[i, 1]), csh2, csc2),
                                       *ffn_p, 1, ctx_len)
    return rmsnorm(x, final_g)


def setup_inputs(seed=0):
    out = dict(first_inputs(seed))
    for name, value in second_inputs(seed + 1).items():
        if name != "x":
            out[name + "_2"] = value
    return out


def reference(
    x, positions, norm_in, w_in, diff_lambda_q1, diff_lambda_k1, diff_lambda_q2, diff_lambda_k2,
    diff_subln, mla_q_norm, w_uq, mla_kv_norm, w_ukv, w_proj_diff, w_proj_mla, w_out,
    norm_final, c_2, ctx_2, c_ctx_2, mod_w_2, mod_b_2, norm_g_2, final_g_2, hy_w_in_2,
    hy_b_in_2, hy_sc_w_2, hy_sc_b_2, hy_f_w1_2, hy_f_b1_2, hy_f_w2_2, hy_f_b2_2, hy_f_w3_2,
    hy_f_b3_2, hy_f_wout_2, hy_freq_2, hy_bias_2, hy_w_out_2, hy_b_out_2, ml_w_in_2,
    ml_conv_w_2, ml_conv_b_2, ml_wq_2, ml_wk_2, ml_wv_2, ml_w_gate_2, ml_b_gate_2, ml_norm_w_2,
    ml_skip_2, ml_w_down_2, ffn_w_up_2, ffn_conv_w_2, ffn_conv_b_2, ffn_w_down_2,
):
    x = first_block(
        x, positions, norm_in, w_in, diff_lambda_q1, diff_lambda_k1, diff_lambda_q2,
        diff_lambda_k2, diff_subln, mla_q_norm, w_uq, mla_kv_norm, w_ukv, w_proj_diff,
        w_proj_mla, w_out, norm_final,
    )
    return second_block(
        x, c_2, ctx_2, c_ctx_2, mod_w_2, mod_b_2, norm_g_2, final_g_2, hy_w_in_2, hy_b_in_2,
        hy_sc_w_2, hy_sc_b_2, hy_f_w1_2, hy_f_b1_2, hy_f_w2_2, hy_f_b2_2, hy_f_w3_2, hy_f_b3_2,
        hy_f_wout_2, hy_freq_2, hy_bias_2, hy_w_out_2, hy_b_out_2, ml_w_in_2, ml_conv_w_2,
        ml_conv_b_2, ml_wq_2, ml_wk_2, ml_wv_2, ml_w_gate_2, ml_b_gate_2, ml_norm_w_2,
        ml_skip_2, ml_w_down_2, ffn_w_up_2, ffn_conv_w_2, ffn_conv_b_2, ffn_w_down_2,
    )


_drawn_inputs = setup_inputs


def setup_inputs(seed=0):
    import zlib

    import numpy as np

    out = dict(_drawn_inputs(seed))
    spreads = {}
    factors = {'diff_lambda_q1': 8.0,
     'diff_lambda_k1': 5.835,
     'diff_lambda_q2': 200.0,
     'diff_lambda_k2': 2.683,
     'diff_subln': 4.235,
     'mla_q_norm': 8.0,
     'mla_kv_norm': 8.0,
     'mod_b_2': 3.383,
     'norm_g_2': 8.0,
     'final_g_2': 19.799,
     'hy_b_in_2': 8.0,
     'hy_sc_b_2': 8.0,
     'hy_f_b1_2': 8.0,
     'hy_f_b2_2': 7.698,
     'hy_f_b3_2': 7.082,
     'hy_freq_2': 8.0,
     'hy_b_out_2': 200.0,
     'ffn_conv_b_2': 59.027}
    for name, (base, spread) in spreads.items():
        noise = np.random.default_rng([zlib.crc32(name.encode()), seed]).standard_normal(out[name].shape)
        drawn = base * np.exp(spread * noise) if base else spread * noise
        out[name] = jnp.asarray(drawn.astype(out[name].dtype))
    for name, factor in factors.items():
        out[name] = (out[name] * factor).astype(out[name].dtype)
    return out
```

```python
from contextlib import ExitStack
import math

import numpy as np
import concourse.bass as bass
from concourse import mybir

F32 = mybir.dt.float32
BF16 = mybir.dt.bfloat16
I32 = mybir.dt.int32
ALU = mybir.AluOpType
ACT = mybir.ActivationFunctionType
AX = mybir.AxisListType

P = 128
SEQ, D = 512, 1024
TT = SEQ // P
KD = D // P
NORM_EPS = 1e-6
HEADS = 4
HALF = 32
UNITS = 2 * HEADS
Q_RANK, KV_RANK = 384, 256
KQ, KKV = Q_RANK // P, KV_RANK // P
DIFF_SCALE = 64 ** -0.5
MLA_SCALE = 192 ** -0.5
LAMBDA_INIT = 0.8 - 0.6 * math.exp(0.0)
FFN = 2816
KF = FFN // P
ROWS, COLS = SEQ // 64, 64
BANDS = 16
EMB = 1 + 2 * BANDS
FW = 64
NF = SEQ // 2
SLOT = 4096
RING = 3
MASKED = -1e30
MOD_POOL_COLS = 128
MOD_POOL = 3 * D // MOD_POOL_COLS
MOD_DVE_COLS = 256
MOD_DVE = 3 * D // MOD_DVE_COLS

TWO_PI = 2.0 * math.pi
PI_1 = 6.28125
PI_2 = float(np.float32(np.round((TWO_PI - PI_1) * 2 ** 20) / 2 ** 20))
PI_3 = float(np.float32(TWO_PI - PI_1 - PI_2))
ROUNDER = 1.5 * 2.0 ** 23
PI_BELOW = float(np.nextafter(np.float32(math.pi), np.float32(0)))

SMALL = {}
_at = 0
for _name, _n in (("norm_in", KD), ("norm_g1", KD), ("norm_g2", KD), ("q_norm", KQ), ("kv_norm", KKV),
                  ("hy_b_in", 24), ("hy_sc_w", 72), ("hy_sc_b", 24), ("conv_w", 9 * KF), ("conv_b", KF),
                  ("cond", KD), ("minus_t", TT), ("ident", P)):
    SMALL[_name] = slice(_at, _at + _n)
    _at += _n
N_SMALL = _at

EARLY = {}
_at = 0
for _name, _n in (("pos_emb", SEQ), ("f_w1", FW), ("f_w2", FW), ("f_w3", FW), ("f_b", 3), ("freq", 1)):
    EARLY[_name] = slice(_at, _at + _n)
    _at += _n
N_EARLY = _at
ROWED = {}
_at = 0
for _name, _n in (("inv_freq", HALF), ("lam", 4 * 64), ("subln", P)):
    ROWED[_name] = slice(_at, _at + _n)
    _at += _n
N_ROWED = _at

(C_DQ, C_DK, C_DV, C_LAT0, C_LAT1, C_DGATE, C_UQ, C_UKV, C_MGATE, C_GD0, C_GD1, C_GM0, C_GM1,
 C_PD, C_PM, C_WO0, C_WO1, C_FOUT, C_HYZ0) = range(19)
C_HYX0 = C_HYZ0 + 4
C_HYO = C_HYX0 + 2
C_UP = C_HYO + 2
C_DOWN = C_UP + KF // 2
DOWN_K = (8, 8, 6)
N_CHUNKS = C_DOWN + 2 * len(DOWN_K)


def build_program(nc, x_d, pos_d, stream_d, mod_d, mod_b_d, small_d, early_d, rowed_d, masks_d,
                  tables_d, deltas_d, rows_d, out_d):
    ctx = ExitStack()
    sems = {}

    def sem(name):
        if name not in sems:
            sems[name] = ctx.enter_context(nc.semaphore(name))
        return sems[name]

    with ctx:
        def sb(name, shape, dt=F32):
            return ctx.enter_context(nc.sbuf_tensor(name, shape, dt))

        x_sb = sb("x_sb", [P, TT, D])
        hT = sb("hT", [P, KD, SEQ])
        ring = sb("ring", [P, RING, SLOT])
        mod_g = sb("mod_g", [P, 2, D])
        row = sb("row", [P, D])
        small = sb("small", [P, N_SMALL])
        pos_sb = sb("pos_sb", [P, TT], I32)
        masks = sb("masks", [P, 2, P], BF16)
        stat = sb("stat", [P, 96])
        sums = sb("sums", [P, 64])
        modc = sb("modc", [P, 4 * KD])
        arena = sb("arena", [P, 111 * 256])
        bank = [ctx.enter_context(nc.psum_tensor(f"bank{i}", [P, 512], F32))[:, :] for i in range(8)]

        def at(kb, n, tiles=None):
            ap = arena[:, int(kb * 256):int(kb * 256) + n]
            return ap if tiles is None else ap.rearrange("p (a b) -> p a b", a=tiles)

        ident = small[:, SMALL["ident"]]

        def sm(name, i, parts=P):
            c = SMALL[name].start + i
            return small[0:parts, c:c + 1]

        qT = at(0, 2048, HEADS)
        kT = at(8, 2048, HEADS)
        dv = at(16, 2048, TT)
        qn = at(24, 2048, HEADS)
        kn = at(32, 2048, HEADS)
        mv = at(40, 2048, TT)
        qrT = at(48, 1024, 2)
        krT = at(52, 512)
        early = at(24, N_EARLY)
        net = [at(27 + 2 * i, 512) for i in range(4)]
        lat = at(54, TT * 704, TT)
        cqT = at(65, KQ * SEQ, KQ)
        ckvT = at(71, KKV * SEQ, KKV)
        roped = [at(75, 2048, TT), at(83, 2048, TT)]
        kr2 = at(83, TT * P, TT)
        qr = at(85, 1024, TT)
        dgate = at(75, 2048, TT)
        mgate = at(83, 2048, TT)
        modw_pool = [at(91, 1024, KD), at(95, 1024, KD)]
        modw_dve = at(99, 2048, KD)
        rowed = at(107, N_ROWED)
        cos_t, sin_t, nsin_t = (at(109 + 0.5 * i, 128) for i in range(3))
        probs1 = [at(54, 1280), at(59, 1280)]
        probs2 = at(64, 1280)
        pT = [at(69, 512), at(71, 512)]
        o_sq = at(73, 512, TT)
        o_tok = [at(107, 512, TT), at(109, 512, TT)]
        sgd = at(91, KD * SEQ, KD)
        sgm = at(32, KD * SEQ, KD)
        junk = at(54, D)
        x_norm = at(16, TT * D, TT)
        norm_row = at(48, D)
        filt = [hT[:, i, :] for i in range(4)]
        abs_sum = [hT[:, 4 + n, :] for n in range(2)]
        deltas = hT[:, 6:8, :].rearrange("p a b -> p (a b)")
        bias_row = at(107, D)[0:1, :]
        norm_sb = at(58, D)[0:1, :]
        decay = [at(62 + 2 * i, 512) for i in range(2)]
        abs_tap = [at(66 + 2 * i, 512) for i in range(2)]
        ones_sq = at(109, P)
        z_buf = [at(52, 512), at(107, 512)]
        x1c, vc = at(48, 512), at(50, 512)
        h3T = row[0:FW, 0:SEQ]
        rope_tmp = row[:, SEQ:D]
        fwd_cos = at(75, 1024, 4)
        fwd_sin = at(79, 1024, 4)
        inv = at(83, 2048, 8)
        kp = at(58, 4096, 4)
        km = at(91, 4096, 4)
        x0c = at(0, KD * SEQ, KD)
        zT = at(16, 4096, 4)
        uv = at(32, 4096, 8)
        padded = [row[:, 0:SEQ + 2], at(55, SEQ + 2)]
        tmp = [at(48 + 2 * i, 512) for i in range(5)] + [at(107 + 2 * i, 512) for i in range(2)]
        hid = at(0, KF * SEQ, KF)
        image = [at(44 + 3 * i, (ROWS + 2) * (COLS + 2)).rearrange("p (r c) -> p r c", c=COLS + 2) for i in range(2)]
        conv = [at(50 + 2 * i, 512) for i in range(2)]
        out_tok = [at(60 + 4 * i, D) for i in range(2)]

        SS, RS, SS_L, RS_L, SS_H, RS_H, SS2, RS2 = 0, 4, 8, 16, 24, 32, 40, 44
        MHALF, ONE, NLAM, CSILU, RNORM = 64, 68, 69, 70, 78

        def st(c, n=1, parts=P):
            return stat[0:parts, c:c + n]

        def chunk(c):
            return ring[:, c % RING, :]

        def chunk_landed(eng, c):
            eng.wait_ge(sem(f"chunk_landed{c % RING}"), 16 * (c // RING + 1))

        OFF = [0, 128, 384, 768]

        def score_place(a, i):
            return ((2 + a, 384), (4, 256 * a), (2 + a, 0), (a, 0))[i]

        chunk_used = {C_DQ: ("in_done", 4), C_DK: ("in_done", 8), C_DV: ("in_done", 12),
                      C_LAT0: ("in_done", 16), C_LAT1: ("in_done", 20), C_UQ: ("latq_done", 8),
                      C_UKV: ("latk_done", 8), C_DGATE: ("dgate_done", 4), C_MGATE: ("fill_done", 4),
                      C_GD0: ("fill_done", 8), C_GD1: ("gate_done", 4), C_GM0: ("gate_done", 8),
                      C_GM1: ("gate_done", 12), C_PD: ("merge_done", 16), C_PM: ("merge_done", 16),
                      C_WO0: ("wo_done", 8), C_WO1: ("wo_done", 8), C_FOUT: ("taps_done", 8)}
        for c in range(4):
            chunk_used[C_HYZ0 + c] = ("hyz_done", 4 * c + 4)
        for c in range(2):
            chunk_used[C_HYX0 + c] = ("hyx_done", 4 * c + 4)
            chunk_used[C_HYO + c] = ("hyo_done", 8)
        for c in range(KF // 2):
            chunk_used[C_UP + c] = ("up_done", 4 * c + 4)
        for c in range(6):
            chunk_used[C_DOWN + c] = ("down_chunk_done", c + 1)

        def exps_before(u):
            return 8 * min(u, HEADS) + 4 * max(u - HEADS, 0)

        def scores_at(u):
            return 2 * u + 2 if u < HEADS else 2 * HEADS + u - HEADS + 1

        def squares_at(name, i):
            if name == "x1":
                return 12 + max(2 * i, 1)
            if name == "x2":
                return min(15 + 2 * i, 20)
            return {"n1": 1, "lat": 5, "x3": 21, "x4": 25}[name] + i

        def mod_acc(j):
            return x_sb[:, j // KD, (j % KD) * P:(j % KD + 1) * P]

        def taps(d, n):
            return at((32, 0)[n] + 8 * d, 2048, 4)

        block = ctx.enter_context(nc.Block())

        @block.sync
        def _(sp):
            for m in range(TT):
                sp.dma_start(x_sb[:, m, :], x_d[m * P:(m + 1) * P, :]).then_inc(sem(f"x_in{m}"), 16)
            for c in range(N_CHUNKS):
                if c >= RING:
                    name, count = chunk_used[c - RING]
                    sp.wait_ge(sem(name), count)
                sp.dma_start(chunk(c), stream_d[c]).then_inc(sem(f"chunk_landed{c % RING}"), 16)
            for m in range(TT):
                sp.wait_ge(sem("y_ready"), m + 1)
                sp.dma_start(out_d[m * P:(m + 1) * P, :], out_tok[m % 2]).then_inc(sem(f"y_stored{m % 2}"), 16)
            for i in range(2):
                sp.wait_ge(sem(f"y_stored{i}"), 16 * TT // 2)

        @block.tensor
        def _(pe):
            held = {}

            def take(b, name, count):
                if b in held and held[b] != (name, count):
                    pe.wait_ge(sem(held[b][0]), held[b][1])
                held[b] = (name, count)

            def product(out, pairs):
                for n, (l, r) in enumerate(pairs):
                    ins = nc.tensor.matmul(out, l, r, start=n == 0, stop=n == len(pairs) - 1)
                return ins

            def turn(b, blocks):
                for n, x in enumerate(blocks):
                    ins = nc.tensor.transpose(bank[b][0:x.shape[1], n * P:(n + 1) * P], x, ident)
                return ins

            def tok(k, m):
                return hT[:, k, m * P:(m + 1) * P]

            def cols(c, k, a, n, width=512):
                return chunk(c)[:, k * width + a:k * width + a + n]

            pe.wait_ge(sem("small_in"), 16)
            pe.wait_ge(sem("n1_scaled"), TT)
            for k in range(KD):
                take(k % 4, "n1_out", k + 1)
                turn(k % 4, [x_sb[:, m, k * P:(k + 1) * P] for m in range(TT)]).then_inc(sem("n1_turned"), 1)
            pe.wait_ge(sem("n1_out"), KD)

            pe.wait_ge(sem("early_in"), 16)

            def net_layer(i):
                take(i, "net_read", i + 1)
                w = early[0:(EMB, FW, FW)[i], EARLY[f"f_w{i + 1}"]]
                if i:
                    pe.wait_ge(sem("net_out"), i)
                x = early[0:EMB, EARLY["pos_emb"]] if i == 0 else net[0][0:FW, :]
                nc.tensor.matmul(bank[i][0:FW, :], w, x, start=True, stop=True).then_inc(sem("net_done"), 1)

            def input_chunk(c, i0, width):
                chunk_landed(pe, c)
                for m in range(TT):
                    i = i0 + m
                    take(4 + i % 4, "rope_out" if i < 8 else "in_out", i + 1 if i < 8 else i - 7)
                    product(bank[4 + i % 4][:, 0:width],
                            [(tok(k, m), cols(c, k, 0, width, width)) for k in range(KD)]).then_inc(sem("in_done"), 1)

            net_layer(0)
            input_chunk(C_DQ, 0, 512)
            net_layer(1)
            input_chunk(C_DK, 4, 512)
            net_layer(2)
            input_chunk(C_DV, 8, 512)

            def turn_roped(t):
                pe.wait_ge(sem("rope_out"), 4 * t + 4)
                for h in range(HEADS):
                    i = 4 * t + h
                    take(i % 4, "qk_out", i + 1)
                    turn(i % 4, [roped[t][:, m, h * P:(h + 1) * P] for m in range(TT)]).then_inc(sem("qk_turned"), 1)

            turn_roped(0)
            input_chunk(C_LAT0, 12, 352)
            input_chunk(C_LAT1, 16, 352)
            turn_roped(1)
            chunk_landed(pe, C_DGATE)
            for m in range(TT):
                take(4 + m, "dgate_out", m + 1)
                product(bank[4 + m], [(tok(k, m), cols(C_DGATE, k, 0, 512)) for k in range(KD)]).then_inc(sem("dgate_done"), 1)
            pe.wait_ge(sem("kr_ready"), 1)
            take(0, "lat_out", 1)
            turn(0, [kr2[:, m, :] for m in range(TT)]).then_inc(sem("lat_turned"), 1)
            pe.wait_ge(sem("lat_scaled"), 2)
            for i in range(KQ + KKV):
                take((i + 1) % 4, "lat_out", i + 2)
                turn((i + 1) % 4, [lat[:, m, i * P:(i + 1) * P] for m in range(TT)]).then_inc(sem("lat_turned"), 1)
            pe.wait_ge(sem("lat_out"), 1 + KQ)
            chunk_landed(pe, C_UQ)
            for m in range(TT):
                take(4 + m, "qr_out", m + 1)
                product(bank[4 + m][:, 0:256], [(cqT[:, k, m * P:(m + 1) * P], cols(C_UQ, k, 512, 256, 768))
                                                for k in range(KQ)]).then_inc(sem("latq_done"), 1)
            for h in range(HEADS):
                take(4 + h, "qn_out", h + 1)
                product(bank[4 + h], [(cols(C_UQ, k, h * P, P, 768), cqT[:, k, :]) for k in range(KQ)]).then_inc(sem("latq_done"), 1)
            pe.wait_ge(sem("lat_out"), 1 + KQ + KKV)
            chunk_landed(pe, C_UKV)
            for h in range(HEADS):
                take(4 + h, "latk_out", h + 1)
                product(bank[4 + h], [(cols(C_UKV, k, h * P, P, 1024), ckvT[:, k, :]) for k in range(KKV)]).then_inc(sem("latk_done"), 1)
            for m in range(TT):
                take(4 + m, "latk_out", HEADS + m + 1)
                product(bank[4 + m], [(ckvT[:, k, m * P:(m + 1) * P], cols(C_UKV, k, 512, 512, 1024))
                                      for k in range(KKV)]).then_inc(sem("latk_done"), 1)
            pe.wait_ge(sem("qr_out"), TT)
            for b in range(2):
                take(b, "qrT_out", b + 1)
                turn(b, [qr[:, m, b * P:(b + 1) * P] for m in range(TT)]).then_inc(sem("qr_turned"), 1)

            pe.wait_ge(sem("masks_in"), 16)

            def scores(u):
                latent, h = u >= HEADS, u % HEADS
                if u == 0:
                    pe.wait_ge(sem("qk_out"), 8)
                if u == HEADS:
                    pe.wait_ge(sem("latk_out"), 2 * HEADS)
                    pe.wait_ge(sem("qn_out"), HEADS)
                    pe.wait_ge(sem("qrT_out"), 2)
                done = exps_before(u + 1)
                for b in range(5):
                    take(b, "exp_out", done)
                for a in range(1 if latent else 2):
                    for i in (0, 2, 3, 1):
                        if a == 1 and i == 1:
                            pe.wait_ge(sem("scores_done"), 2 * u + 1)
                        b, c = score_place(a, i)
                        n = (i + 1) * P
                        out = bank[b][:, c:c + n]
                        q = slice(i * P, (i + 1) * P)
                        if latent:
                            half = slice(64 * (h % 2), 64 * (h % 2) + 64)
                            nc.tensor.matmul(out, qn[:, h, q], kn[:, h, 0:n], start=True, stop=False)
                            nc.tensor.matmul(out, qrT[half, h // 2, q], krT[half, 0:n], start=False, stop=False)
                        else:
                            half = slice(64 * a, 64 * a + 64)
                            nc.tensor.matmul(out, qT[half, h, q], kT[half, h, 0:n], start=True, stop=False)
                        ins = nc.tensor.matmul(bank[b][:, c + i * P:c + n], masks[:, 0, :], masks[:, 1, :],
                                               start=False, stop=True)
                    ins.then_inc(sem("scores_done"), 1)

            def fill(u):
                b = 5
                take(b, "fill_out", u + 1)
                if u < 4:
                    chunk_landed(pe, C_MGATE)
                    ins = product(bank[b], [(tok(k, u), cols(C_MGATE, k, 0, 512)) for k in range(KD)])
                else:
                    chunk_landed(pe, C_GD0)
                    ins = product(bank[b], [(cols(C_GD0, k, (u - 4) * P, P), hT[:, k, :]) for k in range(KD)])
                ins.then_inc(sem("fill_done"), 1)

            def values(u):
                latent, h = u >= HEADS, u % HEADS
                p1 = probs1[u % 2]

                def turn_probs(i):
                    b = 5 + i % 2
                    pe.wait_ge(sem("probs_ready"), 4 * u + i + 1)
                    take(b, "pT_out", 4 * u + i + 1)
                    turn(b, [p1[:, OFF[i] + j * P:OFF[i] + (j + 1) * P] for j in range(i + 1)]).then_inc(sem("p_turned"), 1)

                def weigh(i):
                    pe.wait_ge(sem("pT_out"), 4 * u + i + 1)
                    v = mv if latent else dv
                    if i == 0:
                        take(7, "o_read", u + 1)
                    product(bank[7][:, i * P:(i + 1) * P],
                            [(pT[i % 2][:, j * P:(j + 1) * P], v[:, j, h * P:(h + 1) * P])
                             for j in range(i + 1)]).then_inc(sem("pv_done"), 1)

                turn_probs(0)
                turn_probs(1)
                weigh(0)
                turn_probs(2)
                weigh(1)
                turn_probs(3)
                weigh(2)
                weigh(3)

            def turn_output(u):
                pe.wait_ge(sem("o_ready"), u + 1)
                take(6, "oT_out", u + 1)
                turn(6, [o_tok[u % 2][:, m, :] for m in range(TT)]).then_inc(sem("o_turned"), 1)

            scores(0)
            fill(0)
            for u in range(UNITS):
                if u + 1 < UNITS:
                    scores(u + 1)
                    fill(u + 1)
                values(u)
                if u:
                    turn_output(u - 1)

            for i in range(12):
                c = (C_GD1, C_GM0, C_GM1)[i // 4]
                if i % 4 == 0:
                    chunk_landed(pe, c)
                take(i % 4, "gate_out", i + 1)
                product(bank[i % 4], [(cols(c, k, (i % 4) * P, P), hT[:, k, :]) for k in range(KD)]).then_inc(sem("gate_done"), 1)
                if i == 1:
                    turn_output(UNITS - 1)

            pe.wait_ge(sem("mod_pool_done"), MOD_POOL)
            pe.wait_ge(sem("mod_dve_done"), MOD_DVE)
            pe.wait_ge(sem("ones_ready"), 1)
            take(4, "modc_read", 1)
            for j in range(4 * KD):
                ins = nc.tensor.matmul(bank[4][:, j:j + 1], mod_acc(j), st(ONE), start=True, stop=True)
            ins.then_inc(sem("modc_done"), 1)
            for j in range(4):
                b = (5, 6, 7, 4)[j]
                take(b, "modg_out", j + 1)
                nc.tensor.matmul(bank[b], ones_sq, mod_g[:, j // 2, (j % 2) * 512:(j % 2) * 512 + 512],
                                 start=True, stop=True).then_inc(sem("modg_done"), 1)

            chunk_landed(pe, C_PD)
            chunk_landed(pe, C_PM)
            pe.wait_ge(sem("oT_out"), UNITS)
            for d in range(KD):
                for s, (c, o) in enumerate(((C_PD, qT), (C_PM, qn))):
                    b = (2 * d + s) % 8
                    take(b, "merge_out", d + 1)
                    product(bank[b], [(cols(c, k, d * P, P, D), o[:, k, :]) for k in range(HEADS)]).then_inc(sem("merge_done"), 1)

            pe.wait_ge(sem("merge_out"), KD)
            chunk_landed(pe, C_WO0)
            chunk_landed(pe, C_WO1)
            for m in range(TT):
                for n in range(2):
                    i = 2 * m + n
                    take(i % 3, "wo_out", i + 1)
                    product(bank[i % 3], [(sgd[:, k, m * P:(m + 1) * P], cols(C_WO0 + n, k, 0, 512))
                                          for k in range(KD)]).then_inc(sem("wo_done"), 1)
                    if i == 0:
                        chunk_landed(pe, C_FOUT)
                    tn, t = i // 4, i % 4
                    for d in range(2):
                        b = 4 + 2 * (i % 2) + d
                        take(b, "taps_scaled", i + 1)
                        ins = nc.tensor.matmul(bank[b], h3T[:, t * P:(t + 1) * P],
                                               chunk(C_FOUT)[0:FW, d * D + tn * 512:d * D + tn * 512 + 512],
                                               start=True, stop=True)
                    ins.then_inc(sem("taps_done"), 1)
            for n in range(2):
                pe.wait_ge(sem("abs_step"), 4 * n + 4)
                take(3, "norm_read", n + 1)
                nc.tensor.matmul(bank[3][0:1, :], st(ONE), abs_sum[n], start=True, stop=True).then_inc(sem("norm_done"), 1)
            pe.wait_ge(sem("norm_read"), 2)
            take(3, "rnorm_read", 1)
            for j in range(KD):
                ins = nc.tensor.matmul(bank[3][:, j:j + 1], norm_sb[:, j * P:(j + 1) * P], stat[0:1, ONE:ONE + 1],
                                       start=True, stop=True)
            ins.then_inc(sem("rnorm_done"), 1)

            def transform(jobs_done, out_name, i, cos_in, sin_in, f, n0):
                fs = slice(f * P, (f + 1) * P)
                for b in range(4):
                    take(n0 + b, out_name, i + 1)
                    t, x = (fwd_cos, cos_in) if b < 2 else (fwd_sin, sin_in)
                    k0 = 2 * (b % 2)
                    ins = product(bank[n0 + b], [(t[:, k, fs], x(k)) for k in (k0, k0 + 1)])
                ins.then_inc(sem(jobs_done), 1)

            pe.wait_ge(sem("tables_in"), 16)
            for n in range(2):
                pe.wait_ge(sem("taps_ready"), 4 * n + 4)
                pe.wait_ge(sem("bias_in_taps"), n + 1)
                for f in range(2):
                    i = 2 * n + f
                    transform("kdft_done", "kdft_read", i, lambda k, n=n: taps(0, n)[:, k, :],
                              lambda k, n=n: taps(1, n)[:, k, :], f, 4 * (i % 2))

            def turn_normed(tag, src, b0):
                pe.wait_ge(sem(f"{tag}_scaled"), TT)
                for k in range(KD):
                    take(b0 + k % 4, f"{tag}_out", k + 1)
                    turn(b0 + k % 4, [src[:, m, k * P:(k + 1) * P] for m in range(TT)]).then_inc(sem(f"{tag}_turned"), 1)
                pe.wait_ge(sem(f"{tag}_out"), KD)

            turn_normed("n2", x_norm, 0)

            def hy_tile(c, j, b, name, out, count):
                take(b, out, count)
                product(bank[b], [(cols(c, k, j * P, P), hT[:, k, :]) for k in range(KD)]).then_inc(sem(name), 1)

            def turn_z(c):
                pe.wait_ge(sem("z_ready"), c + 1)
                take(c % 4, "zT_out", c + 1)
                z = z_buf[c % 2].rearrange("p (a two) -> p two a", two=2)
                turn(c % 4, [z[:, t // 2, (t % 2) * P:(t % 2) * P + P] for t in range(4)]).then_inc(sem("z_turned"), 1)

            for i in range(16):
                if i % 4 == 0:
                    chunk_landed(pe, C_HYZ0 + i // 4)
                hy_tile(C_HYZ0 + i // 4, i % 4, 4 + i % 4, "hyz_done", "hyz_out", i + 1)
                if i >= 4 and i % 2 == 1:
                    turn_z((i - 4) // 2)
            hyx_at = [0]

            def hyx(n):
                for _ in range(n):
                    i = hyx_at[0]
                    if i % 4 == 0:
                        chunk_landed(pe, C_HYX0 + i // 4)
                    hy_tile(C_HYX0 + i // 4, i % 4, 4 + i % 2, "hyx_done", "hyx_out", i + 1)
                    hyx_at[0] += 1

            hyx(1)
            turn_z(6)
            hyx(1)
            turn_z(7)
            pe.wait_ge(sem("zT_out"), 8)

            def inverse(n):
                pe.wait_ge(sem("uv_ready"), 2 * n + 2)
                for q in range(4):
                    i = 4 * n + q
                    take(6 + i % 2, "y_out", i + 1)
                    for odd in range(2):
                        parts = [(uv[:, 2 * (2 * odd + s) + f, q * P:(q + 1) * P], inv[:, 4 * s + 2 * odd + f, :])
                                 for s in range(2) for f in range(2)]
                        ins = product(bank[6 + i % 2][:, odd * NF:(odd + 1) * NF], parts)
                    ins.then_inc(sem("y_done"), 1)

            for n in range(2):
                for f in range(2):
                    i = 2 * n + f
                    x = lambda k, n=n: zT[:, k, n * 512:(n + 1) * 512]
                    transform("dft_done", "dft_read", i, x, x, f, 0)
                    hyx(2 if i < 3 else 0)
                inverse(n)

            def project_tokens(name, out, src, c0, b0):
                for n in range(2):
                    chunk_landed(pe, c0 + n)
                for m in range(TT):
                    for n in range(2):
                        i = 2 * m + n
                        take(b0 + i % 4, out, i + 1)
                        product(bank[b0 + i % 4], [(src[:, k, m * P:(m + 1) * P], cols(c0 + n, k, 0, 512))
                                                   for k in range(KD)]).then_inc(sem(name), 1)

            pe.wait_ge(sem("y_out"), KD)
            project_tokens("hyo_done", "hyo_out", x0c, C_HYO, 0)

            turn_normed("n3", x_norm, 4)
            for j in range(KF):
                c = C_UP + j // 2
                if j % 2 == 0:
                    chunk_landed(pe, c)
                for s in range(2):
                    i = 2 * j + s
                    take(i % 8, "image_out" if s == 0 else "hid_out", j + 1)
                    product(bank[i % 8], [(cols(c, k, (2 * (j % 2) + s) * P, P), hT[:, k, :])
                                          for k in range(KD)]).then_inc(sem("up_done"), 1)
            for n in range(2):
                k0 = 0
                for q, kn_ in enumerate(DOWN_K):
                    c = C_DOWN + 3 * n + q
                    chunk_landed(pe, c)
                    if n == 0:
                        pe.wait_ge(sem("hid_out"), k0 + kn_)
                    for k in range(kn_):
                        for m in range(TT):
                            if q == 0 and k == 0:
                                take(4 * n + m, "down_out", 4 * n + m + 1)
                            ins = nc.tensor.matmul(bank[4 * n + m], hid[:, k0 + k, m * P:(m + 1) * P], cols(c, k, 0, 512),
                                                   start=k0 + k == 0, stop=k0 + k == KF - 1)
                    ins.then_inc(sem("down_chunk_done"), 1)
                    k0 += kn_

        @block.scalar
        def _(act):
            def wait(name, count):
                act.wait_ge(sem(name), count)

            def copy(out, in_):
                return nc.scalar.activation(out, in_, ACT.Copy)

            squares = [0]

            def square(x, c, name, i, scratch=junk):
                if squares[0]:
                    wait("squares_done", squares[0])
                squares[0] += 1
                assert squares[0] == squares_at(name, i)
                nc.scalar.activation(scratch[:, 0:x.shape[1]], x, ACT.Square, accum_out=st(c)).then_inc(sem("squares_done"), 1)

            act.dma_start(small[:], small_d).then_inc(sem("small_in"), 16)
            act.dma_start(early, early_d).then_inc(sem("early_in"), 16)
            act.dma_start(rowed, rowed_d).then_inc(sem("rowed_in"), 16)
            act.dma_start(pos_sb[:], pos_d).then_inc(sem("pos_in"), 16)
            act.dma_start(masks[:], masks_d.rearrange("p (a b) -> p a b", a=2)).then_inc(sem("masks_in"), 16)
            for m in range(TT):
                wait(f"x_in{m}", 16)
                square(x_sb[:, m, :], SS + m, "n1", m)
            wait("small_in", 16)
            nc.scalar.activation(st(CSILU, KD), small[:, SMALL["cond"]], ACT.Silu).then_inc(sem("cond_ready"), 1)
            for k in range(KD):
                wait("n1_turned", k + 1)
                nc.scalar.activation(hT[:, k, :], bank[k % 4], ACT.Identity, scale=sm("norm_in", k)).then_inc(sem("n1_out"), 1)
            for i, t in enumerate((sin_t, cos_t)):
                wait("angle_ready", i + 1)
                nc.scalar.activation(t, t, ACT.Sin).then_inc(sem("rope_table"), 1)
            for i in range(3):
                wait("net_angle", i + 1)
                nc.scalar.activation(net[0][0:FW, :] if i < 2 else h3T, net[1][0:FW, :], ACT.Sin).then_inc(sem("net_out"), 1)

            def input_out(i):
                wait("in_done", i + 1)
                m = i % 4
                if i < 12:
                    copy(dv[:, m, :], bank[4 + m]).then_inc(sem("in_out"), 1)
                else:
                    c = 352 * (i // 4 - 3)
                    copy(lat[:, m, c:c + 352], bank[4 + m][:, 0:352]).then_inc(sem("in_out"), 1)

            def qk_out(i):
                wait("qk_turned", i + 1)
                copy((qT, kT)[i // 4][:, i % 4, :], bank[i % 4]).then_inc(sem("qk_out"), 1)

            for i in range(8, 12):
                input_out(i)
            for i in range(4):
                qk_out(i)
            for i in range(12, 20):
                input_out(i)
            wait("lambda_sums", 1)
            nc.scalar.activation(sums[:, 60:62], sums[:, 62:64], ACT.Exp).then_inc(sem("lambda_exps"), 1)
            wait("in_out", 12)
            for m in range(TT):
                square(lat[:, m, 0:Q_RANK], SS_L + m, "lat", 2 * m, cqT[:, 0, :])
                square(lat[:, m, Q_RANK:Q_RANK + KV_RANK], SS_L + 4 + m, "lat", 2 * m + 1, cqT[:, 0, :])
            for i in range(4, 8):
                qk_out(i)
            for m in range(TT):
                wait("dgate_done", m + 1)
                nc.scalar.activation(dgate[:, m, :], bank[4 + m], ACT.Silu).then_inc(sem("dgate_out"), 1)
            for i in range(1 + KQ + KKV):
                wait("lat_turned", i + 1)
                b = bank[i % 4]
                if i == 0:
                    ins = copy(krT, b)
                elif i <= KQ:
                    ins = nc.scalar.activation(cqT[:, i - 1, :], b, ACT.Identity, scale=sm("q_norm", i - 1))
                else:
                    ins = nc.scalar.activation(ckvT[:, i - 1 - KQ, :], b, ACT.Identity, scale=sm("kv_norm", i - 1 - KQ))
                ins.then_inc(sem("lat_out"), 1)
            for h in range(HEADS):
                wait("latq_done", TT + h + 1)
                copy(qn[:, h, :], bank[4 + h]).then_inc(sem("qn_out"), 1)
            for i in range(8):
                wait("latk_done", i + 1)
                copy((kn, mv)[i // 4][:, i % 4, :], bank[4 + i % 4]).then_inc(sem("latk_out"), 1)
            for b in range(2):
                wait("qr_turned", b + 1)
                copy(qrT[:, b, :], bank[b]).then_inc(sem("qrT_out"), 1)

            def exps(u):
                latent = u >= HEADS
                base = 32 * (u % 2)
                wait("neg_max", u + 1)
                for a in range(1 if latent else 2):
                    if a == 0 and u >= 2:
                        wait("p_turned", 4 * (u - 1))
                    if a == 1 and u >= 1:
                        wait("probs_ready", 4 * u)
                    for i in range(TT):
                        b, c = score_place(a, i)
                        n = (i + 1) * P
                        p = (probs2 if a else probs1[u % 2])[:, OFF[i]:OFF[i] + n]
                        nc.scalar.activation(p, bank[b][:, c:c + n], ACT.Exp, bias=sums[:, base + 4 * a + i:base + 4 * a + i + 1],
                                             scale=MLA_SCALE if latent else DIFF_SCALE,
                                             accum_out=sums[:, base + 8 + 4 * a + i:base + 9 + 4 * a + i]).then_inc(sem("exp_out"), 1)

            def fill_out(u):
                wait("fill_done", u + 1)
                if u == 4:
                    wait("mod_pool_done", MOD_POOL)
                copy(mgate[:, u, :] if u < 4 else sgd[:, u - 4, :], bank[5]).then_inc(sem("fill_out"), 1)
                if u == 3:
                    wait("fill_out", 4)
                    nc.scalar.activation(mgate, mgate, ACT.Silu).then_inc(sem("mgate_ready"), 1)

            def probs_out(u):
                for i in range(TT):
                    n = 4 * u + i
                    wait("p_turned", n + 1)
                    if n >= 2:
                        wait("pv_done", n - 1)
                    copy(pT[i % 2][:, 0:(i + 1) * P], bank[5 + i % 2][:, 0:(i + 1) * P]).then_inc(sem("pT_out"), 1)

            def output_out(u):
                wait("o_turned", u + 1)
                copy((qn if u >= HEADS else qT)[:, u % HEADS, :], bank[6]).then_inc(sem("oT_out"), 1)

            exps(0)
            fill_out(0)
            for u in range(UNITS):
                if u + 1 < UNITS:
                    exps(u + 1)
                    fill_out(u + 1)
                probs_out(u)
                if u:
                    output_out(u - 1)
            wait("mod_dve_done", MOD_DVE)
            for i in range(12):
                wait("gate_done", i + 1)
                dst = sgd[:, 4 + i, :] if i < 4 else sgm[:, i - 4, :]
                nc.scalar.activation(dst, bank[i % 4], ACT.Sigmoid).then_inc(sem("gate_out"), 1)
                if i == 1:
                    output_out(UNITS - 1)
                if i == 2:
                    nc.scalar.activation(sgd[:, 0:4, :], sgd[:, 0:4, :], ACT.Sigmoid).then_inc(sem("sgd_ready"), 1)
            act.dma_start(norm_row, rows_d[0:1, :].partition_broadcast(P).rearrange("p a d -> p (a d)")).then_inc(sem("norm_row_in"), 16)
            wait("o_ready", UNITS)
            act.dma_start(at(75, 4096), tables_d).then_inc(sem("tables_in"), 16)
            act.dma_start(deltas, deltas_d.partition_broadcast(P).rearrange("p a d -> p (a d)")).then_inc(sem("deltas_in"), 16)
            wait("modc_done", 1)
            for m in range(TT):
                act.dma_start(x_sb[:, m, :], x_d[m * P:(m + 1) * P, :]).then_inc(sem(f"x_again{m}"), 16)
            for j in range(4):
                wait("modg_done", j + 1)
                copy(mod_g[:, j // 2, (j % 2) * 512:(j % 2) * 512 + 512], bank[(5, 6, 7, 4)[j]]).then_inc(sem("modg_out"), 1)
            act.dma_start(bias_row, rows_d[3:4, :]).then_inc(sem("bias_in"), 16)

            wait("deltas_in", 16)
            for m in range(TT + 1):
                if m < TT:
                    for i in (2 * m, 2 * m + 1):
                        if i >= 2:
                            wait("taps_scaled", i - 1)
                        n, t = i // 4, i % 4
                        nc.scalar.activation(decay[i % 2], deltas[:, n * 512:n * 512 + 512], ACT.Exp,
                                             scale=sm("minus_t", t)).then_inc(sem("decay_ready"), 1)
                    for i in (2 * m, 2 * m + 1):
                        wait("taps_scaled", i + 1)
                        if i:
                            wait("abs_step", i)
                        for d in range(2):
                            nc.scalar.activation(abs_tap[d], filt[2 * (i % 2) + d], ACT.Abs).then_inc(sem("abs_ready"), 1)
                    wait("wo_out", 2 * m + 2)
                    square(x_sb[:, m, :], SS + m, "x1", m)
                if m:
                    wait("x2_ready", m)
                    square(x_sb[:, m - 1, :], SS2 + m - 1, "x2", m - 1)
            wait("taps_ready", 8)
            for i in range(4):
                wait("kdft_done", i + 1)
                if i >= 2:
                    wait("kdft_read", i - 1)
                b0 = 4 * (i % 2)
                copy(filt[2 * (i % 2)], bank[b0 + 1]).then_inc(sem("kdft_copied"), 1)
                copy(filt[2 * (i % 2) + 1], bank[b0 + 3]).then_inc(sem("kdft_copied"), 1)
            wait("kdft_read", 4)
            wait("modc_ready", 1)

            def normed_out(tag, s, b0):
                for k in range(KD):
                    wait(f"{tag}_turned", k + 1)
                    nc.scalar.activation(hT[:, k, :], bank[b0 + k % 4], ACT.Identity,
                                         scale=modc[:, (2 * s + 1) * KD + k:(2 * s + 1) * KD + k + 1],
                                         bias=modc[:, 2 * s * KD + k:2 * s * KD + k + 1]).then_inc(sem(f"{tag}_out"), 1)

            normed_out("n2", 0, 0)

            def hy_out(i, tile, b, place, name, done, conv_name):
                wait(done, i + 1)
                if conv_name:
                    wait(*conv_name)
                nc.scalar.activation(place[:, 1:SEQ + 1], bank[b], ACT.Identity, bias=sm("hy_b_in", tile)).then_inc(sem(name), 1)

            def z_out(c):
                wait("z_turned", c + 1)
                copy(zT[:, :, c * P:(c + 1) * P], bank[c % 4].rearrange("p (a b) -> p a b", a=4)).then_inc(sem("zT_out"), 1)

            wait("pads_ready", 1)
            for i in range(16):
                hy_out(i, (8, 16)[i % 2] + i // 2, 4 + i % 4, padded[i % 2], "hyz_out", "hyz_done",
                       ("hyz_conv", i - 1) if i >= 2 else None)
                if i >= 4 and i % 2 == 1:
                    z_out((i - 4) // 2)

            def hyx_out(i):
                hy_out(i, i, 4 + i % 2, padded[0], "hyx_out", "hyx_done",
                       ("hyx_conv", i) if i >= 1 else ("hyz_conv", 16))

            hyx_out(0)
            z_out(6)
            hyx_out(1)
            z_out(7)
            for i in range(4):
                wait("dft_done", i + 1)
                if i:
                    wait("uv_ready", i)
                copy(tmp[0], bank[1]).then_inc(sem("dft_copied"), 1)
                copy(tmp[1], bank[3]).then_inc(sem("dft_copied"), 1)
                if i < 3:
                    hyx_out(2 * i + 2)
                    hyx_out(2 * i + 3)
            wait("hyx_conv", 8)
            act.dma_start(row[:], rows_d[1:2, :].partition_broadcast(P).rearrange("p a d -> p (a d)")).then_inc(sem("b_out_in"), 16)
            for m in range(TT):
                wait("hyo_out", 2 * m + 2)
                square(x_sb[:, m, :], SS + m, "x3", m)
            act.dma_start(row[:], rows_d[2:3, :].partition_broadcast(P).rearrange("p a d -> p (a d)")).then_inc(sem("final_g_in"), 16)
            normed_out("n3", 1, 4)

            wait("borders_ready", 1)
            for j in range(KF + 1):
                if j < KF:
                    wait("up_done", 2 * j + 1)
                    if j >= 2:
                        wait("conv_done", j - 1)
                    copy(image[j % 2][:, 1:ROWS + 1, 1:COLS + 1],
                         bank[2 * j % 8].rearrange("p (r c) -> p r c", c=COLS)).then_inc(sem("image_out"), 1)
                if j:
                    wait("conv_done", j)
                    nc.scalar.activation(conv[(j - 1) % 2], conv[(j - 1) % 2], ACT.Silu).then_inc(sem("silu_out"), 1)
            for m in range(TT):
                wait("down_out", 4 + m + 1)
                square(x_sb[:, m, :], SS_L + m, "x4", m)

        @block.gpsimd
        def _(pool):
            steps = [0]

            def wait(name, count):
                pool.wait_ge(sem(name), count)

            def link(ins):
                steps[0] += 1
                ins.then_inc(sem("pool_step"), 1)
                pool.wait_ge(sem("pool_step"), steps[0])

            def rsqrt(dst, src, n, width, name):
                link(nc.gpsimd.tensor_scalar(st(dst, n), st(src, n), 1.0 / width, NORM_EPS, ALU.mult, ALU.add))
                nc.gpsimd.tensor_tensor(st(dst, n), st(dst, n), st(MHALF, n), ALU.pow).then_inc(sem(name), 1)

            link(nc.gpsimd.memset(st(MHALF, 4), -0.5))
            nc.gpsimd.memset(st(ONE), 1.0).then_inc(sem("one_ready"), 1)
            nc.gpsimd.memset(mod_g[:], 0.0).then_inc(sem("mod_g_clear"), 1)
            wait("squares_done", squares_at("n1", 3))
            rsqrt(RS, SS, TT, D, "n1_rs")
            wait("mod_g_clear", 1)
            pool.dma_start(mod_g[0:1, :, :].rearrange("p a b -> p (a b)"), mod_b_d[:, 4 * D:6 * D]).then_inc(sem("mod_b_in"), 16)
            acc = x_sb[:].rearrange("p a b -> p (a b)")
            wait("n1_turned", KD)
            link(nc.gpsimd.memset(acc, 0.0))
            pool.dma_start(acc[0:1, :], mod_b_d[:, 0:4 * D]).then_inc(sem("mod_b_in"), 16)
            C = MOD_POOL_COLS

            def load_pool(j):
                pool.dma_start(modw_pool[j % 2], mod_d[0:1, :, j * 1024:(j + 1) * 1024].rearrange("o p (k c) -> (o p) k c", k=KD)).then_inc(sem(f"modw_pool_in{j % 2}"), 16)

            def load_dve(j):
                if j:
                    wait("mod_dve_done", j)
                pool.dma_start(modw_dve, mod_d[1:2, :, j * 2048:(j + 1) * 2048].rearrange("o p (k c) -> (o p) k c", k=KD)).then_inc(sem("modw_dve_in"), 16)

            load_pool(0)
            load_dve(0)
            load_pool(1)
            wait("mod_b_in", 32)
            wait("cond_ready", 1)
            cb = st(CSILU, KD).unsqueeze(2).broadcast_to([P, KD, C])
            for j in range(MOD_POOL):
                w = modw_pool[j % 2]
                wait(f"modw_pool_in{j % 2}", 16 * (j // 2 + 1))
                link(nc.gpsimd.tensor_tensor(w, w, cb, ALU.mult))
                for n in (4, 2, 1):
                    link(nc.gpsimd.tensor_tensor(w[:, 0:n, :], w[:, 0:n, :], w[:, n:2 * n, :], ALU.add))
                nc.gpsimd.tensor_tensor(acc[:, j * C:(j + 1) * C], acc[:, j * C:(j + 1) * C], w[:, 0, :],
                                        ALU.add).then_inc(sem("mod_pool_done"), 1)
                if j + 2 < MOD_POOL:
                    wait("mod_pool_done", j + 1)
                    load_pool(j + 2)
                if j % 2 and j // 2 + 1 < MOD_DVE:
                    load_dve(j // 2 + 1)
            wait("squares_done", squares_at("lat", 7))
            rsqrt(RS_L, SS_L, 4, Q_RANK, "lat_rs")
            rsqrt(RS_L + 4, SS_L + 4, 4, KV_RANK, "lat_rs")
            for h in range(HEADS):
                wait("o_ss", h + 1)
                rsqrt(RS_H + 4 * (h % 2), SS_H + 4 * (h % 2), 4, P, "o_rs")
            wait("o_turned", UNITS)
            nc.gpsimd.memset(ones_sq, 1.0).then_inc(sem("ones_ready"), 1)
            for m in range(TT + 1):
                if m < TT:
                    for i in (2 * m, 2 * m + 1):
                        n, t = i // 4, i % 4
                        wait("taps_scaled", i + 1)
                        h0, h1 = filt[2 * (i % 2)], filt[2 * (i % 2) + 1]
                        nc.gpsimd.tensor_tensor(taps(0, n)[:, t, :], h0, h1, ALU.add).then_inc(sem("taps_step"), 1)
                        nc.gpsimd.tensor_tensor(taps(1, n)[:, t, :], h0, h1, ALU.subtract).then_inc(sem("taps_ready"), 1)
                    wait("squares_done", squares_at("x1", m))
                    rsqrt(RS + m, SS + m, 1, D, "x1_rs")
                if m:
                    wait("squares_done", squares_at("x2", m - 1))
                    rsqrt(RS2 + m - 1, SS2 + m - 1, 1, D, "x2_rs")
            for i in range(4):
                n, f = i // 2, i % 2
                kr, ks = km[:, f, n * 512:n * 512 + 512], km[:, 2 + f, n * 512:n * 512 + 512]
                wait("dft_read", i + 1)
                if i:
                    wait("uv_ready", i)
                link(nc.gpsimd.tensor_tensor(tmp[5], tmp[2], kr, ALU.mult))
                link(nc.gpsimd.tensor_tensor(tmp[6], tmp[3], ks, ALU.mult))
                link(nc.gpsimd.tensor_tensor(tmp[5], tmp[5], tmp[6], ALU.subtract))
                link(nc.gpsimd.tensor_tensor(tmp[6], tmp[2], ks, ALU.mult))
                link(nc.gpsimd.tensor_tensor(tmp[2], tmp[3], kr, ALU.mult))
                nc.gpsimd.tensor_tensor(tmp[6], tmp[6], tmp[2], ALU.add).then_inc(sem("w_ready"), 1)
            for m in range(TT):
                wait("squares_done", squares_at("x3", m))
                rsqrt(RS + m, SS + m, 1, D, "x3_rs")
            for m in range(TT):
                wait("squares_done", squares_at("x4", m))
                rsqrt(RS_L + m, SS_L + m, 1, D, "x4_rs")

        @block.vector
        def _(dve):
            steps = [0]
            V = nc.vector

            def wait(name, count):
                dve.wait_ge(sem(name), count)

            def link(ins):
                steps[0] += 1
                ins.then_inc(sem("dve_step"), 1)
                dve.wait_ge(sem("dve_step"), steps[0])

            def wrap(r, a, k, quarter):
                link(V.tensor_scalar(k, a, 1.0 / TWO_PI, 0.25 * quarter, ALU.mult, ALU.add))
                link(V.tensor_scalar(k, k, ROUNDER, None, ALU.add))
                link(V.tensor_scalar(k, k, ROUNDER, None, ALU.subtract))
                link(V.scalar_tensor_tensor(out=r, in0=k, scalar=-PI_1, in1=a, op0=ALU.mult, op1=ALU.add))
                link(V.scalar_tensor_tensor(out=r, in0=k, scalar=-PI_2, in1=r, op0=ALU.mult, op1=ALU.add))
                link(V.scalar_tensor_tensor(out=r, in0=k, scalar=-PI_3, in1=r, op0=ALU.mult, op1=ALU.add))
                if quarter:
                    link(V.tensor_scalar(r, r, math.pi / 2, None, ALU.add))
                return V.tensor_scalar(r, r, PI_BELOW, -PI_BELOW, ALU.min, ALU.max)

            wait("n1_rs", 1)
            for m in range(TT):
                V.tensor_scalar(x_sb[:, m, :], x_sb[:, m, :], st(RS + m), None, ALU.mult).then_inc(sem("n1_scaled"), 1)

            wait("rowed_in", 16)
            wait("pos_in", 16)
            ang = nsin_t
            posf = sums[:, 0:TT]
            link(V.tensor_copy(posf, pos_sb[:]))
            for m in range(TT):
                ins = V.tensor_scalar(ang[:, m * HALF:(m + 1) * HALF], rowed[:, ROWED["inv_freq"]], posf[:, m:m + 1], None, ALU.mult)
            link(ins)
            for i, t in enumerate((sin_t, cos_t)):
                wrap(t, ang, rope_tmp[:, 0:128], i).then_inc(sem("angle_ready"), 1)
            wait("rope_table", 1)
            wait("angle_ready", 2)
            link(V.tensor_scalar(nsin_t, sin_t, -1.0, None, ALU.mult))
            lam = rowed[:, ROWED["lam"]].rearrange("p (a b c) -> p a b c", a=2, b=2)
            prod = rope_tmp[:, 0:128].rearrange("p (a c) -> p a c", a=2)
            link(V.tensor_tensor(prod, lam[:, :, 0, :], lam[:, :, 1, :], ALU.mult))
            V.tensor_reduce(sums[:, 62:64], prod, AX.X, ALU.add).then_inc(sem("lambda_sums"), 1)

            def net_layer(i):
                wait("net_done", i + 1)
                if i:
                    wait("net_out", i)
                fb = early[0:FW, EARLY["f_b"]][:, i:i + 1]
                a, k, r = net[2][0:FW, :], net[3][0:FW, :], net[1][0:FW, :]
                V.tensor_scalar(a, bank[i][0:FW, :], fb, early[0:FW, EARLY["freq"]], ALU.add, ALU.mult).then_inc(sem("net_read"), 1)
                wait("net_read", i + 1)
                wrap(r, a, k, 0).then_inc(sem("net_angle"), 1)

            def mod_chunk(j):
                C = MOD_DVE_COLS
                wait("modw_dve_in", 16 * (j + 1))
                col = 3 * D + j * C
                acc = (x_sb[:].rearrange("p a b -> p (a b)")[:, col:col + C] if col < 4 * D
                       else mod_g[:].rearrange("p a b -> p (a b)")[:, col - 4 * D:col - 4 * D + C])
                w = modw_dve
                for k in range(KD):
                    ins = V.scalar_tensor_tensor(out=acc, in0=w[:, k, :], scalar=st(CSILU + k), in1=acc, op0=ALU.mult, op1=ALU.add)
                    if k < KD - 1:
                        link(ins)
                ins.then_inc(sem("mod_dve_done"), 1)

            def table(t, m, groups, halves):
                v = t[:, m * HALF:(m + 1) * HALF]
                return v.unsqueeze(1).broadcast_to([P, groups * halves, HALF])

            def rope_tile(out, src, m, groups):
                o3 = out.rearrange("p (g c) -> p g c", c=HALF)
                s3 = src.rearrange("p (g c) -> p g c", c=HALF)
                t3 = rope_tmp[:, 0:groups * 64].rearrange("p (g two c) -> p two g c", two=2, c=HALF)
                s4 = src.rearrange("p (g two c) -> p two g c", two=2, c=HALF)
                link(V.tensor_tensor(o3, s3, table(cos_t, m, groups, 2), ALU.mult))
                link(V.tensor_tensor(t3[:, 0], s4[:, 1], table(nsin_t, m, groups, 1), ALU.mult))
                link(V.tensor_tensor(t3[:, 1], s4[:, 0], table(sin_t, m, groups, 1), ALU.mult))
                return V.tensor_tensor(out, out, rope_tmp[:, 0:groups * 64], ALU.add)

            net_layer(0)
            wait("rope_table", 2)
            wait("mod_b_in", 32)
            wait("cond_ready", 1)
            for i in range(8):
                if i:
                    mod_chunk(i - 1)
                if i in (3, 6):
                    net_layer(i // 3)
                wait("in_done", i + 1)
                rope_tile(roped[i // 4][:, i % 4, :], bank[4 + i % 4], i % 4, 8).then_inc(sem("rope_out"), 1)
            wait("lambda_exps", 1)
            link(V.tensor_scalar(st(NLAM), sums[:, 61:62], sums[:, 60:61], LAMBDA_INIT, ALU.subtract, ALU.subtract))
            for j in range(7, MOD_DVE):
                mod_chunk(j)
            wait("in_out", 12)
            wait("qk_turned", 8)
            for m in range(TT):
                link(rope_tile(kr2[:, m, 0:64], lat[:, m, 640:704], m, 1))
                ins = V.tensor_copy(kr2[:, m, 64:128], kr2[:, m, 0:64])
            ins.then_inc(sem("kr_ready"), 1)
            wait("lat_rs", 2)
            for s, (a, n) in enumerate(((0, Q_RANK), (Q_RANK, KV_RANK))):
                for m in range(TT):
                    ins = V.tensor_scalar(lat[:, m, a:a + n], lat[:, m, a:a + n], st(RS_L + 4 * s + m), None, ALU.mult)
                ins.then_inc(sem("lat_scaled"), 1)
            for m in range(TT):
                wait("latq_done", m + 1)
                rope_tile(qr[:, m, :], bank[4 + m][:, 0:256], m, 4).then_inc(sem("qr_out"), 1)
            wait("dgate_out", TT)
            sub = rowed[:, ROWED["subln"]].unsqueeze(1).broadcast_to([P, HEADS, P])
            for m in range(TT):
                g = dgate[:, m, :].rearrange("p (h c) -> p h c", h=HEADS)
                V.scalar_tensor_tensor(out=g, in0=g, scalar=1.0 - LAMBDA_INIT, in1=sub, op0=ALU.mult,
                                       op1=ALU.mult).then_inc(sem("dgate_ready"), 1)

            def maxima(u):
                latent = u >= HEADS
                base, maps = 32 * (u % 2), 1 if latent else 2
                wait("scores_done", scores_at(u))
                for a in range(maps):
                    for i in range(TT):
                        b, c = score_place(a, i)
                        o = base + 16 + 4 * a + i
                        ins = V.tensor_reduce(sums[:, o:o + 1], bank[b][:, c:c + (i + 1) * P], AX.X, ALU.max)
                link(ins)
                V.tensor_scalar(sums[:, base:base + 4 * maps], sums[:, base + 16:base + 16 + 4 * maps],
                                -(MLA_SCALE if latent else DIFF_SCALE), None, ALU.mult).then_inc(sem("neg_max"), 1)

            def combine(u):
                base = 32 * (u % 2)
                wait("exp_out", exps_before(u + 1))
                r1, ratio = sums[:, base + 24:base + 28], sums[:, base + 28:base + 32]
                if u >= HEADS:
                    for i in range(TT):
                        V.reciprocal(r1[:, i:i + 1], sums[:, base + 8 + i:base + 9 + i]).then_inc(sem("probs_ready"), 1)
                    return
                link(V.reciprocal(ratio, sums[:, base + 12:base + 16]))
                link(V.reciprocal(r1, sums[:, base + 8:base + 12]))
                link(V.tensor_tensor(ratio, ratio, sums[:, base + 8:base + 12], ALU.mult))
                link(V.tensor_scalar(ratio, ratio, st(NLAM), None, ALU.mult))
                for i in range(TT):
                    s = slice(OFF[i], OFF[i] + (i + 1) * P)
                    V.scalar_tensor_tensor(out=probs1[u % 2][:, s], in0=probs2[:, s], scalar=ratio[:, i:i + 1],
                                           in1=probs1[u % 2][:, s], op0=ALU.mult, op1=ALU.add).then_inc(sem("probs_ready"), 1)

            def output(u):
                base = 32 * (u % 2)
                o = o_tok[u % 2]
                wait("pv_done", 4 * u + 4)
                if u >= 2:
                    wait("o_turned", u - 1)
                r1 = sums[:, base + 24:base + 28].unsqueeze(2).broadcast_to([P, TT, P])
                V.tensor_tensor(o, bank[7].rearrange("p (a b) -> p a b", a=TT), r1, ALU.mult).then_inc(sem("o_read"), 1)
                wait("o_read", u + 1)
                if u < HEADS:
                    link(V.tensor_tensor(o_sq, o, o, ALU.mult))
                    c = SS_H + 4 * (u % 2)
                    V.tensor_reduce(st(c, 4), o_sq, AX.X, ALU.add).then_inc(sem("o_ss"), 1)

            def gate_output(u):
                h, o = u % HEADS, o_tok[u % 2]
                if u < HEADS:
                    wait("o_rs", u + 1)
                    r = st(RS_H + 4 * (u % 2), 4).unsqueeze(2).broadcast_to([P, TT, P])
                    link(V.tensor_tensor(o, o, r, ALU.mult))
                    g = dgate
                else:
                    wait("mgate_ready", 1)
                    g = mgate
                V.tensor_tensor(o, o, g[:, :, h * P:(h + 1) * P], ALU.mult).then_inc(sem("o_ready"), 1)

            maxima(0)
            combine(0)
            for u in range(UNITS):
                if u + 1 < UNITS:
                    maxima(u + 1)
                output(u)
                if u + 1 < UNITS:
                    combine(u + 1)
                gate_output(u)

            wait("modc_done", 1)
            V.tensor_copy(modc[:], bank[4][:, 0:4 * KD]).then_inc(sem("modc_read"), 1)
            wait("modc_read", 1)
            for s, name in enumerate(("norm_g1", "norm_g2")):
                c = modc[:, (2 * s + 1) * KD:(2 * s + 2) * KD]
                ins = V.scalar_tensor_tensor(out=c, in0=c, scalar=1.0, in1=small[:, SMALL[name]], op0=ALU.add, op1=ALU.mult)
            ins.then_inc(sem("modc_ready"), 1)

            wait("gate_out", 12)
            wait("sgd_ready", 1)
            for d in range(KD):
                wait("merge_done", 2 * d + 2)
                link(V.tensor_tensor(sgd[:, d, :], sgd[:, d, :], bank[2 * d % 8], ALU.mult))
                link(V.tensor_tensor(sgm[:, d, :], sgm[:, d, :], bank[(2 * d + 1) % 8], ALU.mult))
                V.tensor_tensor(sgd[:, d, :], sgd[:, d, :], sgm[:, d, :], ALU.add).then_inc(sem("merge_out"), 1)

            def add_abs(i):
                a = abs_sum[i // 4]
                wait("abs_ready", 2 * i + 2)
                link(V.tensor_tensor(a, a, abs_tap[0], ALU.add))
                V.tensor_tensor(a, a, abs_tap[1], ALU.add).then_inc(sem("abs_step"), 1)
                wait("abs_step", i + 1)

            wait("norm_row_in", 16)
            link(V.memset(abs_sum[0], 0.0))
            link(V.memset(abs_sum[1], 0.0))
            for m in range(TT + 2):
                if m < TT:
                    wait(f"x_again{m}", 16)
                    for i in (2 * m, 2 * m + 1):
                        s = slice((i % 2) * 512, (i % 2) * 512 + 512)
                        wait("wo_done", i + 1)
                        V.tensor_tensor(x_sb[:, m, s], x_sb[:, m, s], bank[i % 3], ALU.add).then_inc(sem("wo_out"), 1)
                        n, t = i // 4, i % 4
                        wait("taps_done", i + 1)
                        wait("decay_ready", i + 1)
                        if i >= 2:
                            wait("taps_ready", i - 1)
                        h0, h1 = filt[2 * (i % 2)], filt[2 * (i % 2) + 1]
                        b = 4 + 2 * (i % 2)
                        V.tensor_tensor(h0, bank[b], decay[i % 2], ALU.mult)
                        ins = V.tensor_tensor(h1, bank[b + 1], decay[i % 2], ALU.mult)
                        if t == 0:
                            link(ins)
                            ins = V.memset(h1[0:1, :], 0.0)
                        ins.then_inc(sem("taps_scaled"), 1)
                        if i:
                            add_abs(i - 1)
                elif m == TT:
                    add_abs(7)
                if 1 <= m <= TT:
                    wait("x1_rs", m)
                    V.scalar_tensor_tensor(out=x_sb[:, m - 1, :], in0=x_sb[:, m - 1, :], scalar=st(RS + m - 1), in1=norm_row,
                                           op0=ALU.mult, op1=ALU.mult).then_inc(sem("x2_ready"), 1)
                if m >= 2:
                    wait("x2_rs", m - 1)
                    wait("x2_ready", m - 1)
                    V.tensor_scalar(x_norm[:, m - 2, :], x_sb[:, m - 2, :], st(RS2 + m - 2), None, ALU.mult).then_inc(sem("n2_scaled"), 1)
            wait("bias_in", 16)
            for n in range(2):
                s = slice(n * 512, n * 512 + 512)
                wait("norm_done", n + 1)
                V.tensor_copy(norm_sb[:, s], bank[3][0:1, :]).then_inc(sem("norm_read"), 1)
                wait("norm_read", n + 1)
                link(V.tensor_tensor(bias_row[:, s], bias_row[:, s], norm_sb[:, s], ALU.mult))
                wait("taps_ready", 4 * n + 4)
                tap0 = taps(0, n)[0:1, 0, :]
                V.tensor_tensor(tap0, tap0, bias_row[:, s], ALU.add).then_inc(sem("bias_in_taps"), 1)
            wait("rnorm_done", 1)
            V.reciprocal(st(RNORM, KD), bank[3][:, 0:KD]).then_inc(sem("rnorm_read"), 1)
            wait("rnorm_read", 1)
            link(V.tensor_scalar(st(RNORM, KD), st(RNORM, KD), 2.0 / (2 * SEQ), None, ALU.mult))

            for i in range(4):
                n, f = i // 2, i % 2
                b0 = 4 * (i % 2)
                s = slice(n * 512, n * 512 + 512)
                wait("kdft_copied", 2 * i + 2)
                o_cos, o_sin = filt[2 * (i % 2)], filt[2 * (i % 2) + 1]
                V.tensor_tensor(kp[:, f, s], bank[b0], o_cos, ALU.add)
                V.tensor_tensor(km[:, f, s], bank[b0], o_cos, ALU.subtract)
                V.tensor_tensor(kp[:, 2 + f, s], bank[b0 + 2], o_sin, ALU.add)
                V.tensor_tensor(km[:, 2 + f, s], bank[b0 + 2], o_sin, ALU.subtract).then_inc(sem("kdft_read"), 1)

            wait("taps_done", 8)
            wait("squares_done", squares_at("x2", 3))
            for p in padded:
                V.memset(p[:, 0:1], 0.0)
                ins = V.memset(p[:, SEQ + 1:SEQ + 2], 0.0)
            ins.then_inc(sem("pads_ready"), 1)

            def short_conv(out, p, tile):
                w = lambda t: sm("hy_sc_w", 24 * t + tile)
                link(V.tensor_scalar(out, p[:, 0:SEQ], w(0), sm("hy_sc_b", tile), ALU.mult, ALU.add))
                link(V.scalar_tensor_tensor(out=out, in0=p[:, 1:SEQ + 1], scalar=w(1), in1=out, op0=ALU.mult, op1=ALU.add))
                return V.scalar_tensor_tensor(out=out, in0=p[:, 2:SEQ + 2], scalar=w(2), in1=out, op0=ALU.mult, op1=ALU.add)

            wait("pads_ready", 1)
            for i in range(16):
                c = i // 2
                wait("hyz_out", i + 1)
                if i % 2 == 0 and c:
                    wait("z_ready", c)
                short_conv((x1c, vc)[i % 2], padded[i % 2], (8, 16)[i % 2] + c).then_inc(sem("hyz_conv"), 1)
                if i % 2:
                    wait("hyz_conv", i + 1)
                    if c >= 2:
                        wait("z_turned", c - 1)
                    V.tensor_tensor(z_buf[c % 2], x1c, vc, ALU.mult).then_inc(sem("z_ready"), 1)

            def hyx_conv(i):
                wait("hyx_out", i + 1)
                short_conv(x0c[:, i, :], padded[0], i).then_inc(sem("hyx_conv"), 1)

            def inverse_out(n):
                for q in range(4):
                    i = 4 * n + q
                    wait("y_done", i + 1)
                    x = x0c[:, i, :].rearrange("p (t two) -> p two t", two=2)
                    y = bank[6 + i % 2].rearrange("p (two t) -> p two t", two=2)
                    V.scalar_tensor_tensor(out=x, in0=y, scalar=st(RNORM + i), in1=x, op0=ALU.mult,
                                           op1=ALU.mult).then_inc(sem("y_out"), 1)

            hyx_conv(0)
            hyx_conv(1)
            for i in range(4):
                n, f = i // 2, i % 2
                s = slice(n * 512, n * 512 + 512)
                kr, ks = kp[:, f, s], kp[:, 2 + f, s]
                ur, us, vr, vs = (uv[:, 2 * c + f, :] for c in range(4))
                e_cos, e_sin = bank[0], bank[2]
                sr, ss, dr, ds, yr, wr, ws = tmp
                wait("dft_copied", 2 * i + 2)
                link(V.tensor_tensor(dr, e_cos, sr, ALU.subtract))
                link(V.tensor_tensor(ds, e_sin, ss, ALU.subtract))
                link(V.tensor_tensor(sr, e_cos, sr, ALU.add))
                V.tensor_tensor(ss, e_sin, ss, ALU.add).then_inc(sem("dft_read"), 1)
                wait("dft_read", i + 1)
                if n:
                    wait("y_done", 4)
                V.tensor_tensor(yr, sr, kr, ALU.mult)
                link(V.tensor_tensor(ur, ss, ks, ALU.mult))
                V.tensor_tensor(us, sr, ks, ALU.mult)
                link(V.tensor_tensor(yr, yr, ur, ALU.subtract))
                link(V.tensor_tensor(sr, ss, kr, ALU.mult))
                link(V.tensor_tensor(sr, sr, us, ALU.add))
                wait("w_ready", i + 1)
                V.tensor_tensor(ur, yr, wr, ALU.add)
                V.tensor_tensor(vr, yr, wr, ALU.subtract)
                V.tensor_tensor(us, sr, ws, ALU.add)
                V.tensor_tensor(vs, sr, ws, ALU.subtract).then_inc(sem("uv_ready"), 1)
                if i < 3:
                    hyx_conv(2 * i + 2)
                    hyx_conv(2 * i + 3)
                if i % 2:
                    wait("hyx_conv", min(8, 2 * i + 4))
                    wait("dve_step", steps[0])
                    inverse_out(n)
            wait("b_out_in", 16)
            for m in range(TT + 1):
                if m < TT:
                    for n in range(2):
                        i = 2 * m + n
                        s = slice(n * 512, n * 512 + 512)
                        t = tmp[n]
                        wait("hyo_done", i + 1)
                        link(V.tensor_tensor(t, bank[i % 4], row[:, s], ALU.add))
                        link(V.tensor_tensor(t, t, mod_g[:, 0, s], ALU.mult))
                        V.tensor_tensor(x_sb[:, m, s], x_sb[:, m, s], t, ALU.add).then_inc(sem("hyo_out"), 1)
                if m:
                    wait("x3_rs", m)
                    wait("hyo_out", 2 * m)
                    V.tensor_scalar(x_norm[:, m - 1, :], x_sb[:, m - 1, :], st(RS + m - 1), None, ALU.mult).then_inc(sem("n3_scaled"), 1)

            for im in image:
                V.memset(im[:, 0, :], 0.0)
                V.memset(im[:, ROWS + 1, :], 0.0)
                V.memset(im[:, 1:ROWS + 1, 0:1], 0.0)
                ins = V.memset(im[:, 1:ROWS + 1, COLS + 1:COLS + 2], 0.0)
            ins.then_inc(sem("borders_ready"), 1)
            for j in range(KF + 1):
                if j < KF:
                    wait("image_out", j + 1)
                    if j >= 2:
                        wait("hid_out", j - 1)
                    out = conv[j % 2].rearrange("p (r c) -> p r c", c=COLS)
                    for t in range(9):
                        src = image[j % 2][:, t // 3:t // 3 + ROWS, t % 3:t % 3 + COLS]
                        w = sm("conv_w", t * KF + j)
                        if t == 0:
                            ins = V.tensor_scalar(out, src, w, sm("conv_b", j), ALU.mult, ALU.add)
                        else:
                            ins = V.scalar_tensor_tensor(out=out, in0=src, scalar=w, in1=out, op0=ALU.mult, op1=ALU.add)
                        if t < 8:
                            link(ins)
                    ins.then_inc(sem("conv_done"), 1)
                if j:
                    wait("silu_out", j)
                    wait("up_done", 2 * j)
                    V.tensor_tensor(hid[:, j - 1, :], conv[(j - 1) % 2], bank[(2 * j - 1) % 8], ALU.mult).then_inc(sem("hid_out"), 1)
            for n in range(2):
                wait("down_chunk_done", 3 * n + 3)
                for m in range(TT):
                    s = slice(n * 512, n * 512 + 512)
                    t = conv[m % 2]
                    link(V.tensor_tensor(t, bank[4 * n + m], mod_g[:, 1, s], ALU.mult))
                    V.tensor_tensor(x_sb[:, m, s], x_sb[:, m, s], t, ALU.add).then_inc(sem("down_out"), 1)
            wait("final_g_in", 16)
            wait("down_out", 8)
            for m in range(TT):
                wait("x4_rs", m + 1)
                if m >= 2:
                    wait(f"y_stored{m % 2}", 16)
                V.scalar_tensor_tensor(out=out_tok[m % 2], in0=x_sb[:, m, :], scalar=st(RS_L + m), in1=row[:],
                                       op0=ALU.mult, op1=ALU.mult).then_inc(sem("y_ready"), 1)


def _times():
    return np.concatenate([np.arange(0, SEQ, 2), np.arange(1, SEQ, 2)])


def _filter_constants():
    t = np.linspace(0.0, 1.0, SEQ, dtype=np.float32)
    w = (2.0 * math.pi * np.arange(SEQ, dtype=np.float32) / SEQ).astype(np.float32)
    bands = np.linspace(1e-4, BANDS - 1, BANDS, dtype=np.float32)
    angle = (bands[:, None] * w[None, :]).astype(np.float32).astype(np.float64)
    pos = np.concatenate([t[None, :], np.cos(angle), -np.sin(angle)]).astype(np.float32)
    deltas = np.abs(np.linspace(math.log(1e-2) / 1.5, math.log(1e-2) / 0.3, D, dtype=np.float32))
    order = _times()
    return pos[:, order], -t[order].reshape(TT, P).T, deltas[None, :].astype(np.float32)


def _transform_tables():
    t = _times().astype(np.int64)
    k = np.arange(NF, dtype=np.int64)
    angle = np.pi * ((2 * k[None, :] + 1) * t[:, None] % (4 * SEQ)) / (2 * SEQ)
    tables = []
    for f in (np.cos, np.sin):
        tables.append(f(angle).reshape(4, P, NF).transpose(1, 0, 2).reshape(P, 4 * NF))
    for f in (np.cos, np.sin):
        by_f = f(angle).T
        tables.append(by_f.reshape(2, P, 2, NF).transpose(1, 2, 0, 3).reshape(P, 4 * NF))
    return np.concatenate(tables, axis=1).astype(np.float32)


def _by_feature(v, n):
    return v.reshape(n, P).T


def kernel(**inputs):
    import concourse.bacc as _bacc
    from concourse.bass_utils import run_bass_kernel_spmd as _run
    import ml_dtypes

    a = {k: np.asarray(v) for k, v in inputs.items()}
    f32 = np.float32
    w_in = a["w_in"][0]
    pos_emb, minus_t, deltas = _filter_constants()

    stream = np.zeros((N_CHUNKS, P, SLOT), f32)

    def put(c, w):
        n, width = w.shape[0] // P, w.shape[1]
        stream[c, :, 0:n * width] = w.reshape(n, P, width).transpose(1, 0, 2).reshape(P, n * width)

    put(C_DQ, w_in[:, 0:512])
    put(C_DK, w_in[:, 512:1024])
    put(C_DV, w_in[:, 1024:1536])
    put(C_DGATE, w_in[:, 1536:2048])
    put(C_LAT0, w_in[:, 2048:2400])
    put(C_LAT1, w_in[:, 2400:2752])
    put(C_MGATE, w_in[:, 2752:3264])
    for i, c in enumerate((C_GD0, C_GD1, C_GM0, C_GM1)):
        put(c, w_in[:, 3264 + 512 * i:3776 + 512 * i])
    uq = a["w_uq"][0].reshape(Q_RANK, HEADS, 192)
    put(C_UQ, np.concatenate([uq[:, :, 0:128].reshape(Q_RANK, 512), uq[:, :, 128:].reshape(Q_RANK, 256)], axis=1))
    ukv = a["w_ukv"][0].reshape(KV_RANK, HEADS, 256)
    put(C_UKV, np.concatenate([ukv[:, :, 0:128].reshape(KV_RANK, 512), ukv[:, :, 128:].reshape(KV_RANK, 512)], axis=1))
    put(C_PD, a["w_proj_diff"][0])
    put(C_PM, a["w_proj_mla"][0])
    for n in range(2):
        put(C_WO0 + n, a["w_out"][0][:, 512 * n:512 * n + 512])
        put(C_HYO + n, a["hy_w_out_2"][0][:, 512 * n:512 * n + 512])
    stream[C_FOUT, 0:FW, 0:2 * D] = a["hy_f_wout_2"][0]
    hy = a["hy_w_in_2"][0]
    for c in range(4):
        tiles = [8 + 2 * c, 16 + 2 * c, 9 + 2 * c, 17 + 2 * c]
        put(C_HYZ0 + c, np.concatenate([hy[:, t * P:(t + 1) * P] for t in tiles], axis=1))
    for c in range(2):
        put(C_HYX0 + c, hy[:, 512 * c:512 * c + 512])
    up = a["ffn_w_up_2"][0]
    for c in range(KF // 2):
        cols = []
        for j in (2 * c, 2 * c + 1):
            cols += [up[:, FFN + j * P:FFN + (j + 1) * P], up[:, j * P:(j + 1) * P]]
        put(C_UP + c, np.concatenate(cols, axis=1))
    down = a["ffn_w_down_2"][0]
    for n in range(2):
        k0 = 0
        for q, k in enumerate(DOWN_K):
            put(C_DOWN + 3 * n + q, down[k0 * P:(k0 + k) * P, 512 * n:512 * n + 512])
            k0 += k

    def mod_part(w, width):
        n = w.shape[1] // width
        return w.reshape(KD, P, n, width).transpose(1, 2, 0, 3).reshape(P, n * KD * width)

    by_use = np.concatenate([np.arange(i * D, (i + 1) * D) for i in (0, 1, 3, 4, 2, 5)])
    mod_w = a["mod_w_2"][0][:, by_use]
    mod = np.stack([mod_part(mod_w[:, 0:3 * D], MOD_POOL_COLS), mod_part(mod_w[:, 3 * D:], MOD_DVE_COLS)])

    small = np.zeros((P, N_SMALL), f32)
    for name, v, n in (("norm_in", a["norm_in"][0], KD), ("norm_g1", a["norm_g_2"][0, 0], KD),
                       ("norm_g2", a["norm_g_2"][0, 1], KD), ("q_norm", a["mla_q_norm"][0], KQ),
                       ("kv_norm", a["mla_kv_norm"][0], KKV), ("hy_b_in", a["hy_b_in_2"][0], 24),
                       ("hy_sc_w", a["hy_sc_w_2"][0].reshape(-1), 72), ("hy_sc_b", a["hy_sc_b_2"][0], 24),
                       ("conv_w", a["ffn_conv_w_2"][0].reshape(-1), 9 * KF), ("conv_b", a["ffn_conv_b_2"][0], KF),
                       ("cond", a["c_2"][0], KD)):
        small[:, SMALL[name]] = _by_feature(v, n)
    small[:, SMALL["minus_t"]] = minus_t
    small[:, SMALL["ident"]] = np.eye(P, dtype=f32)
    early = np.zeros((P, N_EARLY), f32)
    early[0:EMB, EARLY["pos_emb"]] = pos_emb
    early[0:EMB, EARLY["f_w1"]] = a["hy_f_w1_2"][0]
    early[0:FW, EARLY["f_w2"]] = a["hy_f_w2_2"][0]
    early[0:FW, EARLY["f_w3"]] = a["hy_f_w3_2"][0]
    for i in range(3):
        early[0:FW, EARLY["f_b"].start + i] = a[f"hy_f_b{i + 1}_2"][0]
    early[0:FW, EARLY["freq"].start] = a["hy_freq_2"][0]
    rowed = np.zeros((P, N_ROWED), f32)
    rowed[:, ROWED["inv_freq"]] = (10000.0 ** (-np.arange(0, 64, 2, dtype=f32) / 64)).astype(f32)[None, :]
    rowed[:, ROWED["lam"]] = np.concatenate([a["diff_lambda_q1"][0], a["diff_lambda_k1"][0],
                                             a["diff_lambda_q2"][0], a["diff_lambda_k2"][0]])[None, :]
    rowed[:, ROWED["subln"]] = a["diff_subln"][0][None, :]
    masks = np.zeros((P, 2, P), f32)
    masks[:, 0, :] = np.eye(P)
    masks[:, 1, :] = np.where(np.arange(P)[None, :] > np.arange(P)[:, None], MASKED, 0.0)
    rows = np.stack([a["norm_final"], a["hy_b_out_2"][0], a["final_g_2"], a["hy_bias_2"][0]])

    arrays = {
        "x_in": a["x"][0], "pos_in": np.ascontiguousarray(a["positions"][0].reshape(TT, P).T.astype(np.int32)),
        "weights_in": stream, "mod_w_in": mod, "mod_b_in": a["mod_b_2"][:, by_use], "small_in": small, "early_in": early,
        "rowed_in": rowed, "masks_in": masks.reshape(P, 2 * P).astype(ml_dtypes.bfloat16),
        "tables_in": _transform_tables(), "deltas_in": deltas, "rows_in": rows,
    }
    arrays = {k: np.ascontiguousarray(v) for k, v in arrays.items()}
    nc = _bacc.Bacc("TRN2", target_bir_lowering=False, num_devices=1)
    args = [nc.dram_tensor(k, v.shape, mybir.dt.from_np(v.dtype), kind="ExternalInput").ap() for k, v in arrays.items()]
    out = nc.dram_tensor("y_out", (SEQ, D), F32, kind="ExternalOutput").ap()
    build_program(nc, *args, out)
    r = _run(nc, [arrays], core_ids=[0])
    return r.results[0]["y_out"].reshape(1, SEQ, D)
```

```python
from contextlib import ExitStack
import math

import numpy as np
import concourse.bass as bass
from concourse import mybir

F32 = mybir.dt.float32
BF16 = mybir.dt.bfloat16
F32R = mybir.dt.float32r
I32 = mybir.dt.int32
ALU = mybir.AluOpType
ACT = mybir.ActivationFunctionType
AX = mybir.AxisListType

P = 128
SEQ, D = 512, 1024
TT = SEQ // P
KD = D // P
NORM_EPS = 1e-6
HEADS = 4
HALF = 32
UNITS = 2 * HEADS
Q_RANK, KV_RANK = 384, 256
KQ, KKV = Q_RANK // P, KV_RANK // P
DIFF_SCALE = 64 ** -0.5
MLA_SCALE = 192 ** -0.5
LAMBDA_INIT = 0.8 - 0.6 * math.exp(0.0)
FFN = 2816
KF = FFN // P
ROWS, COLS = SEQ // 64, 64
BANDS = 16
EMB = 1 + 2 * BANDS
FW = 64
NF = SEQ // 2
SLOT = 4096
RING = 3
MASKED = -1e30
MOD_POOL_COLS = 128
MOD_POOL = 4 * D // MOD_POOL_COLS
MOD_DVE_COLS = 256
LOADS_AFTER = (1, 6, 9, 11, 14, 16, 20)
ROOTS_AFTER = (12, 20, 22, 24, 26)
MOD_DVE = 2 * D // MOD_DVE_COLS

TWO_PI = 2.0 * math.pi
PI_1 = 6.28125
PI_2 = float(np.float32(np.round((TWO_PI - PI_1) * 2 ** 20) / 2 ** 20))
PI_3 = float(np.float32(TWO_PI - PI_1 - PI_2))
ROUNDER = 1.5 * 2.0 ** 23
PI_BELOW = float(np.nextafter(np.float32(math.pi), np.float32(0)))

SMALL = {}
_at = 0
for _name, _n in (("norm_in", KD), ("norm_g1", KD), ("norm_g2", KD), ("q_norm", KQ), ("kv_norm", KKV),
                  ("hy_b_in", 24), ("hy_sc_w", 72), ("hy_sc_b", 24), ("conv_w", 9 * KF), ("conv_b", KF),
                  ("cond", KD), ("mod_b", 4 * KD), ("minus_t", TT), ("ident", P)):
    SMALL[_name] = slice(_at, _at + _n)
    _at += _n
N_SMALL = _at

EARLY = {}
_at = 0
for _name, _n in (("pos_emb", SEQ), ("f_w1", FW), ("f_w2", FW), ("f_w3", FW), ("f_b", 3), ("freq", 1)):
    EARLY[_name] = slice(_at, _at + _n)
    _at += _n
N_EARLY = _at
ROWED = {}
_at = 0
for _name, _n in (("inv_freq", HALF), ("lam", 4 * 64), ("subln", P)):
    ROWED[_name] = slice(_at, _at + _n)
    _at += _n
N_ROWED = _at

(C_DQ, C_DK, C_DV, C_LAT0, C_LAT1, C_DGATE, C_UQ, C_UKV, C_MGATE, C_GD0, C_GD1, C_GM0, C_GM1,
 C_PD, C_PM, C_WO0, C_WO1, C_FOUT, C_HYZ0) = range(19)
C_HYX0 = C_HYZ0 + 4
C_HYO = C_HYX0 + 2
C_UP = C_HYO + 2
C_DOWN = C_UP + KF // 2
DOWN_K = (8, 8, 6)
N_CHUNKS = C_DOWN + 2 * len(DOWN_K)


WHOLE = (C_UQ, C_UKV, C_PD, C_PM, C_WO0, C_WO1, C_FOUT)
BY_TOKENS = (C_DQ, C_DK, C_DV, C_LAT0, C_LAT1, C_DGATE, C_MGATE, C_HYO, C_HYO + 1)
LAT_W = (Q_RANK + KV_RANK + 2 * HALF) // 2
PIECE = SLOT // 4
PIECES = 4


def slot_of(c):
    return RING - 1 if c == C_WO0 else (c if c < C_WO0 else c - 1) % (RING - 1)


def build_program(nc, x_d, pos_d, stream_d, mod_d, mod_b_d, small_d, early_d, rowed_d, masks_d,
                  tables_d, deltas_d, rows_d, spill_d, mod_spill_d, out_d):
    ctx = ExitStack()
    sems = {}

    def sem(name):
        if name not in sems:
            sems[name] = ctx.enter_context(nc.semaphore(name))
        return sems[name]

    with ctx:
        def sb(name, shape, dt=F32):
            return ctx.enter_context(nc.sbuf_tensor(name, shape, dt))

        twins = {}

        def sb_twice(name, shape, places=None):
            t = sb(name, shape)
            size = math.prod(shape[1:])
            at = nc.sbuf_base - 4 * size
            if places is None:
                twins[name] = [(0, size, nc.alloc_sbuf_tensor_at(name + "_parts", shape, F32R, offset=at))]
            else:
                twins[name] = [(a, b, nc.alloc_sbuf_tensor_at(f"{name}_parts{a}", [P, b - a], F32R, offset=at + 4 * a))
                               for a, b in places]
            return t

        def part(ap):
            n = ap.ap[0][1]
            a, b, twin = next(x for x in twins[ap.tensor.name] if x[0] <= ap.offset < x[1])
            return bass.AP(twin, ap.offset - a, [[b - a, n]] + [list(x) for x in ap.ap[1:]])

        x_sb = sb_twice("x_sb", [P, TT, D])
        hT = sb_twice("hT", [P, KD, SEQ])
        ring = sb_twice("ring", [P, RING, SLOT])
        mod_g = sb("mod_g", [P, 2, D])
        row = sb("row", [P, D])
        small = sb("small", [P, N_SMALL])
        pos_sb = sb("pos_sb", [P, TT], I32)
        masks = sb("masks", [P, 2, P], BF16)
        stat = sb("stat", [P, 96])
        sums = sb("sums", [P, 64])
        mod_part = sb("mod_part", [P, 2 * MOD_POOL_COLS])
        modc = sb("modc", [P, 4 * KD])
        arena = sb_twice("arena", [P, 111 * 256], [(256 * a, 256 * b) for a, b in ((0, 44), (54, 70), (70, 111))])
        bank = [ctx.enter_context(nc.psum_tensor(f"bank{i}", [P, 512], F32))[:, :] for i in range(8)]

        def at(kb, n, tiles=None):
            ap = arena[:, int(kb * 256):int(kb * 256) + n]
            return ap if tiles is None else ap.rearrange("p (a b) -> p a b", a=tiles)

        ident = small[:, SMALL["ident"]]

        def sm(name, i, parts=P):
            c = SMALL[name].start + i
            return small[0:parts, c:c + 1]

        qT = at(0, 2048, HEADS)
        kT = at(8, 2048, HEADS)
        dv = at(16, 2048, TT)
        qn = at(24, 2048, HEADS)
        kn = at(32, 2048, HEADS)
        mv = at(40, 2048, TT)
        qrT = at(48, 1024, 2)
        krT = at(52, 512)
        early = at(24, N_EARLY)
        net = [at(27 + 2 * i, 512) for i in range(4)]
        lat = at(54, TT * 704, TT)
        cqT = at(65, KQ * SEQ, KQ)
        ckvT = at(71, KKV * SEQ, KKV)
        roped = [at(75, 2048, TT), at(83, 2048, TT)]
        kr2 = at(83, TT * P, TT)
        qr = at(85, 1024, TT)
        dgate = at(75, 2048, TT)
        mgate = at(83, 2048, TT)
        modw_dve = at(91, 2048, KD)
        modw_pool = [at(99, 1024, KD), at(103, 1024, KD)]
        n1_temp = at(75, KD * SEQ, KD)
        mod_back = at(75, 4 * D)
        rowed = at(107, N_ROWED)
        cos_t, sin_t, nsin_t = (at(109 + 0.5 * i, 128) for i in range(3))
        probs1 = [at(54, 1280), at(59, 1280)]
        probs2 = at(64, 1280)
        pT = [at(69, 512), at(71, 512)]
        o_sq = at(73, 512, TT)
        o_tok = [at(107, 512, TT), at(109, 512, TT)]
        sgd = at(91, KD * SEQ, KD)
        sgm = at(32, KD * SEQ, KD)
        junk = at(54, D)
        x_norm = at(16, TT * D, TT)
        norm_row = at(48, D)
        filt = [hT[:, i, :] for i in range(4)]
        abs_sum = [hT[:, 4 + n, :] for n in range(2)]
        deltas = hT[:, 6:8, :].rearrange("p a b -> p (a b)")
        bias_row = at(107, D)[0:1, :]
        norm_sb = at(58, D)[0:1, :]
        decay = [at(62 + 2 * i, 512) for i in range(2)]
        abs_tap = [at(66 + 2 * i, 512) for i in range(2)]
        ones_sq = at(109, P)
        z_buf = [at(52, 512), at(107, 512)]
        x1c, vc = at(48, 512), at(50, 512)
        h3T = row[0:FW, 0:SEQ]
        rope_tmp = row[:, SEQ:D]
        fwd_cos = at(75, 1024, 4)
        fwd_sin = at(79, 1024, 4)
        inv = at(83, 2048, 8)
        kp = at(58, 4096, 4)
        km = at(91, 4096, 4)
        x0c = at(0, KD * SEQ, KD)
        zT = at(16, 4096, 4)
        uv = at(32, 4096, 8)
        padded = [row[:, 0:SEQ + 2], at(55, SEQ + 2)]
        tmp = [at(48 + 2 * i, 512) for i in range(5)] + [at(107 + 2 * i, 512) for i in range(2)]
        hid = at(0, KF * SEQ, KF)
        image = [at(44 + 3 * i, (ROWS + 2) * (COLS + 2)).rearrange("p (r c) -> p r c", c=COLS + 2) for i in range(2)]
        conv = [at(50 + 2 * i, 512) for i in range(2)]
        x_low = x_sb[:].rearrange("p a (b c) -> p (a b) c", c=SEQ)
        hT_low = at(54, KD * SEQ, KD)
        out_tok = [at(58 + 4 * i, D) for i in range(2)]

        def hid_high(k):
            return at(70 + 2 * k, 512) if k < 20 else hT[:, k - 20, :]

        SS, RS, SS_L, RS_L, SS_H, RS_H, SS2, RS2 = 0, 4, 8, 16, 24, 32, 40, 44
        MHALF, ONE, NLAM, CSILU, RNORM = 64, 68, 69, 70, 78

        def st(c, n=1, parts=P):
            return stat[0:parts, c:c + n]

        def chunk(c):
            return ring[:, slot_of(c), :]

        def chunk_landed(eng, c):
            i = sum(slot_of(b) == slot_of(c) for b in range(c + 1))
            eng.wait_ge(sem(f"chunk_landed{slot_of(c)}"), 16 * i)

        pieces = []
        for n, c in enumerate((C_DQ, C_DK, C_DV, C_LAT0, C_LAT1)):
            pieces += [(c, j, "in_done", TT * (4 * n + j + 1)) for j in range(4)]
        pieces += [(C_DGATE, j, "dgate_done", TT * (j + 1)) for j in range(4)]
        FIRST_MGATE = len(pieces)
        pieces += [(C_MGATE, j, "fill_done", 4) for j in range(4)]
        FIRST_GATE = len(pieces)
        pieces += [(C_GD0, j, "fill_done", j + 5) for j in range(4)]
        pieces += [((C_GD1, C_GM0, C_GM1)[j // 4], j % 4, "gate_done", j + 1) for j in range(12)]
        FIRST_HYZ = len(pieces)
        pieces += [(C_HYZ0 + j // 4, j % 4, "hyz_done", j + 1) for j in range(16)]
        FIRST_HYX = len(pieces)
        pieces += [(C_HYX0 + j // 4, j % 4, "hyx_done", j + 1) for j in range(KD)]
        FIRST_HYO = len(pieces)
        pieces += [(C_HYO + j // 4, j % 4, "hyo_done", TT * (j + 1)) for j in range(KD)]
        FIRST_UP = len(pieces)
        pieces += [(C_UP + j // 4, j % 4, "up_done", j + 1) for j in range(2 * KF)]
        FIRST_DOWN = len(pieces)
        for n in range(2):
            for q, k in enumerate(DOWN_K):
                pieces += [(C_DOWN + 3 * n + q, j, "down_done", TT * (len(pieces) + j - FIRST_DOWN + 1)) for j in range(k // 2)]

        def piece_parts(p):
            c, j = pieces[p][0:2]
            high = ring[:, RING - 1, (p % PIECES) * PIECE:(p % PIECES + 1) * PIECE]
            if c in BY_TOKENS or c >= C_DOWN:
                n = 2 * (LAT_W if c in (C_LAT0, C_LAT1) else 512)
                return chunk(c)[:, j * n:(j + 1) * n], high[:, 0:n]
            return (chunk(c).rearrange("p (k f) -> p k f", k=KD)[:, :, j * P:(j + 1) * P],
                    high.rearrange("p (k f) -> p k f", k=KD))

        def piece_done(p):
            return pieces[p][2:4]

        OFF = [0, 128, 384, 768]

        def score_place(a, i):
            return ((2 + a, 384), (4, 256 * a), (2 + a, 0), (a, 0))[i]

        chunk_used = {C_UQ: ("latq_done", 8), C_UKV: ("latk_done", 8), C_PD: ("merge_done", 16),
                      C_PM: ("merge_done", 16), C_WO0: ("wo_done", 8), C_WO1: ("wo_done", 8),
                      C_FOUT: ("taps_done", 8)}
        for c, _, name, count in pieces:
            chunk_used[c] = (name, count)

        split_at = {"n1": 0, "n2": 2 * KD, "n3": 4 * KD}

        def exps_before(u):
            return 8 * min(u, HEADS) + 4 * max(u - HEADS, 0)

        def scores_at(u):
            return 2 * u + 2 if u < HEADS else 2 * HEADS + u - HEADS + 1

        def squares_at(name, i):
            if name == "x1":
                return 12 + max(2 * i, 1)
            if name == "x2":
                return min(15 + 2 * i, 20)
            return {"n1": 1, "lat": 5, "x3": 21, "x4": 25}[name] + i

        def mod_sum(j):
            return mod_back[:, j * P:(j + 1) * P]

        def in_done_at(i):
            return 16 * (i // 4) + 12 + i % 4 + 1

        def in_bank(i):
            return bank[(4, 0)[i // 4 % 2] + i % 4]

        def taps(d, n):
            return at((32, 0)[n] + 8 * d, 2048, 4)

        block = ctx.enter_context(nc.Block())

        @block.sync
        def _(sp):
            for m in range(TT):
                sp.dma_start(x_sb[:, m, :], x_d[m * P:(m + 1) * P, :]).then_inc(sem(f"x_in{m}"), 16)
            for c in range(N_CHUNKS):
                before = [b for b in range(c) if slot_of(b) == slot_of(c)]
                if c == C_WO0:
                    sp.wait_ge(sem("gate_done"), 12)
                elif before:
                    name, count = chunk_used[before[-1]]
                    sp.wait_ge(sem(name), count)
                sp.dma_start(chunk(c), stream_d[c]).then_inc(sem(f"chunk_landed{slot_of(c)}"), 16)
                if c == C_HYO + 1:
                    for m in range(TT):
                        sp.dma_start(x_sb[:, m, :], spill_d[m * P:(m + 1) * P, :]).then_inc(sem(f"x_in{m}"), 16)
            for m in range(TT):
                sp.wait_ge(sem("y_ready"), m + 1)
                sp.dma_start(out_d[m * P:(m + 1) * P, :], out_tok[m % 2]).then_inc(sem(f"y_stored{m % 2}"), 16)
            for i in range(2):
                sp.wait_ge(sem(f"y_stored{i}"), 16 * TT // 2)

        @block.tensor
        def _(pe):
            held = {}

            def take(b, name, count):
                if b in held and held[b] != (name, count):
                    pe.wait_ge(sem(held[b][0]), held[b][1])
                held[b] = (name, count)

            def product(out, pairs):
                for n, (l, r) in enumerate(pairs):
                    ins = nc.tensor.matmul(out, l, r, start=n == 0, stop=n == len(pairs) - 1)
                return ins

            def product3(out, lefts, rights, start=True, stop=True):
                passes = [(part(l[i]), part(r[j])) for i, j in ((0, 0), (0, 1), (1, 0))
                          for l, r in zip(lefts, rights)]
                for n, (l, r) in enumerate(passes):
                    ins = nc.tensor.matmul(out, l, r, start=start and n == 0, stop=stop and n == len(passes) - 1)
                return ins

            def turn(b, blocks):
                for n, x in enumerate(blocks):
                    ins = nc.tensor.transpose(bank[b][0:x.shape[1], n * P:(n + 1) * P], x, ident)
                return ins

            def split_tile(p, low_input, b, name, out, count):
                pe.wait_ge(sem("piece_low"), p + 1)
                take(b, out, count)
                low, high = piece_parts(p)
                product3(bank[b], [(high[:, k, :], low[:, k, :]) for k in range(KD)],
                         [(hT[:, k, :], low_input[:, k, :]) for k in range(KD)]).then_inc(sem(name), 1)

            def tok(k, m):
                return hT[:, k, m * P:(m + 1) * P]

            def cols(c, k, a, n, width=512):
                return chunk(c)[:, k * width + a:k * width + a + n]

            pe.wait_ge(sem("small_in"), 16)
            pe.wait_ge(sem("n1_scaled"), TT)
            for k in range(KD):
                take(k % 4, "n1_out", k + 1)
                turn(k % 4, [x_sb[:, m, k * P:(k + 1) * P] for m in range(TT)]).then_inc(sem("n1_turned"), 1)
            pe.wait_ge(sem("n1_out"), KD)

            pe.wait_ge(sem("early_in"), 16)

            def net_layer(i, b):
                take(b, "net_read", i + 1)
                w = early[0:(EMB, FW, FW)[i], EARLY[f"f_w{i + 1}"]]
                if i:
                    pe.wait_ge(sem("net_out"), i)
                x = early[0:EMB, EARLY["pos_emb"]] if i == 0 else net[0][0:FW, :]
                nc.tensor.matmul(bank[b][0:FW, :], w, x, start=True, stop=True).then_inc(sem("net_done"), 1)

            def project_tokens(p, n_pieces, width, b0, name, held_by, inputs, high_part, low_part):
                for q in range(n_pieces):
                    pe.wait_ge(sem("piece_low"), p + q + 1)
                    inputs(q)
                    low, high = piece_parts(p + q)
                    for m in range(TT):
                        if q == 0:
                            take(b0 + m, *held_by(m))
                        tokens = slice(m * P, (m + 1) * P)
                        product3(bank[b0 + m][:, 0:width],
                                 [(high_part(2 * q + i)[:, tokens], low_part(2 * q + i)[:, tokens]) for i in range(2)],
                                 [(high[:, i * width:(i + 1) * width], low[:, i * width:(i + 1) * width]) for i in range(2)],
                                 start=q == 0, stop=q == n_pieces - 1).then_inc(sem(name), 1)

            def hT_high(k):
                return hT[:, k, :]

            def x_low_k(k):
                return x_low[:, k, :]

            def input_chunk(n, width):
                def held_by(m):
                    i = 4 * n + m
                    return ("rope_out", i + 1) if i < 8 else ("in_out", i - 7)

                def inputs(q):
                    if n == 0:
                        pe.wait_ge(sem("input_split"), KD + 2 * q + 2)

                project_tokens(4 * n, 4, width, (4, 0)[n % 2], "in_done", held_by, inputs, hT_high, x_low_k)

            net_layer(0, 0)
            input_chunk(0, 512)
            input_chunk(1, 512)
            input_chunk(2, 512)

            def turn_roped(t):
                pe.wait_ge(sem("rope_out"), 4 * t + 4)
                for h in range(HEADS):
                    i = 4 * t + h
                    take(i % 4, "qk_out", i + 1)
                    turn(i % 4, [roped[t][:, m, h * P:(h + 1) * P] for m in range(TT)]).then_inc(sem("qk_turned"), 1)

            turn_roped(0)
            net_layer(1, 3)
            input_chunk(3, LAT_W)
            net_layer(2, 7)
            input_chunk(4, LAT_W)
            turn_roped(1)
            project_tokens(20, 4, 512, 4, "dgate_done", lambda m: ("dgate_out", m + 1), lambda q: None, hT_high, x_low_k)
            pe.wait_ge(sem("kr_ready"), 1)
            take(0, "lat_out", 1)
            turn(0, [kr2[:, m, :] for m in range(TT)]).then_inc(sem("lat_turned"), 1)
            pe.wait_ge(sem("lat_scaled"), 2)
            for i in range(KQ + KKV):
                take((i + 1) % 4, "lat_out", i + 2)
                turn((i + 1) % 4, [lat[:, m, i * P:(i + 1) * P] for m in range(TT)]).then_inc(sem("lat_turned"), 1)
            pe.wait_ge(sem("lat_out"), 1 + KQ)
            chunk_landed(pe, C_UQ)
            for m in range(TT):
                take(4 + m, "qr_out", m + 1)
                product(bank[4 + m][:, 0:256], [(cqT[:, k, m * P:(m + 1) * P], cols(C_UQ, k, 512, 256, 768))
                                                for k in range(KQ)]).then_inc(sem("latq_done"), 1)
            for h in range(HEADS):
                take(4 + h, "qn_out", h + 1)
                product(bank[4 + h], [(cols(C_UQ, k, h * P, P, 768), cqT[:, k, :]) for k in range(KQ)]).then_inc(sem("latq_done"), 1)
            pe.wait_ge(sem("lat_out"), 1 + KQ + KKV)
            chunk_landed(pe, C_UKV)
            for h in range(HEADS):
                take(4 + h, "latk_out", h + 1)
                product(bank[4 + h], [(cols(C_UKV, k, h * P, P, 1024), ckvT[:, k, :]) for k in range(KKV)]).then_inc(sem("latk_done"), 1)
            for m in range(TT):
                take(4 + m, "latk_out", HEADS + m + 1)
                product(bank[4 + m], [(ckvT[:, k, m * P:(m + 1) * P], cols(C_UKV, k, 512, 512, 1024))
                                      for k in range(KKV)]).then_inc(sem("latk_done"), 1)
            pe.wait_ge(sem("qr_out"), TT)
            for b in range(2):
                take(b, "qrT_out", b + 1)
                turn(b, [qr[:, m, b * P:(b + 1) * P] for m in range(TT)]).then_inc(sem("qr_turned"), 1)

            pe.wait_ge(sem("masks_in"), 16)

            def scores(u):
                latent, h = u >= HEADS, u % HEADS
                if u == 0:
                    pe.wait_ge(sem("qk_out"), 8)
                if u == HEADS:
                    pe.wait_ge(sem("latk_out"), 2 * HEADS)
                    pe.wait_ge(sem("qn_out"), HEADS)
                    pe.wait_ge(sem("qrT_out"), 2)
                done = exps_before(u + 1)
                for b in range(5):
                    take(b, "exp_out", done)
                for a in range(1 if latent else 2):
                    for i in (0, 2, 3, 1):
                        if a == 1 and i == 1:
                            pe.wait_ge(sem("scores_done"), 2 * u + 1)
                        b, c = score_place(a, i)
                        n = (i + 1) * P
                        out = bank[b][:, c:c + n]
                        q = slice(i * P, (i + 1) * P)
                        if latent:
                            half = slice(64 * (h % 2), 64 * (h % 2) + 64)
                            nc.tensor.matmul(out, qn[:, h, q], kn[:, h, 0:n], start=True, stop=False)
                            nc.tensor.matmul(out, qrT[half, h // 2, q], krT[half, 0:n], start=False, stop=False)
                        else:
                            half = slice(64 * a, 64 * a + 64)
                            nc.tensor.matmul(out, qT[half, h, q], kT[half, h, 0:n], start=True, stop=False)
                        ins = nc.tensor.matmul(bank[b][:, c + i * P:c + n], masks[:, 0, :], masks[:, 1, :],
                                               start=False, stop=True)
                    ins.then_inc(sem("scores_done"), 1)

            def fill(u):
                b = 5
                take(b, "fill_out", u + 1)
                if u < 4:
                    pe.wait_ge(sem("piece_low"), FIRST_MGATE + 4)
                    tokens = slice(u * P, (u + 1) * P)
                    lefts = [(hT[:, k, tokens], x_low[:, k, tokens]) for k in range(KD)]
                    rights = []
                    for k in range(KD):
                        low, high = piece_parts(FIRST_MGATE + k // 2)
                        c = slice(512 * (k % 2), 512 * (k % 2) + 512)
                        rights.append((high[:, c], low[:, c]))
                    ins = product3(bank[b], lefts, rights)
                else:
                    pe.wait_ge(sem("piece_low"), FIRST_GATE + u - 4 + 1)
                    low, high = piece_parts(FIRST_GATE + u - 4)
                    ins = product3(bank[b], [(high[:, k, :], low[:, k, :]) for k in range(KD)],
                                   [(hT[:, k, :], x_low[:, k, :]) for k in range(KD)])
                ins.then_inc(sem("fill_done"), 1)

            def values(u):
                latent, h = u >= HEADS, u % HEADS
                p1 = probs1[u % 2]

                def turn_probs(i):
                    b = 5 + i % 2
                    pe.wait_ge(sem("probs_ready"), 4 * u + i + 1)
                    take(b, "pT_out", 4 * u + i + 1)
                    turn(b, [p1[:, OFF[i] + j * P:OFF[i] + (j + 1) * P] for j in range(i + 1)]).then_inc(sem("p_turned"), 1)

                def weigh(i):
                    pe.wait_ge(sem("pT_out"), 4 * u + i + 1)
                    v = mv if latent else dv
                    if i == 0:
                        take(7, "o_read", u + 1)
                    product(bank[7][:, i * P:(i + 1) * P],
                            [(pT[i % 2][:, j * P:(j + 1) * P], v[:, j, h * P:(h + 1) * P])
                             for j in range(i + 1)]).then_inc(sem("pv_done"), 1)

                turn_probs(0)
                turn_probs(1)
                weigh(0)
                turn_probs(2)
                weigh(1)
                turn_probs(3)
                weigh(2)
                weigh(3)

            def turn_output(u):
                pe.wait_ge(sem("o_ready"), u + 1)
                take(6, "oT_out", u + 1)
                turn(6, [o_tok[u % 2][:, m, :] for m in range(TT)]).then_inc(sem("o_turned"), 1)

            scores(0)
            fill(0)
            for u in range(UNITS):
                if u + 1 < UNITS:
                    scores(u + 1)
                    fill(u + 1)
                values(u)
                if u:
                    turn_output(u - 1)

            for i in range(12):
                split_tile(FIRST_GATE + 4 + i, x_low, i % 4, "gate_done", "gate_out", i + 1)
                if i == 1:
                    turn_output(UNITS - 1)

            chunk_landed(pe, C_PD)
            chunk_landed(pe, C_PM)
            pe.wait_ge(sem("oT_out"), UNITS)
            for d in range(KD):
                for s, (c, o) in enumerate(((C_PD, qT), (C_PM, qn))):
                    b = (2 * d + s) % 8
                    take(b, "merge_out", d + 1)
                    product(bank[b], [(cols(c, k, d * P, P, D), o[:, k, :]) for k in range(HEADS)]).then_inc(sem("merge_done"), 1)

            pe.wait_ge(sem("mod_back_in"), 16)
            pe.wait_ge(sem("mod_dve_done"), MOD_DVE)
            pe.wait_ge(sem("ones_ready"), 1)
            take(4, "modc_read", 1)
            for j in range(4 * KD):
                ins = nc.tensor.matmul(bank[4][:, j:j + 1], mod_sum(j), st(ONE), start=True, stop=True)
            ins.then_inc(sem("modc_done"), 1)
            for j in range(4):
                b = (5, 6, 7, 4)[j]
                take(b, "modg_out", j + 1)
                nc.tensor.matmul(bank[b], ones_sq, mod_g[:, j // 2, (j % 2) * 512:(j % 2) * 512 + 512],
                                 start=True, stop=True).then_inc(sem("modg_done"), 1)

            pe.wait_ge(sem("merge_out"), KD)
            chunk_landed(pe, C_WO0)
            chunk_landed(pe, C_WO1)
            for m in range(TT):
                for n in range(2):
                    i = 2 * m + n
                    take(i % 3, "wo_out", i + 1)
                    product(bank[i % 3], [(sgd[:, k, m * P:(m + 1) * P], cols(C_WO0 + n, k, 0, 512))
                                          for k in range(KD)]).then_inc(sem("wo_done"), 1)
                    if i == 0:
                        chunk_landed(pe, C_FOUT)
                    tn, t = i // 4, i % 4
                    for d in range(2):
                        b = 4 + 2 * (i % 2) + d
                        take(b, "taps_scaled", i + 1)
                        ins = nc.tensor.matmul(bank[b], h3T[:, t * P:(t + 1) * P],
                                               chunk(C_FOUT)[0:FW, d * D + tn * 512:d * D + tn * 512 + 512],
                                               start=True, stop=True)
                    ins.then_inc(sem("taps_done"), 1)
            for n in range(2):
                pe.wait_ge(sem("abs_step"), 4 * n + 4)
                take(3, "norm_read", n + 1)
                nc.tensor.matmul(bank[3][0:1, :], st(ONE), abs_sum[n], start=True, stop=True).then_inc(sem("norm_done"), 1)
            pe.wait_ge(sem("norm_read"), 2)
            take(3, "rnorm_read", 1)
            for j in range(KD):
                ins = nc.tensor.matmul(bank[3][:, j:j + 1], norm_sb[:, j * P:(j + 1) * P], stat[0:1, ONE:ONE + 1],
                                       start=True, stop=True)
            ins.then_inc(sem("rnorm_done"), 1)

            def transform(jobs_done, out_name, i, cos_in, sin_in, f, n0):
                fs = slice(f * P, (f + 1) * P)
                for b in range(4):
                    take(n0 + b, out_name, i + 1)
                    t, x = (fwd_cos, cos_in) if b < 2 else (fwd_sin, sin_in)
                    k0 = 2 * (b % 2)
                    ins = product(bank[n0 + b], [(t[:, k, fs], x(k)) for k in (k0, k0 + 1)])
                ins.then_inc(sem(jobs_done), 1)

            pe.wait_ge(sem("tables_in"), 16)
            for n in range(2):
                pe.wait_ge(sem("taps_ready"), 4 * n + 4)
                pe.wait_ge(sem("bias_in_taps"), n + 1)
                for f in range(2):
                    i = 2 * n + f
                    transform("kdft_done", "kdft_read", i, lambda k, n=n: taps(0, n)[:, k, :],
                              lambda k, n=n: taps(1, n)[:, k, :], f, 4 * (i % 2))

            def turn_normed(tag, src, b0):
                pe.wait_ge(sem(f"{tag}_scaled"), TT)
                for k in range(KD):
                    take(b0 + k % 4, f"{tag}_out", k + 1)
                    turn(b0 + k % 4, [src[:, m, k * P:(k + 1) * P] for m in range(TT)]).then_inc(sem(f"{tag}_turned"), 1)
                pe.wait_ge(sem("input_split"), split_at[tag] + 2 * KD)

            turn_normed("n2", x_norm, 0)

            def turn_z(c):
                pe.wait_ge(sem("z_ready"), c + 1)
                take(c % 4, "zT_out", c + 1)
                z = z_buf[c % 2].rearrange("p (a two) -> p two a", two=2)
                turn(c % 4, [z[:, t // 2, (t % 2) * P:(t % 2) * P + P] for t in range(4)]).then_inc(sem("z_turned"), 1)

            for i in range(16):
                split_tile(FIRST_HYZ + i, x_low, 4 + i % 4, "hyz_done", "hyz_out", i + 1)
                if i >= 4 and i % 2 == 1:
                    turn_z((i - 4) // 2)
            hyx_at = [0]

            def hyx(n):
                for _ in range(n):
                    i = hyx_at[0]
                    split_tile(FIRST_HYX + i, x_low, 4 + i % 2, "hyx_done", "hyx_out", i + 1)
                    hyx_at[0] += 1

            hyx(1)
            turn_z(6)
            hyx(1)
            turn_z(7)
            pe.wait_ge(sem("zT_out"), 8)

            def inverse(n):
                pe.wait_ge(sem("uv_ready"), 2 * n + 2)
                for q in range(4):
                    i = 4 * n + q
                    take(6 + i % 2, "y_out", i + 1)
                    for odd in range(2):
                        parts = [(uv[:, 2 * (2 * odd + s) + f, q * P:(q + 1) * P], inv[:, 4 * s + 2 * odd + f, :])
                                 for s in range(2) for f in range(2)]
                        ins = product(bank[6 + i % 2][:, odd * NF:(odd + 1) * NF], parts)
                    ins.then_inc(sem("y_done"), 1)

            for n in range(2):
                for f in range(2):
                    i = 2 * n + f
                    x = lambda k, n=n: zT[:, k, n * 512:(n + 1) * 512]
                    transform("dft_done", "dft_read", i, x, x, f, 0)
                    hyx(2 if i < 3 else 0)
                inverse(n)

            def output_half(n, p, n_pieces, name, out, k_ready, high_part, low_part):
                def inputs(q):
                    if n == 0:
                        pe.wait_ge(sem(k_ready), 2 * q + 2)

                project_tokens(p + n * n_pieces, n_pieces, 512, 4 * n, name, lambda m: (out, 4 * n + m + 1),
                               inputs, high_part, low_part)

            for n in range(2):
                output_half(n, FIRST_HYO, 4, "hyo_done", "hyo_out", "y_low", hT_high, lambda k: x0c[:, k, :])

            turn_normed("n3", x_norm, 0)
            for i in range(2 * KF):
                split_tile(FIRST_UP + i, hT_low, i % 8, "up_done", "image_out" if i % 2 == 0 else "hid_out", i // 2 + 1)
            for n in range(2):
                output_half(n, FIRST_DOWN, KF // 2, "down_done", "down_out", "hid_low", hid_high, lambda k: hid[:, k, :])

        @block.scalar
        def _(act):
            def wait(name, count):
                act.wait_ge(sem(name), count)

            def copy(out, in_):
                return nc.scalar.activation(out, in_, ACT.Copy)

            def split_high(p):
                chunk_landed(act, pieces[p][0])
                if p == FIRST_HYZ:
                    wait(*chunk_used[C_WO0])
                elif p >= PIECES and not FIRST_HYZ < p < FIRST_HYZ + PIECES:
                    wait(*piece_done(p - PIECES))
                low, high = piece_parts(p)
                copy(part(high), low).then_inc(sem("piece_high"), 1)

            squares = [0]

            def square(x, c, name, i, scratch=junk):
                if squares[0]:
                    wait("squares_done", squares[0])
                squares[0] += 1
                assert squares[0] == squares_at(name, i)
                nc.scalar.activation(scratch[:, 0:x.shape[1]], x, ACT.Square, accum_out=st(c)).then_inc(sem("squares_done"), 1)

            act.dma_start(small[:], small_d).then_inc(sem("small_in"), 16)
            act.dma_start(early, early_d).then_inc(sem("early_in"), 16)
            act.dma_start(rowed, rowed_d).then_inc(sem("rowed_in"), 16)
            act.dma_start(pos_sb[:], pos_d).then_inc(sem("pos_in"), 16)
            act.dma_start(masks[:], masks_d.rearrange("p (a b) -> p a b", a=2)).then_inc(sem("masks_in"), 16)
            for m in range(TT):
                wait(f"x_in{m}", 16)
                square(x_sb[:, m, :], SS + m, "n1", m)
            wait("small_in", 16)
            nc.scalar.activation(st(CSILU, KD), small[:, SMALL["cond"]], ACT.Silu).then_inc(sem("cond_ready"), 1)
            for k in range(KD):
                wait("n1_turned", k + 1)
                nc.scalar.activation(n1_temp[:, k, :], bank[k % 4], ACT.Identity, scale=sm("norm_in", k)).then_inc(sem("n1_out"), 1)
            for p in range(4):
                split_high(p)
            for i, t in enumerate((sin_t, cos_t)):
                wait("angle_ready", i + 1)
                nc.scalar.activation(t, t, ACT.Sin).then_inc(sem("rope_table"), 1)

            def net_out(i):
                wait("net_angle", i + 1)
                nc.scalar.activation(net[0][0:FW, :] if i < 2 else h3T, net[1][0:FW, :], ACT.Sin).then_inc(sem("net_out"), 1)

            def input_out(i):
                wait("in_done", in_done_at(i))
                m = i % 4
                if i < 12:
                    copy(dv[:, m, :], in_bank(i)).then_inc(sem("in_out"), 1)
                else:
                    c = LAT_W * (i // 4 - 3)
                    copy(lat[:, m, c:c + LAT_W], in_bank(i)[:, 0:LAT_W]).then_inc(sem("in_out"), 1)

            def qk_out(i):
                wait("qk_turned", i + 1)
                copy((qT, kT)[i // 4][:, i % 4, :], bank[i % 4]).then_inc(sem("qk_out"), 1)

            net_out(0)
            for p in range(4, 16):
                split_high(p)
            for i in range(8, 12):
                input_out(i)
            for i in range(4):
                qk_out(i)
            net_out(1)
            for p in range(16, 20):
                split_high(p)
            for i in range(12, 16):
                input_out(i)
            net_out(2)
            for p in range(20, 24):
                split_high(p)
            for i in range(16, 20):
                input_out(i)
            wait("lambda_sums", 1)
            nc.scalar.activation(sums[:, 60:62], sums[:, 62:64], ACT.Exp).then_inc(sem("lambda_exps"), 1)
            wait("in_out", 12)
            for m in range(TT):
                square(lat[:, m, 0:Q_RANK], SS_L + m, "lat", 2 * m, cqT[:, 0, :])
                square(lat[:, m, Q_RANK:Q_RANK + KV_RANK], SS_L + 4 + m, "lat", 2 * m + 1, cqT[:, 0, :])
            for i in range(4, 8):
                qk_out(i)
            for m in range(TT):
                wait("dgate_done", 12 + m + 1)
                nc.scalar.activation(dgate[:, m, :], bank[4 + m], ACT.Silu).then_inc(sem("dgate_out"), 1)
            for i in range(1 + KQ + KKV):
                wait("lat_turned", i + 1)
                b = bank[i % 4]
                if i == 0:
                    ins = copy(krT, b)
                elif i <= KQ:
                    ins = nc.scalar.activation(cqT[:, i - 1, :], b, ACT.Identity, scale=sm("q_norm", i - 1))
                else:
                    ins = nc.scalar.activation(ckvT[:, i - 1 - KQ, :], b, ACT.Identity, scale=sm("kv_norm", i - 1 - KQ))
                ins.then_inc(sem("lat_out"), 1)
            for h in range(HEADS):
                wait("latq_done", TT + h + 1)
                copy(qn[:, h, :], bank[4 + h]).then_inc(sem("qn_out"), 1)
            for i in range(8):
                wait("latk_done", i + 1)
                copy((kn, mv)[i // 4][:, i % 4, :], bank[4 + i % 4]).then_inc(sem("latk_out"), 1)
            for b in range(2):
                wait("qr_turned", b + 1)
                copy(qrT[:, b, :], bank[b]).then_inc(sem("qrT_out"), 1)

            for p in range(FIRST_MGATE, FIRST_GATE):
                split_high(p)

            def exps(u):
                latent = u >= HEADS
                base = 32 * (u % 2)
                wait("neg_max", u + 1)
                for a in range(1 if latent else 2):
                    if a == 0 and u >= 2:
                        wait("p_turned", 4 * (u - 1))
                    if a == 1 and u >= 1:
                        wait("probs_ready", 4 * u)
                    for i in range(TT):
                        b, c = score_place(a, i)
                        n = (i + 1) * P
                        p = (probs2 if a else probs1[u % 2])[:, OFF[i]:OFF[i] + n]
                        nc.scalar.activation(p, bank[b][:, c:c + n], ACT.Exp, bias=sums[:, base + 4 * a + i:base + 4 * a + i + 1],
                                             scale=MLA_SCALE if latent else DIFF_SCALE,
                                             accum_out=sums[:, base + 8 + 4 * a + i:base + 9 + 4 * a + i]).then_inc(sem("exp_out"), 1)

            def fill_out(u):
                wait("fill_done", u + 1)
                if u == 4:
                    wait("mod_dve_done", MOD_DVE)
                copy(mgate[:, u, :] if u < 4 else sgd[:, u - 4, :], bank[5]).then_inc(sem("fill_out"), 1)
                if u == 3:
                    wait("fill_out", 4)
                    nc.scalar.activation(mgate, mgate, ACT.Silu).then_inc(sem("mgate_ready"), 1)

            def probs_out(u):
                for i in range(TT):
                    n = 4 * u + i
                    wait("p_turned", n + 1)
                    if n >= 2:
                        wait("pv_done", n - 1)
                    copy(pT[i % 2][:, 0:(i + 1) * P], bank[5 + i % 2][:, 0:(i + 1) * P]).then_inc(sem("pT_out"), 1)

            def output_out(u):
                wait("o_turned", u + 1)
                copy((qn if u >= HEADS else qT)[:, u % HEADS, :], bank[6]).then_inc(sem("oT_out"), 1)

            exps(0)
            fill_out(0)
            for u in range(UNITS):
                if u + 1 < UNITS:
                    exps(u + 1)
                    fill_out(u + 1)
                if u >= 2:
                    split_high(FIRST_GATE + u - 2)
                probs_out(u)
                if u:
                    output_out(u - 1)
            split_high(FIRST_GATE + 6)
            split_high(FIRST_GATE + 7)
            wait("mod_pool_done", MOD_POOL)
            for i in range(12):
                if i < 8:
                    split_high(FIRST_GATE + 8 + i)
                wait("gate_done", i + 1)
                dst = sgd[:, 4 + i, :] if i < 4 else sgm[:, i - 4, :]
                nc.scalar.activation(dst, bank[i % 4], ACT.Sigmoid).then_inc(sem("gate_out"), 1)
                if i == 1:
                    output_out(UNITS - 1)
                if i == 2:
                    nc.scalar.activation(sgd[:, 0:4, :], sgd[:, 0:4, :], ACT.Sigmoid).then_inc(sem("sgd_ready"), 1)
            act.dma_start(norm_row, rows_d[0:1, :].partition_broadcast(P).rearrange("p a d -> p (a d)")).then_inc(sem("norm_row_in"), 16)
            wait("o_ready", UNITS)
            wait("mod_spilled", 16 * MOD_POOL // 2)
            act.dma_start(mod_back, mod_spill_d).then_inc(sem("mod_back_in"), 16)
            act.dma_start(deltas, deltas_d.partition_broadcast(P).rearrange("p a d -> p (a d)")).then_inc(sem("deltas_in"), 16)
            wait("gate_done", 12)
            for m in range(TT):
                act.dma_start(x_sb[:, m, :], x_d[m * P:(m + 1) * P, :]).then_inc(sem(f"x_in{m}"), 16)
            wait("modc_done", 1)
            act.dma_start(at(75, 4096), tables_d).then_inc(sem("tables_in"), 16)
            for j in range(4):
                wait("modg_done", j + 1)
                copy(mod_g[:, j // 2, (j % 2) * 512:(j % 2) * 512 + 512], bank[(5, 6, 7, 4)[j]]).then_inc(sem("modg_out"), 1)
            act.dma_start(bias_row, rows_d[3:4, :]).then_inc(sem("bias_in"), 16)

            wait("deltas_in", 16)
            for m in range(TT + 1):
                if m < TT:
                    for i in (2 * m, 2 * m + 1):
                        if i >= 2:
                            wait("taps_scaled", i - 1)
                        n, t = i // 4, i % 4
                        nc.scalar.activation(decay[i % 2], deltas[:, n * 512:n * 512 + 512], ACT.Exp,
                                             scale=sm("minus_t", t)).then_inc(sem("decay_ready"), 1)
                    for i in (2 * m, 2 * m + 1):
                        wait("taps_scaled", i + 1)
                        if i:
                            wait("abs_step", i)
                        for d in range(2):
                            nc.scalar.activation(abs_tap[d], filt[2 * (i % 2) + d], ACT.Abs).then_inc(sem("abs_ready"), 1)
                    wait("wo_out", 2 * m + 2)
                    square(x_sb[:, m, :], SS + m, "x1", m)
                if m:
                    wait("x2_ready", m)
                    act.dma_start(spill_d[(m - 1) * P:m * P, :], x_sb[:, m - 1, :]).then_inc(sem("x_spilled"), 16)
                    square(x_sb[:, m - 1, :], SS2 + m - 1, "x2", m - 1)
            wait("taps_ready", 8)
            for i in range(4):
                wait("kdft_done", i + 1)
                if i >= 2:
                    wait("kdft_read", i - 1)
                b0 = 4 * (i % 2)
                copy(filt[2 * (i % 2)], bank[b0 + 1]).then_inc(sem("kdft_copied"), 1)
                copy(filt[2 * (i % 2) + 1], bank[b0 + 3]).then_inc(sem("kdft_copied"), 1)
            wait("kdft_read", 4)
            wait("modc_ready", 1)

            def normed_out(tag, s, b0, dst=hT):
                for k in range(KD):
                    wait(f"{tag}_turned", k + 1)
                    nc.scalar.activation(dst[:, k, :], bank[b0 + k % 4], ACT.Identity,
                                         scale=modc[:, (2 * s + 1) * KD + k:(2 * s + 1) * KD + k + 1],
                                         bias=modc[:, 2 * s * KD + k:2 * s * KD + k + 1]).then_inc(sem(f"{tag}_out"), 1)

            for p in range(PIECES - 1):
                split_high(FIRST_HYZ + p)
            wait("x_spilled", 16 * TT)
            normed_out("n2", 0, 0, x_low)
            split_high(FIRST_HYZ + PIECES - 1)

            def hy_out(i, tile, b, place, name, done, conv_name):
                wait(done, i + 1)
                if conv_name:
                    wait(*conv_name)
                nc.scalar.activation(place[:, 1:SEQ + 1], bank[b], ACT.Identity, bias=sm("hy_b_in", tile)).then_inc(sem(name), 1)

            def z_out(c):
                wait("z_turned", c + 1)
                copy(zT[:, :, c * P:(c + 1) * P], bank[c % 4].rearrange("p (a b) -> p a b", a=4)).then_inc(sem("zT_out"), 1)

            wait("pads_ready", 1)
            for i in range(16):
                split_high(FIRST_HYZ + i + PIECES)
                hy_out(i, (8, 16)[i % 2] + i // 2, 4 + i % 4, padded[i % 2], "hyz_out", "hyz_done",
                       ("hyz_conv", i - 1) if i >= 2 else None)
                if i >= 4 and i % 2 == 1:
                    z_out((i - 4) // 2)

            def hyx_out(i):
                hy_out(i, i, 4 + i % 2, padded[0], "hyx_out", "hyx_done",
                       ("hyx_conv", i) if i >= 1 else ("hyz_conv", 16))

            hyx_out(0)
            split_high(FIRST_HYX + PIECES)
            z_out(6)
            hyx_out(1)
            split_high(FIRST_HYX + PIECES + 1)
            z_out(7)
            for i in range(4):
                wait("dft_done", i + 1)
                if i:
                    wait("uv_ready", i)
                copy(tmp[0], bank[1]).then_inc(sem("dft_copied"), 1)
                copy(tmp[1], bank[3]).then_inc(sem("dft_copied"), 1)
                if i < 3:
                    for t in (2 * i + 2, 2 * i + 3):
                        hyx_out(t)
                        split_high(FIRST_HYX + PIECES + t)
            for k in range(KD):
                wait("y_out", k + 1)
                copy(part(hT[:, k, :]), x0c[:, k, :]).then_inc(sem("y_high"), 1)
            wait("hyx_conv", 8)
            act.dma_start(row[:], rows_d[1:2, :].partition_broadcast(P).rearrange("p a d -> p (a d)")).then_inc(sem("b_out_in"), 16)
            for p in range(FIRST_HYO + PIECES, FIRST_UP + 3):
                split_high(p)
            for m in range(TT):
                wait("hyo_out", TT + m + 1)
                square(x_sb[:, m, :], SS + m, "x3", m)
            act.dma_start(row[:], rows_d[2:3, :].partition_broadcast(P).rearrange("p a d -> p (a d)")).then_inc(sem("final_g_in"), 16)
            normed_out("n3", 1, 0, hT_low)
            split_high(FIRST_UP + 3)

            def hid_high_out(j):
                wait("hid_out", j + 1)
                if j >= 20:
                    wait("up_done", 2 * KF)
                copy(part(hid_high(j)), hid[:, j, :]).then_inc(sem("hid_high"), 1)

            wait("borders_ready", 1)
            for j in range(KF + 1):
                if j < KF:
                    wait("up_done", 2 * j + 1)
                    if j >= 2:
                        wait("conv_done", j - 1)
                    copy(image[j % 2][:, 1:ROWS + 1, 1:COLS + 1],
                         bank[2 * j % 8].rearrange("p (r c) -> p r c", c=COLS)).then_inc(sem("image_out"), 1)
                    split_high(FIRST_UP + 2 * j + 4)
                if j >= 2:
                    hid_high_out(j - 2)
                if j:
                    wait("conv_done", j)
                    nc.scalar.activation(conv[(j - 1) % 2], conv[(j - 1) % 2], ACT.Silu).then_inc(sem("silu_out"), 1)
                if j < KF:
                    split_high(FIRST_UP + 2 * j + 5)
            hid_high_out(KF - 1)
            for p in range(FIRST_DOWN + 4, len(pieces)):
                split_high(p)
            for m in range(TT):
                wait("down_out", 4 + m + 1)
                square(x_sb[:, m, :], SS_L + m, "x4", m)

        @block.gpsimd
        def _(pool):
            steps = [0]

            def wait(name, count):
                pool.wait_ge(sem(name), count)

            def link(ins):
                steps[0] += 1
                ins.then_inc(sem("pool_step"), 1)
                pool.wait_ge(sem("pool_step"), steps[0])

            def rsqrt(dst, src, n, width, name):
                link(nc.gpsimd.tensor_scalar(st(dst, n), st(src, n), 1.0 / width, NORM_EPS, ALU.mult, ALU.add))
                nc.gpsimd.tensor_tensor(st(dst, n), st(dst, n), st(MHALF, n), ALU.pow).then_inc(sem(name), 1)

            link(nc.gpsimd.memset(st(MHALF, 4), -0.5))
            nc.gpsimd.memset(st(ONE), 1.0).then_inc(sem("one_ready"), 1)
            nc.gpsimd.memset(mod_g[:], 0.0).then_inc(sem("mod_g_clear"), 1)
            wait("squares_done", squares_at("n1", 3))
            rsqrt(RS, SS, TT, D, "roots")
            wait("mod_g_clear", 1)
            pool.dma_start(mod_g[0:1, :, :].rearrange("p a b -> p (a b)"), mod_b_d).then_inc(sem("mod_b_in"), 16)
            C = MOD_POOL_COLS

            def load_pool(j):
                pool.dma_start(modw_pool[j % 2], mod_d[:, j * 1024:(j + 1) * 1024].rearrange("p (k c) -> p k c", k=KD)).then_inc(sem(f"modw_pool_in{j % 2}"), 16)

            def load_dve(j):
                if j:
                    wait("mod_dve_done", j)
                a = MOD_POOL * 1024 + j * 2048
                pool.dma_start(modw_dve, mod_d[:, a:a + 2048].rearrange("p (k c) -> p k c", k=KD)).then_inc(sem("modw_dve_in"), 16)

            def latent_roots():
                wait("squares_done", squares_at("lat", 7))
                rsqrt(RS_L, SS_L, 4, Q_RANK, "roots")
                rsqrt(RS_L + 4, SS_L + 4, 4, KV_RANK, "roots")

            def head_roots(h):
                wait("o_ss", h + 1)
                rsqrt(RS_H + 4 * (h % 2), SS_H + 4 * (h % 2), 4, P, "roots")

            load_pool(0)
            load_dve(0)
            load_pool(1)
            wait("cond_ready", 1)
            cb = st(CSILU, KD).unsqueeze(2).broadcast_to([P, KD, C])
            for j in range(MOD_POOL):
                w = modw_pool[j % 2]
                wait(f"modw_pool_in{j % 2}", 16 * (j // 2 + 1))
                link(nc.gpsimd.tensor_tensor(w, w, cb, ALU.mult))
                for n in (4, 2):
                    link(nc.gpsimd.tensor_tensor(w[:, 0:n, :], w[:, 0:n, :], w[:, n:2 * n, :], ALU.add))
                if j % 2 == 0 and j:
                    wait("mod_spilled", 16 * j // 2)
                nc.gpsimd.tensor_tensor(mod_part[:, j % 2 * C:(j % 2 + 1) * C], w[:, 0, :], w[:, 1, :],
                                        ALU.add).then_inc(sem("mod_pool_done"), 1)
                wait("mod_pool_done", j + 1)
                if j % 2:
                    pool.dma_start(mod_spill_d[:, (j - 1) * C:(j + 1) * C], mod_part[:]).then_inc(sem("mod_spilled"), 16)
                if j + 2 < MOD_POOL:
                    load_pool(j + 2)
                if j == ROOTS_AFTER[0]:
                    latent_roots()
                for h in range(HEADS):
                    if j == ROOTS_AFTER[1 + h]:
                        head_roots(h)
                if j in LOADS_AFTER:
                    load_dve(LOADS_AFTER.index(j) + 1)
            wait("o_turned", UNITS)
            nc.gpsimd.memset(ones_sq, 1.0).then_inc(sem("ones_ready"), 1)
            for m in range(TT + 1):
                if m < TT:
                    for i in (2 * m, 2 * m + 1):
                        n, t = i // 4, i % 4
                        wait("taps_scaled", i + 1)
                        h0, h1 = filt[2 * (i % 2)], filt[2 * (i % 2) + 1]
                        nc.gpsimd.tensor_tensor(taps(0, n)[:, t, :], h0, h1, ALU.add).then_inc(sem("taps_step"), 1)
                        nc.gpsimd.tensor_tensor(taps(1, n)[:, t, :], h0, h1, ALU.subtract).then_inc(sem("taps_ready"), 1)
                    wait("squares_done", squares_at("x1", m))
                    rsqrt(RS + m, SS + m, 1, D, "x_rs")
                if m:
                    wait("squares_done", squares_at("x2", m - 1))
                    rsqrt(RS2 + m - 1, SS2 + m - 1, 1, D, "x2_rs")
            def subtract(low, high):
                return nc.gpsimd.tensor_tensor(part(low), low, part(high), ALU.subtract)

            def split_low(p):
                wait("piece_high", p + 1)
                subtract(*piece_parts(p)).then_inc(sem("piece_low"), 1)

            def hid_low_out(j):
                wait("hid_high", j + 1)
                subtract(hid[:, j, :], hid_high(j)).then_inc(sem("hid_low"), 1)

            for p in range(FIRST_HYZ, FIRST_HYX + PIECES + 2):
                split_low(p)
            for i in range(4):
                n, f = i // 2, i % 2
                kr, ks = km[:, f, n * 512:n * 512 + 512], km[:, 2 + f, n * 512:n * 512 + 512]
                wait("dft_read", i + 1)
                if i:
                    wait("uv_ready", i)
                link(nc.gpsimd.tensor_tensor(tmp[5], tmp[2], kr, ALU.mult))
                link(nc.gpsimd.tensor_tensor(tmp[6], tmp[3], ks, ALU.mult))
                link(nc.gpsimd.tensor_tensor(tmp[5], tmp[5], tmp[6], ALU.subtract))
                link(nc.gpsimd.tensor_tensor(tmp[6], tmp[2], ks, ALU.mult))
                link(nc.gpsimd.tensor_tensor(tmp[2], tmp[3], kr, ALU.mult))
                nc.gpsimd.tensor_tensor(tmp[6], tmp[6], tmp[2], ALU.add).then_inc(sem("w_ready"), 1)
                if i < 3:
                    split_low(FIRST_HYX + PIECES + 2 * i + 2)
                    split_low(FIRST_HYX + PIECES + 2 * i + 3)
            for k in range(KD):
                wait("y_high", k + 1)
                subtract(x0c[:, k, :], hT[:, k, :]).then_inc(sem("y_low"), 1)
            for p in range(FIRST_HYO + PIECES, FIRST_UP + 3):
                split_low(p)
            for m in range(TT):
                wait("squares_done", squares_at("x3", m))
                rsqrt(RS + m, SS + m, 1, D, "x_rs")

            split_low(FIRST_UP + 3)
            for j in range(KF):
                split_low(FIRST_UP + 2 * j + 4)
                if j >= 2:
                    hid_low_out(j - 2)
                split_low(FIRST_UP + 2 * j + 5)
            hid_low_out(KF - 2)
            hid_low_out(KF - 1)
            for p in range(FIRST_DOWN + 4, len(pieces)):
                split_low(p)
            for m in range(TT):
                wait("squares_done", squares_at("x4", m))
                rsqrt(RS_L + m, SS_L + m, 1, D, "x_rs")

        @block.vector
        def _(dve):
            steps = [0]
            V = nc.vector

            def wait(name, count):
                dve.wait_ge(sem(name), count)

            def link(ins):
                steps[0] += 1
                ins.then_inc(sem("dve_step"), 1)
                dve.wait_ge(sem("dve_step"), steps[0])

            def split_low(p):
                wait("piece_high", p + 1)
                low, high = piece_parts(p)
                V.tensor_tensor(part(low), low, part(high), ALU.subtract).then_inc(sem("piece_low"), 1)

            def wrap(r, a, k, quarter):
                link(V.tensor_scalar(k, a, 1.0 / TWO_PI, 0.25 * quarter, ALU.mult, ALU.add))
                link(V.tensor_scalar(k, k, ROUNDER, None, ALU.add))
                link(V.tensor_scalar(k, k, ROUNDER, None, ALU.subtract))
                link(V.scalar_tensor_tensor(out=r, in0=k, scalar=-PI_1, in1=a, op0=ALU.mult, op1=ALU.add))
                link(V.scalar_tensor_tensor(out=r, in0=k, scalar=-PI_2, in1=r, op0=ALU.mult, op1=ALU.add))
                link(V.scalar_tensor_tensor(out=r, in0=k, scalar=-PI_3, in1=r, op0=ALU.mult, op1=ALU.add))
                if quarter:
                    link(V.tensor_scalar(r, r, math.pi / 2, None, ALU.add))
                return V.tensor_scalar(r, r, PI_BELOW, -PI_BELOW, ALU.min, ALU.max)

            wait("roots", 1)
            for m in range(TT):
                V.tensor_scalar(x_sb[:, m, :], x_sb[:, m, :], st(RS + m), None, ALU.mult).then_inc(sem("n1_scaled"), 1)

            for k in range(KD):
                wait("n1_out", k + 1)
                V.tensor_copy(part(hT[:, k, :]), n1_temp[:, k, :]).then_inc(sem("input_split"), 1)
            for k in range(KD):
                wait("input_split", k + 1)
                wait("n1_turned", KD)
                V.tensor_tensor(part(x_low[:, k, :]), n1_temp[:, k, :], part(hT[:, k, :]), ALU.subtract).then_inc(sem("input_split"), 1)
                if k % 2:
                    split_low(k // 2)
            wait("input_split", 2 * KD)

            wait("rowed_in", 16)
            wait("pos_in", 16)
            ang = nsin_t
            posf = sums[:, 0:TT]
            link(V.tensor_copy(posf, pos_sb[:]))
            for m in range(TT):
                ins = V.tensor_scalar(ang[:, m * HALF:(m + 1) * HALF], rowed[:, ROWED["inv_freq"]], posf[:, m:m + 1], None, ALU.mult)
            link(ins)
            for i, t in enumerate((sin_t, cos_t)):
                wrap(t, ang, rope_tmp[:, 0:128], i).then_inc(sem("angle_ready"), 1)
            wait("rope_table", 1)
            wait("angle_ready", 2)
            link(V.tensor_scalar(nsin_t, sin_t, -1.0, None, ALU.mult))
            lam = rowed[:, ROWED["lam"]].rearrange("p (a b c) -> p a b c", a=2, b=2)
            prod = rope_tmp[:, 0:128].rearrange("p (a c) -> p a c", a=2)
            link(V.tensor_tensor(prod, lam[:, :, 0, :], lam[:, :, 1, :], ALU.mult))
            V.tensor_reduce(sums[:, 62:64], prod, AX.X, ALU.add).then_inc(sem("lambda_sums"), 1)

            def net_layer(i):
                wait("net_done", i + 1)
                if i:
                    wait("net_out", i)
                fb = early[0:FW, EARLY["f_b"]][:, i:i + 1]
                a, k, r = net[2][0:FW, :], net[3][0:FW, :], net[1][0:FW, :]
                V.tensor_scalar(a, bank[(0, 3, 7)[i]][0:FW, :], fb, early[0:FW, EARLY["freq"]], ALU.add, ALU.mult).then_inc(sem("net_read"), 1)
                wait("net_read", i + 1)
                wrap(r, a, k, 0).then_inc(sem("net_angle"), 1)

            def mod_chunk(j):
                C = MOD_DVE_COLS
                wait("modw_dve_in", 16 * (j + 1))
                acc = mod_g[:].rearrange("p a b -> p (a b)")[:, j * C:(j + 1) * C]
                w = modw_dve
                for k in range(KD):
                    ins = V.scalar_tensor_tensor(out=acc, in0=w[:, k, :], scalar=st(CSILU + k), in1=acc, op0=ALU.mult, op1=ALU.add)
                    if k < KD - 1:
                        link(ins)
                ins.then_inc(sem("mod_dve_done"), 1)

            def table(t, m, groups, halves):
                v = t[:, m * HALF:(m + 1) * HALF]
                return v.unsqueeze(1).broadcast_to([P, groups * halves, HALF])

            def rope_tile(out, src, m, groups):
                o3 = out.rearrange("p (g c) -> p g c", c=HALF)
                s3 = src.rearrange("p (g c) -> p g c", c=HALF)
                t3 = rope_tmp[:, 0:groups * 64].rearrange("p (g two c) -> p two g c", two=2, c=HALF)
                s4 = src.rearrange("p (g two c) -> p two g c", two=2, c=HALF)
                link(V.tensor_tensor(o3, s3, table(cos_t, m, groups, 2), ALU.mult))
                link(V.tensor_tensor(t3[:, 0], s4[:, 1], table(nsin_t, m, groups, 1), ALU.mult))
                link(V.tensor_tensor(t3[:, 1], s4[:, 0], table(sin_t, m, groups, 1), ALU.mult))
                return V.tensor_tensor(out, out, rope_tmp[:, 0:groups * 64], ALU.add)

            net_layer(0)
            wait("rope_table", 2)
            for p in range(4, 8):
                split_low(p)
            wait("mod_b_in", 16)
            wait("cond_ready", 1)
            mod_chunk(0)
            for i in range(8):
                wait("in_done", in_done_at(i))
                rope_tile(roped[i // 4][:, i % 4, :], in_bank(i), i % 4, 8).then_inc(sem("rope_out"), 1)
                split_low(8 + i)
                if i % 4 == 3:
                    mod_chunk(1 + i // 4)
            for i in range(2):
                net_layer(i + 1)
                for p in range(16 + 4 * i, 20 + 4 * i):
                    split_low(p)
                if i == 0:
                    mod_chunk(3)
            wait("lambda_exps", 1)
            link(V.tensor_scalar(st(NLAM), sums[:, 61:62], sums[:, 60:61], LAMBDA_INIT, ALU.subtract, ALU.subtract))
            wait("in_out", 12)
            wait("qk_turned", 8)
            for m in range(TT):
                link(rope_tile(kr2[:, m, 0:64], lat[:, m, 640:704], m, 1))
                ins = V.tensor_copy(kr2[:, m, 64:128], kr2[:, m, 0:64])
            ins.then_inc(sem("kr_ready"), 1)
            wait("roots", 3)
            for s, (a, n) in enumerate(((0, Q_RANK), (Q_RANK, KV_RANK))):
                for m in range(TT):
                    ins = V.tensor_scalar(lat[:, m, a:a + n], lat[:, m, a:a + n], st(RS_L + 4 * s + m), None, ALU.mult)
                ins.then_inc(sem("lat_scaled"), 1)
            for m in range(TT):
                wait("latq_done", m + 1)
                rope_tile(qr[:, m, :], bank[4 + m][:, 0:256], m, 4).then_inc(sem("qr_out"), 1)
            wait("dgate_out", TT)
            sub = rowed[:, ROWED["subln"]].unsqueeze(1).broadcast_to([P, HEADS, P])
            for m in range(TT):
                g = dgate[:, m, :].rearrange("p (h c) -> p h c", h=HEADS)
                V.scalar_tensor_tensor(out=g, in0=g, scalar=1.0 - LAMBDA_INIT, in1=sub, op0=ALU.mult,
                                       op1=ALU.mult).then_inc(sem("dgate_ready"), 1)
            for p in range(FIRST_MGATE, FIRST_GATE):
                split_low(p)
            mod_chunk(4)

            def maxima(u):
                latent = u >= HEADS
                base, maps = 32 * (u % 2), 1 if latent else 2
                wait("scores_done", scores_at(u))
                for a in range(maps):
                    for i in range(TT):
                        b, c = score_place(a, i)
                        o = base + 16 + 4 * a + i
                        ins = V.tensor_reduce(sums[:, o:o + 1], bank[b][:, c:c + (i + 1) * P], AX.X, ALU.max)
                link(ins)
                V.tensor_scalar(sums[:, base:base + 4 * maps], sums[:, base + 16:base + 16 + 4 * maps],
                                -(MLA_SCALE if latent else DIFF_SCALE), None, ALU.mult).then_inc(sem("neg_max"), 1)

            def combine(u):
                base = 32 * (u % 2)
                wait("exp_out", exps_before(u + 1))
                r1, ratio = sums[:, base + 24:base + 28], sums[:, base + 28:base + 32]
                if u >= HEADS:
                    for i in range(TT):
                        V.reciprocal(r1[:, i:i + 1], sums[:, base + 8 + i:base + 9 + i]).then_inc(sem("probs_ready"), 1)
                    return
                link(V.reciprocal(ratio, sums[:, base + 12:base + 16]))
                link(V.reciprocal(r1, sums[:, base + 8:base + 12]))
                link(V.tensor_tensor(ratio, ratio, sums[:, base + 8:base + 12], ALU.mult))
                link(V.tensor_scalar(ratio, ratio, st(NLAM), None, ALU.mult))
                for i in range(TT):
                    s = slice(OFF[i], OFF[i] + (i + 1) * P)
                    V.scalar_tensor_tensor(out=probs1[u % 2][:, s], in0=probs2[:, s], scalar=ratio[:, i:i + 1],
                                           in1=probs1[u % 2][:, s], op0=ALU.mult, op1=ALU.add).then_inc(sem("probs_ready"), 1)

            def output(u):
                base = 32 * (u % 2)
                o = o_tok[u % 2]
                wait("pv_done", 4 * u + 4)
                if u >= 2:
                    wait("o_turned", u - 1)
                r1 = sums[:, base + 24:base + 28].unsqueeze(2).broadcast_to([P, TT, P])
                V.tensor_tensor(o, bank[7].rearrange("p (a b) -> p a b", a=TT), r1, ALU.mult).then_inc(sem("o_read"), 1)
                wait("o_read", u + 1)
                if u < HEADS:
                    link(V.tensor_tensor(o_sq, o, o, ALU.mult))
                    c = SS_H + 4 * (u % 2)
                    V.tensor_reduce(st(c, 4), o_sq, AX.X, ALU.add).then_inc(sem("o_ss"), 1)

            def gate_output(u):
                h, o = u % HEADS, o_tok[u % 2]
                if u < HEADS:
                    wait("roots", 3 + u + 1)
                    r = st(RS_H + 4 * (u % 2), 4).unsqueeze(2).broadcast_to([P, TT, P])
                    link(V.tensor_tensor(o, o, r, ALU.mult))
                    g = dgate
                else:
                    wait("mgate_ready", 1)
                    g = mgate
                V.tensor_tensor(o, o, g[:, :, h * P:(h + 1) * P], ALU.mult).then_inc(sem("o_ready"), 1)

            maxima(0)
            combine(0)
            mod_chunk(5)
            for u in range(UNITS):
                if u + 1 < UNITS:
                    maxima(u + 1)
                output(u)
                if u + 1 < UNITS:
                    combine(u + 1)
                gate_output(u)
                if u >= 2:
                    split_low(FIRST_GATE + u - 2)
                else:
                    mod_chunk(6 + u)
            for p in range(FIRST_GATE + 6, FIRST_GATE + 16):
                split_low(p)

            wait("gate_out", 12)
            wait("sgd_ready", 1)
            for d in range(KD):
                wait("merge_done", 2 * d + 2)
                link(V.tensor_tensor(sgd[:, d, :], sgd[:, d, :], bank[2 * d % 8], ALU.mult))
                link(V.tensor_tensor(sgm[:, d, :], sgm[:, d, :], bank[(2 * d + 1) % 8], ALU.mult))
                V.tensor_tensor(sgd[:, d, :], sgd[:, d, :], sgm[:, d, :], ALU.add).then_inc(sem("merge_out"), 1)

            wait("modc_done", 1)
            V.tensor_tensor(modc[:], bank[4][:, 0:4 * KD], small[:, SMALL["mod_b"]], ALU.add).then_inc(sem("modc_read"), 1)
            wait("modc_read", 1)
            for s, name in enumerate(("norm_g1", "norm_g2")):
                c = modc[:, (2 * s + 1) * KD:(2 * s + 2) * KD]
                ins = V.scalar_tensor_tensor(out=c, in0=c, scalar=1.0, in1=small[:, SMALL[name]], op0=ALU.add, op1=ALU.mult)
            ins.then_inc(sem("modc_ready"), 1)

            def add_abs(i):
                a = abs_sum[i // 4]
                wait("abs_ready", 2 * i + 2)
                link(V.tensor_tensor(a, a, abs_tap[0], ALU.add))
                V.tensor_tensor(a, a, abs_tap[1], ALU.add).then_inc(sem("abs_step"), 1)
                wait("abs_step", i + 1)

            wait("norm_row_in", 16)
            link(V.memset(abs_sum[0], 0.0))
            link(V.memset(abs_sum[1], 0.0))
            for m in range(TT + 2):
                if m < TT:
                    wait(f"x_in{m}", 32)
                    for i in (2 * m, 2 * m + 1):
                        s = slice((i % 2) * 512, (i % 2) * 512 + 512)
                        wait("wo_done", i + 1)
                        V.tensor_tensor(x_sb[:, m, s], x_sb[:, m, s], bank[i % 3], ALU.add).then_inc(sem("wo_out"), 1)
                        n, t = i // 4, i % 4
                        wait("taps_done", i + 1)
                        wait("decay_ready", i + 1)
                        if i >= 2:
                            wait("taps_ready", i - 1)
                        h0, h1 = filt[2 * (i % 2)], filt[2 * (i % 2) + 1]
                        b = 4 + 2 * (i % 2)
                        V.tensor_tensor(h0, bank[b], decay[i % 2], ALU.mult)
                        ins = V.tensor_tensor(h1, bank[b + 1], decay[i % 2], ALU.mult)
                        if t == 0:
                            link(ins)
                            ins = V.memset(h1[0:1, :], 0.0)
                        ins.then_inc(sem("taps_scaled"), 1)
                        if i:
                            add_abs(i - 1)
                elif m == TT:
                    add_abs(7)
                if 1 <= m <= TT:
                    wait("x_rs", m)
                    V.scalar_tensor_tensor(out=x_sb[:, m - 1, :], in0=x_sb[:, m - 1, :], scalar=st(RS + m - 1), in1=norm_row,
                                           op0=ALU.mult, op1=ALU.mult).then_inc(sem("x2_ready"), 1)
                if m >= 2:
                    wait("x2_rs", m - 1)
                    wait("x2_ready", m - 1)
                    V.tensor_scalar(x_norm[:, m - 2, :], x_sb[:, m - 2, :], st(RS2 + m - 2), None, ALU.mult).then_inc(sem("n2_scaled"), 1)
            wait("bias_in", 16)
            for n in range(2):
                s = slice(n * 512, n * 512 + 512)
                wait("norm_done", n + 1)
                V.tensor_copy(norm_sb[:, s], bank[3][0:1, :]).then_inc(sem("norm_read"), 1)
                wait("norm_read", n + 1)
                link(V.tensor_tensor(bias_row[:, s], bias_row[:, s], norm_sb[:, s], ALU.mult))
                wait("taps_ready", 4 * n + 4)
                tap0 = taps(0, n)[0:1, 0, :]
                V.tensor_tensor(tap0, tap0, bias_row[:, s], ALU.add).then_inc(sem("bias_in_taps"), 1)
            wait("rnorm_done", 1)
            V.reciprocal(st(RNORM, KD), bank[3][:, 0:KD]).then_inc(sem("rnorm_read"), 1)
            wait("rnorm_read", 1)
            link(V.tensor_scalar(st(RNORM, KD), st(RNORM, KD), 2.0 / (2 * SEQ), None, ALU.mult))

            for i in range(4):
                n, f = i // 2, i % 2
                b0 = 4 * (i % 2)
                s = slice(n * 512, n * 512 + 512)
                wait("kdft_copied", 2 * i + 2)
                o_cos, o_sin = filt[2 * (i % 2)], filt[2 * (i % 2) + 1]
                V.tensor_tensor(kp[:, f, s], bank[b0], o_cos, ALU.add)
                V.tensor_tensor(km[:, f, s], bank[b0], o_cos, ALU.subtract)
                V.tensor_tensor(kp[:, 2 + f, s], bank[b0 + 2], o_sin, ALU.add)
                V.tensor_tensor(km[:, 2 + f, s], bank[b0 + 2], o_sin, ALU.subtract).then_inc(sem("kdft_read"), 1)

            def split_input(tag, x):
                for k in range(KD):
                    wait(f"{tag}_out", k + 1)
                    V.tensor_copy(part(hT[:, k, :]), x[:, k, :]).then_inc(sem("input_split"), 1)
                    wait("input_split", split_at[tag] + 2 * k + 1)
                    V.tensor_tensor(part(x[:, k, :]), x[:, k, :], part(hT[:, k, :]), ALU.subtract).then_inc(sem("input_split"), 1)

            split_input("n2", x_low)

            wait("taps_done", 8)
            wait("squares_done", squares_at("x2", 3))
            for p in padded:
                V.memset(p[:, 0:1], 0.0)
                ins = V.memset(p[:, SEQ + 1:SEQ + 2], 0.0)
            ins.then_inc(sem("pads_ready"), 1)

            def short_conv(out, p, tile):
                w = lambda t: sm("hy_sc_w", 24 * t + tile)
                link(V.tensor_scalar(out, p[:, 0:SEQ], w(0), sm("hy_sc_b", tile), ALU.mult, ALU.add))
                link(V.scalar_tensor_tensor(out=out, in0=p[:, 1:SEQ + 1], scalar=w(1), in1=out, op0=ALU.mult, op1=ALU.add))
                return V.scalar_tensor_tensor(out=out, in0=p[:, 2:SEQ + 2], scalar=w(2), in1=out, op0=ALU.mult, op1=ALU.add)

            wait("pads_ready", 1)
            for i in range(16):
                c = i // 2
                wait("hyz_out", i + 1)
                if i % 2 == 0 and c:
                    wait("z_ready", c)
                short_conv((x1c, vc)[i % 2], padded[i % 2], (8, 16)[i % 2] + c).then_inc(sem("hyz_conv"), 1)
                if i % 2:
                    wait("hyz_conv", i + 1)
                    if c >= 2:
                        wait("z_turned", c - 1)
                    V.tensor_tensor(z_buf[c % 2], x1c, vc, ALU.mult).then_inc(sem("z_ready"), 1)

            def hyx_conv(i):
                wait("hyx_out", i + 1)
                short_conv(x0c[:, i, :], padded[0], i).then_inc(sem("hyx_conv"), 1)

            def inverse_out(n):
                for q in range(4):
                    i = 4 * n + q
                    wait("y_done", i + 1)
                    x = x0c[:, i, :].rearrange("p (t two) -> p two t", two=2)
                    y = bank[6 + i % 2].rearrange("p (two t) -> p two t", two=2)
                    V.scalar_tensor_tensor(out=x, in0=y, scalar=st(RNORM + i), in1=x, op0=ALU.mult,
                                           op1=ALU.mult).then_inc(sem("y_out"), 1)

            hyx_conv(0)
            hyx_conv(1)
            for i in range(4):
                n, f = i // 2, i % 2
                s = slice(n * 512, n * 512 + 512)
                kr, ks = kp[:, f, s], kp[:, 2 + f, s]
                ur, us, vr, vs = (uv[:, 2 * c + f, :] for c in range(4))
                e_cos, e_sin = bank[0], bank[2]
                sr, ss, dr, ds, yr, wr, ws = tmp
                wait("dft_copied", 2 * i + 2)
                link(V.tensor_tensor(dr, e_cos, sr, ALU.subtract))
                link(V.tensor_tensor(ds, e_sin, ss, ALU.subtract))
                link(V.tensor_tensor(sr, e_cos, sr, ALU.add))
                V.tensor_tensor(ss, e_sin, ss, ALU.add).then_inc(sem("dft_read"), 1)
                wait("dft_read", i + 1)
                if n:
                    wait("y_done", 4)
                V.tensor_tensor(yr, sr, kr, ALU.mult)
                link(V.tensor_tensor(ur, ss, ks, ALU.mult))
                V.tensor_tensor(us, sr, ks, ALU.mult)
                link(V.tensor_tensor(yr, yr, ur, ALU.subtract))
                link(V.tensor_tensor(sr, ss, kr, ALU.mult))
                link(V.tensor_tensor(sr, sr, us, ALU.add))
                wait("w_ready", i + 1)
                V.tensor_tensor(ur, yr, wr, ALU.add)
                V.tensor_tensor(vr, yr, wr, ALU.subtract)
                V.tensor_tensor(us, sr, ws, ALU.add)
                V.tensor_tensor(vs, sr, ws, ALU.subtract).then_inc(sem("uv_ready"), 1)
                if i < 3:
                    hyx_conv(2 * i + 2)
                    hyx_conv(2 * i + 3)
                if i % 2:
                    wait("hyx_conv", min(8, 2 * i + 4))
                    wait("dve_step", steps[0])
                    inverse_out(n)
            wait("b_out_in", 16)
            for i in range(2 * TT + 1):
                if i < 2 * TT:
                    n, m = i // TT, i % TT
                    s = slice(n * 512, n * 512 + 512)
                    t = tmp[i % 2]
                    if n == 0:
                        wait(f"x_in{m}", 48)
                    wait("hyo_done", TT * (4 * n + 3) + m + 1)
                    link(V.tensor_tensor(t, bank[i], row[:, s], ALU.add))
                    link(V.tensor_tensor(t, t, mod_g[:, 0, s], ALU.mult))
                    V.tensor_tensor(x_sb[:, m, s], x_sb[:, m, s], t, ALU.add).then_inc(sem("hyo_out"), 1)
                if i > TT:
                    m = i - TT - 1
                    wait("x_rs", TT + m + 1)
                    wait("hyo_out", i)
                    V.tensor_scalar(x_norm[:, m, :], x_sb[:, m, :], st(RS + m), None, ALU.mult).then_inc(sem("n3_scaled"), 1)

            split_input("n3", hT_low)

            for im in image:
                V.memset(im[:, 0, :], 0.0)
                V.memset(im[:, ROWS + 1, :], 0.0)
                V.memset(im[:, 1:ROWS + 1, 0:1], 0.0)
                ins = V.memset(im[:, 1:ROWS + 1, COLS + 1:COLS + 2], 0.0)
            ins.then_inc(sem("borders_ready"), 1)
            for j in range(KF + 1):
                if j < KF:
                    wait("image_out", j + 1)
                    if j >= 2:
                        wait("hid_out", j - 1)
                    out = conv[j % 2].rearrange("p (r c) -> p r c", c=COLS)
                    for t in range(9):
                        src = image[j % 2][:, t // 3:t // 3 + ROWS, t % 3:t % 3 + COLS]
                        w = sm("conv_w", t * KF + j)
                        if t == 0:
                            ins = V.tensor_scalar(out, src, w, sm("conv_b", j), ALU.mult, ALU.add)
                        else:
                            ins = V.scalar_tensor_tensor(out=out, in0=src, scalar=w, in1=out, op0=ALU.mult, op1=ALU.add)
                        if t < 8:
                            link(ins)
                    ins.then_inc(sem("conv_done"), 1)
                if j:
                    wait("silu_out", j)
                    wait("up_done", 2 * j)
                    V.tensor_tensor(hid[:, j - 1, :], conv[(j - 1) % 2], bank[(2 * j - 1) % 8], ALU.mult).then_inc(sem("hid_out"), 1)
            for n in range(2):
                for m in range(TT):
                    wait("down_done", TT * ((n + 1) * KF // 2 - 1) + m + 1)
                    s = slice(n * 512, n * 512 + 512)
                    t = conv[m % 2]
                    link(V.tensor_tensor(t, bank[4 * n + m], mod_g[:, 1, s], ALU.mult))
                    V.tensor_tensor(x_sb[:, m, s], x_sb[:, m, s], t, ALU.add).then_inc(sem("down_out"), 1)
            wait("final_g_in", 16)
            wait("down_out", 8)
            for m in range(TT):
                wait("x_rs", 2 * TT + m + 1)
                if m >= 2:
                    wait(f"y_stored{m % 2}", 16)
                V.scalar_tensor_tensor(out=out_tok[m % 2], in0=x_sb[:, m, :], scalar=st(RS_L + m), in1=row[:],
                                       op0=ALU.mult, op1=ALU.mult).then_inc(sem("y_ready"), 1)


def _times():
    return np.concatenate([np.arange(0, SEQ, 2), np.arange(1, SEQ, 2)])


def _filter_constants():
    t = np.linspace(0.0, 1.0, SEQ, dtype=np.float32)
    w = (2.0 * math.pi * np.arange(SEQ, dtype=np.float32) / SEQ).astype(np.float32)
    bands = np.linspace(1e-4, BANDS - 1, BANDS, dtype=np.float32)
    angle = (bands[:, None] * w[None, :]).astype(np.float32).astype(np.float64)
    pos = np.concatenate([t[None, :], np.cos(angle), -np.sin(angle)]).astype(np.float32)
    deltas = np.abs(np.linspace(math.log(1e-2) / 1.5, math.log(1e-2) / 0.3, D, dtype=np.float32))
    order = _times()
    return pos[:, order], -t[order].reshape(TT, P).T, deltas[None, :].astype(np.float32)


def _transform_tables():
    t = _times().astype(np.int64)
    k = np.arange(NF, dtype=np.int64)
    angle = np.pi * ((2 * k[None, :] + 1) * t[:, None] % (4 * SEQ)) / (2 * SEQ)
    tables = []
    for f in (np.cos, np.sin):
        tables.append(f(angle).reshape(4, P, NF).transpose(1, 0, 2).reshape(P, 4 * NF))
    for f in (np.cos, np.sin):
        by_f = f(angle).T
        tables.append(by_f.reshape(2, P, 2, NF).transpose(1, 2, 0, 3).reshape(P, 4 * NF))
    return np.concatenate(tables, axis=1).astype(np.float32)


def _by_feature(v, n):
    return v.reshape(n, P).T


def kernel(**inputs):
    import concourse.bacc as _bacc
    from concourse.bass_utils import run_bass_kernel_spmd as _run
    import ml_dtypes

    a = {k: np.asarray(v) for k, v in inputs.items()}
    f32 = np.float32
    w_in = a["w_in"][0]
    pos_emb, minus_t, deltas = _filter_constants()

    stream = np.zeros((N_CHUNKS, P, SLOT), f32)

    def put(c, w):
        n, width = w.shape[0] // P, w.shape[1]
        stream[c, :, 0:n * width] = w.reshape(n, P, width).transpose(1, 0, 2).reshape(P, n * width)

    put(C_DQ, w_in[:, 0:512])
    put(C_DK, w_in[:, 512:1024])
    put(C_DV, w_in[:, 1024:1536])
    put(C_DGATE, w_in[:, 1536:2048])
    put(C_LAT0, w_in[:, 2048:2400])
    put(C_LAT1, w_in[:, 2400:2752])
    put(C_MGATE, w_in[:, 2752:3264])
    for i, c in enumerate((C_GD0, C_GD1, C_GM0, C_GM1)):
        put(c, w_in[:, 3264 + 512 * i:3776 + 512 * i])
    uq = a["w_uq"][0].reshape(Q_RANK, HEADS, 192)
    put(C_UQ, np.concatenate([uq[:, :, 0:128].reshape(Q_RANK, 512), uq[:, :, 128:].reshape(Q_RANK, 256)], axis=1))
    ukv = a["w_ukv"][0].reshape(KV_RANK, HEADS, 256)
    put(C_UKV, np.concatenate([ukv[:, :, 0:128].reshape(KV_RANK, 512), ukv[:, :, 128:].reshape(KV_RANK, 512)], axis=1))
    put(C_PD, a["w_proj_diff"][0])
    put(C_PM, a["w_proj_mla"][0])
    for n in range(2):
        put(C_WO0 + n, a["w_out"][0][:, 512 * n:512 * n + 512])
        put(C_HYO + n, a["hy_w_out_2"][0][:, 512 * n:512 * n + 512])
    stream[C_FOUT, 0:FW, 0:2 * D] = a["hy_f_wout_2"][0]
    hy = a["hy_w_in_2"][0]
    for c in range(4):
        tiles = [8 + 2 * c, 16 + 2 * c, 9 + 2 * c, 17 + 2 * c]
        put(C_HYZ0 + c, np.concatenate([hy[:, t * P:(t + 1) * P] for t in tiles], axis=1))
    for c in range(2):
        put(C_HYX0 + c, hy[:, 512 * c:512 * c + 512])
    up = a["ffn_w_up_2"][0]
    for c in range(KF // 2):
        cols = []
        for j in (2 * c, 2 * c + 1):
            cols += [up[:, FFN + j * P:FFN + (j + 1) * P], up[:, j * P:(j + 1) * P]]
        put(C_UP + c, np.concatenate(cols, axis=1))
    down = a["ffn_w_down_2"][0]
    for n in range(2):
        k0 = 0
        for q, k in enumerate(DOWN_K):
            put(C_DOWN + 3 * n + q, down[k0 * P:(k0 + k) * P, 512 * n:512 * n + 512])
            k0 += k

    def mod_part(w, width):
        n = w.shape[1] // width
        return w.reshape(KD, P, n, width).transpose(1, 2, 0, 3).reshape(P, n * KD * width)

    by_use = np.concatenate([np.arange(i * D, (i + 1) * D) for i in (0, 1, 3, 4, 2, 5)])
    mod_w = a["mod_w_2"][0][:, by_use]
    mod = np.concatenate([mod_part(mod_w[:, 0:4 * D], MOD_POOL_COLS), mod_part(mod_w[:, 4 * D:], MOD_DVE_COLS)], axis=1)

    small = np.zeros((P, N_SMALL), f32)
    for name, v, n in (("norm_in", a["norm_in"][0], KD), ("norm_g1", a["norm_g_2"][0, 0], KD),
                       ("norm_g2", a["norm_g_2"][0, 1], KD), ("q_norm", a["mla_q_norm"][0], KQ),
                       ("kv_norm", a["mla_kv_norm"][0], KKV), ("hy_b_in", a["hy_b_in_2"][0], 24),
                       ("hy_sc_w", a["hy_sc_w_2"][0].reshape(-1), 72), ("hy_sc_b", a["hy_sc_b_2"][0], 24),
                       ("conv_w", a["ffn_conv_w_2"][0].reshape(-1), 9 * KF), ("conv_b", a["ffn_conv_b_2"][0], KF),
                       ("cond", a["c_2"][0], KD), ("mod_b", a["mod_b_2"][0, by_use[0:4 * D]], 4 * KD)):
        small[:, SMALL[name]] = _by_feature(v, n)
    small[:, SMALL["minus_t"]] = minus_t
    small[:, SMALL["ident"]] = np.eye(P, dtype=f32)
    early = np.zeros((P, N_EARLY), f32)
    early[0:EMB, EARLY["pos_emb"]] = pos_emb
    early[0:EMB, EARLY["f_w1"]] = a["hy_f_w1_2"][0]
    early[0:FW, EARLY["f_w2"]] = a["hy_f_w2_2"][0]
    early[0:FW, EARLY["f_w3"]] = a["hy_f_w3_2"][0]
    for i in range(3):
        early[0:FW, EARLY["f_b"].start + i] = a[f"hy_f_b{i + 1}_2"][0]
    early[0:FW, EARLY["freq"].start] = a["hy_freq_2"][0]
    rowed = np.zeros((P, N_ROWED), f32)
    rowed[:, ROWED["inv_freq"]] = (10000.0 ** (-np.arange(0, 64, 2, dtype=f32) / 64)).astype(f32)[None, :]
    rowed[:, ROWED["lam"]] = np.concatenate([a["diff_lambda_q1"][0], a["diff_lambda_k1"][0],
                                             a["diff_lambda_q2"][0], a["diff_lambda_k2"][0]])[None, :]
    rowed[:, ROWED["subln"]] = a["diff_subln"][0][None, :]
    masks = np.zeros((P, 2, P), f32)
    masks[:, 0, :] = np.eye(P)
    masks[:, 1, :] = np.where(np.arange(P)[None, :] > np.arange(P)[:, None], MASKED, 0.0)
    rows = np.stack([a["norm_final"], a["hy_b_out_2"][0], a["final_g_2"], a["hy_bias_2"][0]])

    arrays = {
        "x_in": a["x"][0], "pos_in": np.ascontiguousarray(a["positions"][0].reshape(TT, P).T.astype(np.int32)),
        "weights_in": stream, "mod_w_in": mod, "mod_b_in": a["mod_b_2"][:, by_use[4 * D:]], "small_in": small, "early_in": early,
        "rowed_in": rowed, "masks_in": masks.reshape(P, 2 * P).astype(ml_dtypes.bfloat16),
        "tables_in": _transform_tables(), "deltas_in": deltas, "rows_in": rows,
    }
    arrays = {k: np.ascontiguousarray(v) for k, v in arrays.items()}
    nc = _bacc.Bacc("TRN2", target_bir_lowering=False, num_devices=1)
    args = [nc.dram_tensor(k, v.shape, mybir.dt.from_np(v.dtype), kind="ExternalInput").ap() for k, v in arrays.items()]
    out = nc.dram_tensor("y_out", (SEQ, D), F32, kind="ExternalOutput").ap()
    spill = nc.dram_tensor("x_spill", (SEQ, D), F32, kind="Internal").ap()
    mod_spill = nc.dram_tensor("mod_spill", (P, 4 * D), F32, kind="Internal").ap()
    build_program(nc, *args, spill, mod_spill, out)
    r = _run(nc, [arrays], core_ids=[0])
    return r.results[0]["y_out"].reshape(1, SEQ, D)
```

```python
from contextlib import ExitStack
import math

import numpy as np
import concourse.bass as bass
from concourse import mybir

F32 = mybir.dt.float32
BF16 = mybir.dt.bfloat16
F32R = mybir.dt.float32r
I32 = mybir.dt.int32
ALU = mybir.AluOpType
ACT = mybir.ActivationFunctionType
AX = mybir.AxisListType

P = 128
SEQ, D = 512, 1024
TT = SEQ // P
KD = D // P
NORM_EPS = 1e-6
HEADS = 4
HALF = 32
UNITS = 2 * HEADS
Q_RANK, KV_RANK = 384, 256
KQ, KKV = Q_RANK // P, KV_RANK // P
DIFF_SCALE = 64 ** -0.5
MLA_SCALE = 192 ** -0.5
LAMBDA_INIT = 0.8 - 0.6 * math.exp(0.0)
FFN = 2816
KF = FFN // P
ROWS, COLS = SEQ // 64, 64
BANDS = 16
EMB = 1 + 2 * BANDS
FW = 64
NF = SEQ // 2
SLOT = 4096
RING = 3
MASKED = -1e30
MOD_POOL_COLS = 128
MOD_POOL = 4 * D // MOD_POOL_COLS
MOD_DVE_COLS = 256
LOADS_AFTER = (1, 6, 9, 11, 13, 15, 17)
ROOTS_AFTER = (12, 19, 21, 24, 26)
MOD_DVE = 2 * D // MOD_DVE_COLS

TWO_PI = 2.0 * math.pi
PI_1 = 6.28125
PI_2 = float(np.float32(np.round((TWO_PI - PI_1) * 2 ** 20) / 2 ** 20))
PI_3 = float(np.float32(TWO_PI - PI_1 - PI_2))
ROUNDER = 1.5 * 2.0 ** 23
PI_BELOW = float(np.nextafter(np.float32(math.pi), np.float32(0)))

SMALL = {}
_at = 0
for _name, _n in (("norm_in", KD), ("norm_g1", KD), ("norm_g2", KD), ("q_norm", KQ), ("kv_norm", KKV),
                  ("hy_b_in", 24), ("hy_sc_w", 72), ("hy_sc_b", 24), ("conv_w", 9 * KF), ("conv_b", KF),
                  ("cond", KD), ("mod_b", 4 * KD), ("minus_t", TT), ("ident", P)):
    SMALL[_name] = slice(_at, _at + _n)
    _at += _n
N_SMALL = _at

EARLY = {}
_at = 0
for _name, _n in (("pos_emb", SEQ), ("f_w1", FW), ("f_w2", FW), ("f_w3", FW), ("f_b", 3), ("freq", 1)):
    EARLY[_name] = slice(_at, _at + _n)
    _at += _n
N_EARLY = _at
ROWED = {}
_at = 0
for _name, _n in (("inv_freq", HALF), ("lam", 4 * 64), ("subln", P)):
    ROWED[_name] = slice(_at, _at + _n)
    _at += _n
N_ROWED = _at

(C_DQ, C_DK, C_DV, C_LAT0, C_LAT1, C_DGATE, C_UQ, C_UKV, C_MGATE, C_GD0, C_GD1, C_GM0, C_GM1,
 C_PD, C_PM, C_WO0, C_WO1, C_FOUT, C_HYZ0) = range(19)
C_HYX0 = C_HYZ0 + 4
C_HYO = C_HYX0 + 2
C_UP = C_HYO + 2
C_DOWN = C_UP + KF // 2
DOWN_K = (8, 8, 6)
N_CHUNKS = C_DOWN + 2 * len(DOWN_K)


BY_TOKENS = (C_DQ, C_DK, C_DV, C_LAT0, C_LAT1, C_DGATE, C_MGATE, C_HYO, C_HYO + 1)
LAT_W = (Q_RANK + KV_RANK + 2 * HALF) // 2
PIECE = SLOT // 4
NET_AFTER = (2, 4, 6)
HYX_AFTER = (1, 2, 1, 2)
PIECES = 4


def slot_of(c):
    return RING - 1 if c == C_FOUT else (c if c < C_FOUT else c - 1) % (RING - 1)


def build_program(nc, x_d, pos_d, stream_d, mod_d, mod_b_d, small_d, early_d, rowed_d, masks_d,
                  tables_d, deltas_d, rows_d, spill_d, mod_spill_d, out_d):
    ctx = ExitStack()
    sems = {}

    def sem(name):
        if name not in sems:
            sems[name] = ctx.enter_context(nc.semaphore(name))
        return sems[name]

    with ctx:
        def sb(name, shape, dt=F32):
            return ctx.enter_context(nc.sbuf_tensor(name, shape, dt))

        twins = {}

        def sb_twice(name, shape, places=None):
            t = sb(name, shape)
            size = math.prod(shape[1:])
            at = nc.sbuf_base - 4 * size
            if places is None:
                twins[name] = [(0, size, nc.alloc_sbuf_tensor_at(name + "_parts", shape, F32R, offset=at))]
            else:
                twins[name] = [(a, b, nc.alloc_sbuf_tensor_at(f"{name}_parts{a}", [P, b - a], F32R, offset=at + 4 * a))
                               for a, b in places]
            return t

        def part(ap):
            n = ap.ap[0][1]
            a, b, twin = next(x for x in twins[ap.tensor.name] if x[0] <= ap.offset < x[1])
            return bass.AP(twin, ap.offset - a, [[b - a, n]] + [list(x) for x in ap.ap[1:]])

        x_sb = sb_twice("x_sb", [P, TT, D])
        hT = sb_twice("hT", [P, KD, SEQ])
        ring = sb_twice("ring", [P, RING, SLOT])
        mod_g = sb("mod_g", [P, 2, D])
        row = sb("row", [P, D])
        small = sb("small", [P, N_SMALL])
        pos_sb = sb("pos_sb", [P, TT], I32)
        masks = sb("masks", [P, 2, P], BF16)
        stat = sb("stat", [P, 96])
        sums = sb("sums", [P, 64])
        mod_part = sb("mod_part", [P, 2 * MOD_POOL_COLS])
        modc = sb("modc", [P, 4 * KD])
        arena = sb_twice("arena", [P, 111 * 256], [(256 * a, 256 * b) for a, b in ((0, 44), (54, 70), (70, 111))])
        bank = [ctx.enter_context(nc.psum_tensor(f"bank{i}", [P, 512], F32))[:, :] for i in range(8)]

        def at(kb, n, tiles=None):
            ap = arena[:, int(kb * 256):int(kb * 256) + n]
            return ap if tiles is None else ap.rearrange("p (a b) -> p a b", a=tiles)

        ident = small[:, SMALL["ident"]]

        def sm(name, i, parts=P):
            c = SMALL[name].start + i
            return small[0:parts, c:c + 1]

        qT = at(0, 2048, HEADS)
        kT = at(8, 2048, HEADS)
        dv = at(16, 2048, TT)
        qn = at(24, 2048, HEADS)
        kn = at(32, 2048, HEADS)
        mv = at(40, 2048, TT)
        qrT = at(48, 1024, 2)
        krT = at(52, 512)
        early = at(54, N_EARLY)
        net = [at(57 + 2 * i, 512) for i in range(4)]
        lat = at(54, TT * 704, TT)
        cqT = at(65, KQ * SEQ, KQ)
        ckvT = at(71, KKV * SEQ, KKV)
        roped = [at(75, 2048, TT), at(83, 2048, TT)]
        kr2 = at(83, TT * P, TT)
        qr = at(85, 1024, TT)
        dgate = at(75, 2048, TT)
        mgate = at(83, 2048, TT)
        modw_dve = at(91, 2048, KD)
        modw_pool = [at(99, 1024, KD), at(103, 1024, KD)]
        n1_temp = at(75, KD * SEQ, KD)
        mod_back = at(75, 4 * D)
        rowed = at(107, N_ROWED)
        cos_t, sin_t, nsin_t = (at(109 + 0.5 * i, 128) for i in range(3))
        probs1 = [at(54, 1280), at(59, 1280)]
        probs2 = at(64, 1280)
        pT = [at(69, 512), at(71, 512)]
        o_sq = at(73, 512, TT)
        o_tok = [at(107, 512, TT), at(109, 512, TT)]
        sgd = at(91, KD * SEQ, KD)
        sgm = at(32, KD * SEQ, KD)
        junk = at(54, D)
        x_norm = at(16, TT * D, TT)
        norm_row = at(48, D)
        filt = [hT[:, i, :] for i in range(4)]
        abs_sum = [hT[:, 4 + n, :] for n in range(2)]
        deltas = hT[:, 6:8, :].rearrange("p a b -> p (a b)")
        bias_row = at(107, D)[0:1, :]
        norm_half = [at(52, 512)[0:1, :], row[0:1, SEQ:D]]
        KDFT_BANK = (0, 4, 4, 0)
        decay = [at(62 + 2 * i, 512) for i in range(2)]
        abs_tap = [at(66 + 2 * i, 512) for i in range(2)]
        ones_sq = at(109, P)
        z_buf = [at(52, 512), at(107, 512)]
        x1c, vc = at(48, 512), at(50, 512)
        h3T = row[0:FW, 0:SEQ]
        rope_tmp = row[:, SEQ:D]
        fwd_cos = at(75, 1024, 4)
        fwd_sin = at(79, 1024, 4)
        inv = at(83, 2048, 8)
        kp = at(58, 4096, 4)
        km = at(91, 4096, 4)
        x0c = at(0, KD * SEQ, KD)
        zT = at(16, 4096, 4)
        uv = at(32, 4096, 8)
        padded = [row[:, 0:SEQ + 2], at(55, SEQ + 2)]
        tmp = [at(48 + 2 * i, 512) for i in range(5)] + [at(107 + 2 * i, 512) for i in range(2)]
        hid = at(0, KF * SEQ, KF)
        image = [at(44 + 3 * i, (ROWS + 2) * (COLS + 2)).rearrange("p (r c) -> p r c", c=COLS + 2) for i in range(2)]
        conv = [at(50 + 2 * i, 512) for i in range(2)]
        x_low = x_sb[:].rearrange("p a (b c) -> p (a b) c", c=SEQ)
        hT_low = at(54, KD * SEQ, KD)
        out_tok = [at(54 + 4 * i, D) for i in range(TT)]
        x4_squares = at(44, D)

        hid_highs = at(70, 20 * SEQ, 20)

        def hid_high(k):
            return at(70 + 2 * k, 512) if k < 20 else hT[:, k - 20, :]

        SS, RS, SS_L, RS_L, SS_H, RS_H, SS2, RS2 = 0, 4, 8, 16, 24, 32, 40, 44
        MHALF, ONE, NLAM, CSILU, RNORM = 64, 68, 69, 70, 78

        def st(c, n=1, parts=P):
            return stat[0:parts, c:c + n]

        def chunk(c):
            return ring[:, slot_of(c), :]

        def chunk_landed(eng, c, more=0):
            i = sum(slot_of(b) == slot_of(c) for b in range(c + 1))
            eng.wait_ge(sem(f"chunk_landed{slot_of(c)}"), 16 * i + more)

        pieces = []
        for n, c in enumerate((C_DQ, C_DK, C_DV, C_LAT0, C_LAT1)):
            pieces += [(c, j, "in_done", TT * (4 * n + j + 1)) for j in range(4)]
        pieces += [(C_DGATE, j, "dgate_done", TT * (j + 1)) for j in range(4)]
        FIRST_MGATE = len(pieces)
        pieces += [(C_MGATE, j, "fill_done", 4) for j in range(4)]
        FIRST_GATE = len(pieces)
        pieces += [(C_GD0, j, "fill_done", j + 5) for j in range(4)]
        pieces += [((C_GD1, C_GM0, C_GM1)[j // 4], j % 4, "gate_done", j + 1) for j in range(12)]
        FIRST_PD = len(pieces)
        pieces += [(C_PD + j // 4, j % 4, "merge_done", 2 * (j + 1)) for j in range(8)]
        FIRST_HYZ = len(pieces)
        pieces += [(C_HYZ0 + j // 4, j % 4, "hyz_done", j + 1) for j in range(16)]
        FIRST_HYX = len(pieces)
        pieces += [(C_HYX0 + j // 4, j % 4, "hyx_done", j + 1) for j in range(KD)]
        FIRST_HYO = len(pieces)
        pieces += [(C_HYO + j // 4, j % 4, "hyo_done", TT * (j + 1)) for j in range(KD)]
        FIRST_UP = len(pieces)
        pieces += [(C_UP + j // 4, j % 4, "up_done", j + 1) for j in range(2 * KF)]
        FIRST_DOWN = len(pieces)
        for n in range(2):
            for q, k in enumerate(DOWN_K):
                pieces += [(C_DOWN + 3 * n + q, j, "down_done", TT * (len(pieces) + j - FIRST_DOWN + 1)) for j in range(k // 2)]

        def tile_done(n_pieces, m, by_tile=0):
            if by_tile:
                return TT * (n_pieces - by_tile) + by_tile * (m + 1)
            return TT * (n_pieces - 1) + m + 1

        for p in range(len(pieces) - 1):
            c, j, name, count = pieces[p]
            last = pieces[p + 1]
            if name == "hyo_done" and j == 2 or name == "down_done" and (c - C_DOWN) % 3 == 2 and j == 1:
                pieces[p] = (c, j, name, last[3])

        def piece_parts(p):
            c, j = pieces[p][0:2]
            high = ring[:, RING - 1, (p % PIECES) * PIECE:(p % PIECES + 1) * PIECE]
            if c in BY_TOKENS or c >= C_DOWN:
                n = 2 * (LAT_W if c in (C_LAT0, C_LAT1) else 512)
                return chunk(c)[:, j * n:(j + 1) * n], high[:, 0:n]
            if c in (C_PD, C_PM):
                return (chunk(c).rearrange("p (k f) -> p k f", k=HEADS)[:, :, j * 2 * P:(j + 1) * 2 * P],
                        high.rearrange("p (k f) -> p k f", k=HEADS))
            return (chunk(c).rearrange("p (k f) -> p k f", k=KD)[:, :, j * P:(j + 1) * P],
                    high.rearrange("p (k f) -> p k f", k=KD))

        def piece_done(p):
            return pieces[p][2:4]

        OFF = [0, 128, 384, 768]

        def score_place(a, i):
            return ((2 + a, 384), (4, 256 * a), (2 + a, 0), (a, 0))[i]

        chunk_used = {C_UQ: ("latq_done", 8), C_UKV: ("latk_done", 8), C_WO0: ("wo_done", 8), C_WO1: ("wo_done", 8),
                      C_FOUT: ("taps_done", 8)}
        for c, _, name, count in pieces:
            chunk_used[c] = (name, count)

        def split_at(tag, k, low):
            if tag == "n2":
                return 2 * KD + 8 * (k // 4) + 4 * low + k % 4 + 1
            return {"n1": 0, "n3": 4 * KD}[tag] + KD * low + k + 1

        def hyx_tiles(i):
            first = 2 + sum(HYX_AFTER[0:i])
            return range(first, first + HYX_AFTER[i])

        def exps_before(u):
            return 8 * min(u, HEADS) + 4 * max(u - HEADS, 0)

        def scores_at(u):
            return 2 * u + 2 if u < HEADS else 2 * HEADS + u - HEADS + 1

        def squares_at(name, i):
            if name == "x1":
                return 12 + max(2 * i, 1)
            if name == "x2":
                return min(15 + 2 * i, 20)
            return {"n1": 1, "lat": 5, "x3": 21, "x4": 25}[name] + i

        def mod_sum(j):
            return mod_back[:, j * P:(j + 1) * P]

        def in_done_at(i):
            return 16 * (i // 4) + tile_done(4, i % 4)

        def in_bank(i):
            return bank[(4, 0)[i // 4 % 2] + i % 4]

        def taps(d, n):
            return at((32, 0)[n] + 8 * d, 2048, 4)

        block = ctx.enter_context(nc.Block())

        @block.sync
        def _(sp):
            for m in range(TT):
                sp.dma_start(x_sb[:, m, :], x_d[m * P:(m + 1) * P, :]).then_inc(sem(f"x_in{m}"), 16)
            def load_chunk(c):
                before = [b for b in range(c) if slot_of(b) == slot_of(c)]
                if c == C_FOUT:
                    sp.wait_ge(sem("merge_done"), 2 * KD)
                elif before:
                    name, count = chunk_used[before[-1]]
                    sp.wait_ge(sem(name), count)
                parts, n = (FW, 2 * D) if c == C_FOUT else (P, SLOT)
                sp.dma_start(chunk(c)[0:parts, 0:n], stream_d[c][0:parts, 0:n]).then_inc(sem(f"chunk_landed{slot_of(c)}"), 16)

            for c in range(C_HYO + 2):
                load_chunk(c)
            for m in range(TT):
                sp.dma_start(x_sb[:, m, :], spill_d[m * P:(m + 1) * P, :]).then_inc(sem(f"x_in{m}"), 16)
            load_chunk(C_UP)
            load_chunk(C_UP + 1)
            with nc.sync.Fori(0, 7, 2) as past:
                for t in range(2):
                    c = C_UP + 2 + t
                    sp.wait_ge(sem("up_done"), 4 * past + 4 * (t + 1))
                    sp.dma_start(chunk(c), stream_d[past + c]).then_inc(sem(f"chunk_landed{slot_of(c)}"), 16)
            for c in range(C_UP + 10, N_CHUNKS):
                load_chunk(c)
            for m in range(TT):
                sp.wait_ge(sem("y_ready"), m + 1)
                sp.dma_start(out_d[m * P:(m + 1) * P, :], out_tok[m]).then_inc(sem("y_stored"), 16)
            sp.wait_ge(sem("y_stored"), 16 * TT)

        @block.tensor
        def _(pe):
            held = {}

            def take(b, name, count):
                if b in held and held[b] != (name, count):
                    pe.wait_ge(sem(held[b][0]), held[b][1])
                held[b] = (name, count)

            def product(out, pairs):
                for n, (l, r) in enumerate(pairs):
                    ins = nc.tensor.matmul(out, l, r, start=n == 0, stop=n == len(pairs) - 1)
                return ins

            def product3(out, lefts, rights, start=True, stop=True, terms=((0, 0), (0, 1), (1, 0))):
                passes = [(part(l[i]), part(r[j])) for i, j in terms
                          for l, r in zip(lefts, rights)]
                for n, (l, r) in enumerate(passes):
                    ins = nc.tensor.matmul(out, l, r, start=start and n == 0, stop=stop and n == len(passes) - 1)
                return ins

            def turn(b, blocks):
                for n, x in enumerate(blocks):
                    ins = nc.tensor.transpose(bank[b][0:x.shape[1], n * P:(n + 1) * P], x, ident)
                return ins

            def first_tiles(p, low_input, b0, name, tag, readers):
                for i in range(PIECES):
                    low, high = piece_parts(p + i)
                    pe.wait_ge(sem("piece_low"), p + i + 1)
                    take(b0 + i, *readers(i))
                    for k in range(KD):
                        if i == 0:
                            pe.wait_ge(sem("input_split"), split_at(tag, k, 0))
                        product3(bank[b0 + i], [(high[:, k, :],)], [(hT[:, k, :],)], start=k == 0, stop=False, terms=((0, 0),))
                for i in range(PIECES):
                    low, high = piece_parts(p + i)
                    for k in range(KD):
                        if i == 0:
                            pe.wait_ge(sem("input_split"), split_at(tag, k, 1))
                        ins = product3(bank[b0 + i], [(high[:, k, :], low[:, k, :])], [(hT[:, k, :], low_input[:, k, :])],
                                       start=False, stop=k == KD - 1, terms=((0, 1), (1, 0)))
                    ins.then_inc(sem(name), 1)

            def split_tile(p, low_input, b, name, out, count):
                pe.wait_ge(sem("piece_low"), p + 1)
                take(b, out, count)
                low, high = piece_parts(p)
                product3(bank[b], [(high[:, k, :], low[:, k, :]) for k in range(KD)],
                         [(hT[:, k, :], low_input[:, k, :]) for k in range(KD)]).then_inc(sem(name), 1)

            def tok(k, m):
                return hT[:, k, m * P:(m + 1) * P]

            def cols(c, k, a, n, width=512):
                return chunk(c)[:, k * width + a:k * width + a + n]

            pe.wait_ge(sem("small_in"), 16)
            pe.wait_ge(sem("n1_scaled"), TT)
            for k in range(KD):
                take(k % 4, "n1_out", k + 1)
                turn(k % 4, [x_sb[:, m, k * P:(k + 1) * P] for m in range(TT)]).then_inc(sem("n1_turned"), 1)
            pe.wait_ge(sem("n1_out"), KD)

            def project_tokens(p, n_pieces, width, b0, name, held_by, inputs, high_part, low_part, by_tile=0):
                def piece_product(q, m):
                    low, high = piece_parts(p + q)
                    tokens = slice(m * P, (m + 1) * P)
                    product3(bank[b0 + m][:, 0:width],
                             [(high_part(2 * q + i)[:, tokens], low_part(2 * q + i)[:, tokens]) for i in range(2)],
                             [(high[:, i * width:(i + 1) * width], low[:, i * width:(i + 1) * width]) for i in range(2)],
                             start=q == 0, stop=q == n_pieces - 1).then_inc(sem(name), 1)

                for q in range(n_pieces - by_tile):
                    pe.wait_ge(sem("piece_low"), p + q + 1)
                    inputs(q)
                    for m in range(TT):
                        if q == 0:
                            take(b0 + m, *held_by(m))
                        piece_product(q, m)
                if by_tile:
                    pe.wait_ge(sem("piece_low"), p + n_pieces)
                    inputs(n_pieces - 1)
                for m in range(TT):
                    for q in range(n_pieces - by_tile, n_pieces):
                        piece_product(q, m)

            def hT_high(k):
                return hT[:, k, :]

            def x_low_k(k):
                return x_low[:, k, :]

            def input_chunk(n, width):
                def held_by(m):
                    i = 4 * n + m
                    return ("rope_out", i + 1) if i < 8 else ("in_out", i - 7)

                def inputs(q):
                    if n == 0:
                        pe.wait_ge(sem("input_split"), split_at("n1", 2 * q + 1, 1))

                project_tokens(4 * n, 4, width, (4, 0)[n % 2], "in_done", held_by, inputs, hT_high, x_low_k)

            input_chunk(0, 512)
            input_chunk(1, 512)
            input_chunk(2, 512)

            def turn_roped(t):
                pe.wait_ge(sem("rope_out"), 4 * t + 4)
                for h in range(HEADS):
                    i = 4 * t + h
                    take(i % 4, "qk_out", i + 1)
                    turn(i % 4, [roped[t][:, m, h * P:(h + 1) * P] for m in range(TT)]).then_inc(sem("qk_turned"), 1)

            turn_roped(0)
            input_chunk(3, LAT_W)
            input_chunk(4, LAT_W)
            turn_roped(1)
            project_tokens(20, 4, 512, 4, "dgate_done", lambda m: ("dgate_out", m + 1), lambda q: None, hT_high, x_low_k)
            pe.wait_ge(sem("kr_ready"), 1)
            take(0, "lat_out", 1)
            turn(0, [kr2[:, m, :] for m in range(TT)]).then_inc(sem("lat_turned"), 1)
            pe.wait_ge(sem("lat_scaled"), 2)
            for i in range(KQ + KKV):
                take((i + 1) % 4, "lat_out", i + 2)
                turn((i + 1) % 4, [lat[:, m, i * P:(i + 1) * P] for m in range(TT)]).then_inc(sem("lat_turned"), 1)
            pe.wait_ge(sem("lat_out"), 1 + KQ)
            chunk_landed(pe, C_UQ)
            for m in range(TT):
                take(4 + m, "qr_out", m + 1)
                product(bank[4 + m][:, 0:256], [(cqT[:, k, m * P:(m + 1) * P], cols(C_UQ, k, 512, 256, 768))
                                                for k in range(KQ)]).then_inc(sem("latq_done"), 1)
            for h in range(HEADS):
                take(4 + h, "qn_out", h + 1)
                product(bank[4 + h], [(cols(C_UQ, k, h * P, P, 768), cqT[:, k, :]) for k in range(KQ)]).then_inc(sem("latq_done"), 1)
            pe.wait_ge(sem("lat_out"), 1 + KQ + KKV)
            chunk_landed(pe, C_UKV)
            for h in range(HEADS):
                take(4 + h, "latk_out", h + 1)
                product(bank[4 + h], [(cols(C_UKV, k, h * P, P, 1024), ckvT[:, k, :]) for k in range(KKV)]).then_inc(sem("latk_done"), 1)
            for m in range(TT):
                take(4 + m, "latk_out", HEADS + m + 1)
                product(bank[4 + m], [(ckvT[:, k, m * P:(m + 1) * P], cols(C_UKV, k, 512, 512, 1024))
                                      for k in range(KKV)]).then_inc(sem("latk_done"), 1)
            pe.wait_ge(sem("qr_out"), TT)
            for b in range(2):
                take(b, "qrT_out", b + 1)
                turn(b, [qr[:, m, b * P:(b + 1) * P] for m in range(TT)]).then_inc(sem("qr_turned"), 1)

            pe.wait_ge(sem("masks_in"), 16)

            def scores(u):
                latent, h = u >= HEADS, u % HEADS
                if u == 0:
                    pe.wait_ge(sem("qk_out"), 8)
                if u == HEADS:
                    pe.wait_ge(sem("latk_out"), 2 * HEADS)
                    pe.wait_ge(sem("qn_out"), HEADS)
                    pe.wait_ge(sem("qrT_out"), 2)
                done = exps_before(u + 1)
                for b in range(5):
                    take(b, "exp_out", done)
                for a in range(1 if latent else 2):
                    for i in (0, 2, 3, 1):
                        if a == 1 and i == 1:
                            pe.wait_ge(sem("scores_done"), 2 * u + 1)
                        b, c = score_place(a, i)
                        n = (i + 1) * P
                        out = bank[b][:, c:c + n]
                        q = slice(i * P, (i + 1) * P)
                        if latent:
                            half = slice(64 * (h % 2), 64 * (h % 2) + 64)
                            nc.tensor.matmul(out, qn[:, h, q], kn[:, h, 0:n], start=True, stop=False)
                            nc.tensor.matmul(out, qrT[half, h // 2, q], krT[half, 0:n], start=False, stop=False)
                        else:
                            half = slice(64 * a, 64 * a + 64)
                            nc.tensor.matmul(out, qT[half, h, q], kT[half, h, 0:n], start=True, stop=False)
                        ins = nc.tensor.matmul(bank[b][:, c + i * P:c + n], masks[:, 0, :], masks[:, 1, :],
                                               start=False, stop=True)
                    ins.then_inc(sem("scores_done"), 1)

            def fill(u):
                b = 5
                take(b, "fill_out", u + 1)
                if u < 4:
                    pe.wait_ge(sem("piece_low"), FIRST_MGATE + 4)
                    tokens = slice(u * P, (u + 1) * P)
                    lefts = [(hT[:, k, tokens], x_low[:, k, tokens]) for k in range(KD)]
                    rights = []
                    for k in range(KD):
                        low, high = piece_parts(FIRST_MGATE + k // 2)
                        c = slice(512 * (k % 2), 512 * (k % 2) + 512)
                        rights.append((high[:, c], low[:, c]))
                    ins = product3(bank[b], lefts, rights)
                else:
                    pe.wait_ge(sem("piece_low"), FIRST_GATE + u - 4 + 1)
                    low, high = piece_parts(FIRST_GATE + u - 4)
                    ins = product3(bank[b], [(high[:, k, :], low[:, k, :]) for k in range(KD)],
                                   [(hT[:, k, :], x_low[:, k, :]) for k in range(KD)])
                ins.then_inc(sem("fill_done"), 1)

            def values(u):
                latent, h = u >= HEADS, u % HEADS
                p1 = probs1[u % 2]

                def turn_probs(i):
                    b = 5 + i % 2
                    pe.wait_ge(sem("probs_ready"), 4 * u + i + 1)
                    take(b, "pT_out", 4 * u + i + 1)
                    turn(b, [p1[:, OFF[i] + j * P:OFF[i] + (j + 1) * P] for j in range(i + 1)]).then_inc(sem("p_turned"), 1)

                def weigh(i):
                    pe.wait_ge(sem("pT_out"), 4 * u + i + 1)
                    v = mv if latent else dv
                    if i == 0:
                        take(7, "o_read", u + 1)
                    product(bank[7][:, i * P:(i + 1) * P],
                            [(pT[i % 2][:, j * P:(j + 1) * P], v[:, j, h * P:(h + 1) * P])
                             for j in range(i + 1)]).then_inc(sem("pv_done"), 1)

                turn_probs(0)
                turn_probs(1)
                weigh(0)
                turn_probs(2)
                weigh(1)
                turn_probs(3)
                weigh(2)
                weigh(3)

            def turn_output(u):
                pe.wait_ge(sem("o_ready"), u + 1)
                take(6, "oT_out", u + 1)
                turn(6, [o_tok[u % 2][:, m, :] for m in range(TT)]).then_inc(sem("o_turned"), 1)

            scores(0)
            fill(0)
            for u in range(UNITS):
                if u + 1 < UNITS:
                    scores(u + 1)
                    fill(u + 1)
                values(u)
                if u:
                    turn_output(u - 1)

            def net_layer(i, b):
                take(b, "net_read", i + 1)
                w = early[0:(EMB, FW, FW)[i], EARLY[f"f_w{i + 1}"]]
                if i:
                    pe.wait_ge(sem("net_out"), i)
                else:
                    pe.wait_ge(sem("early_in"), 16)
                x = early[0:EMB, EARLY["pos_emb"]] if i == 0 else net[0][0:FW, :]
                nc.tensor.matmul(bank[b][0:FW, :], w, x, start=True, stop=True).then_inc(sem("net_done"), 1)

            for i in range(12):
                split_tile(FIRST_GATE + 4 + i, x_low, i % 4, "gate_done", "gate_out", i + 1)
                if i == 1:
                    turn_output(UNITS - 1)
                if i in NET_AFTER:
                    net_layer(NET_AFTER.index(i), 4)

            for i in range(2 * KD):
                o = ((qT, kT), (qn, dv))[i // KD]
                d = i % KD
                if d == 0:
                    pe.wait_ge(sem("oT_low"), (HEADS, UNITS)[i // KD])
                if i % 2 == 0:
                    pe.wait_ge(sem("piece_low"), FIRST_PD + i // 2 + 1)
                low, high = piece_parts(FIRST_PD + i // 2)
                c = slice(i % 2 * P, (i % 2 + 1) * P)
                take(d, "merge_out", i + 1)
                product3(bank[d], [(high[:, k, c], low[:, k, c]) for k in range(HEADS)],
                         [(o[0][:, k, :], o[1][:, k, :]) for k in range(HEADS)]).then_inc(sem("merge_done"), 1)

            pe.wait_ge(sem("mod_back_in"), 16)
            pe.wait_ge(sem("mod_dve_done"), MOD_DVE)
            pe.wait_ge(sem("ones_ready"), 1)
            take(4, "modc_read", 1)
            for j in range(4 * KD):
                ins = nc.tensor.matmul(bank[4][:, j:j + 1], mod_sum(j), st(ONE), start=True, stop=True)
            ins.then_inc(sem("modc_done"), 1)
            for j in range(4):
                b = (5, 6, 7, 4)[j]
                take(b, "modg_out", j + 1)
                nc.tensor.matmul(bank[b], ones_sq, mod_g[:, j // 2, (j % 2) * 512:(j % 2) * 512 + 512],
                                 start=True, stop=True).then_inc(sem("modg_done"), 1)

            def abs_norm(n):
                pe.wait_ge(sem("abs_step"), 4 * n + 4)
                take(3, "norm_read", n + 1)
                nc.tensor.matmul(bank[3][0:1, :], st(ONE), abs_sum[n], start=True, stop=True).then_inc(sem("norm_done"), 1)

            pe.wait_ge(sem("merge_out"), 2 * KD)
            chunk_landed(pe, C_WO0)
            chunk_landed(pe, C_WO1)
            for m in range(TT):
                for n in range(2):
                    i = 2 * m + n
                    take(i % 3, "wo_out", i + 1)
                    product(bank[i % 3], [(sgd[:, k, m * P:(m + 1) * P], cols(C_WO0 + n, k, 0, 512))
                                          for k in range(KD)]).then_inc(sem("wo_done"), 1)
                    if i == 0:
                        chunk_landed(pe, C_FOUT)
                    tn, t = i // 4, i % 4
                    for d in range(2):
                        b = 4 + 2 * (i % 2) + d
                        take(b, "taps_scaled", i + 1)
                        ins = nc.tensor.matmul(bank[b], h3T[:, t * P:(t + 1) * P],
                                               chunk(C_FOUT)[0:FW, d * D + tn * 512:d * D + tn * 512 + 512],
                                               start=True, stop=True)
                    ins.then_inc(sem("taps_done"), 1)
                    if i == 5:
                        abs_norm(0)
            def transform(jobs_done, out_name, i, cos_in, sin_in, f, n0):
                fs = slice(f * P, (f + 1) * P)
                for b in range(4):
                    take(n0 + b, out_name, i + 1)
                    t, x = (fwd_cos, cos_in) if b < 2 else (fwd_sin, sin_in)
                    k0 = 2 * (b % 2)
                    ins = product(bank[n0 + b], [(t[:, k, fs], x(k)) for k in (k0, k0 + 1)])
                    if b % 2:
                        ins.then_inc(sem(jobs_done), 1)

            pe.wait_ge(sem("tables_in"), 16)

            def taps_spectrum(i):
                n, f = i // 2, i % 2
                pe.wait_ge(sem("taps_ready"), 4 * n + 4)
                pe.wait_ge(sem("bias_in_taps"), n + 1)
                transform("kdft_done", "kdft_read", i, lambda k: taps(0, n)[:, k, :],
                          lambda k: taps(1, n)[:, k, :], f, KDFT_BANK[i])

            def turn_normed(tag, src, b0):
                pe.wait_ge(sem(f"{tag}_scaled"), TT)
                for k in range(KD):
                    take(b0 + k % 4, f"{tag}_out", k + 1)
                    turn(b0 + k % 4, [src[:, m, k * P:(k + 1) * P] for m in range(TT)]).then_inc(sem(f"{tag}_turned"), 1)

            taps_spectrum(0)
            taps_spectrum(1)
            abs_norm(1)
            turn_normed("n2", x_norm, 0)
            taps_spectrum(2)
            pe.wait_ge(sem("norm_read"), 2)
            take(3, "rnorm_read", 1)
            for j in range(KD):
                n, c = j // 4, j % 4 * P
                ins = nc.tensor.matmul(bank[3][:, j:j + 1], norm_half[n][:, c:c + P], stat[0:1, ONE:ONE + 1],
                                       start=True, stop=True)
            ins.then_inc(sem("rnorm_done"), 1)
            taps_spectrum(3)


            def turn_z(c):
                pe.wait_ge(sem("z_ready"), c + 1)
                take(c % 4, "zT_out", c + 1)
                z = z_buf[c % 2].rearrange("p (a two) -> p two a", two=2)
                turn(c % 4, [z[:, t // 2, (t % 2) * P:(t % 2) * P + P] for t in range(4)]).then_inc(sem("z_turned"), 1)

            first_tiles(FIRST_HYZ, x_low, 4, "hyz_done", "n2", lambda i: ("hyz_out", i + 1))
            for i in range(PIECES, 16):
                split_tile(FIRST_HYZ + i, x_low, 4 + i % 4, "hyz_done", "hyz_out", i + 1)
                if i >= 4 and i % 2 == 1:
                    turn_z((i - 4) // 2)
            hyx_at = [0]

            def hyx(n):
                for _ in range(n):
                    i = hyx_at[0]
                    split_tile(FIRST_HYX + i, x_low, 4 + i % 2, "hyx_done", "hyx_out", i + 1)
                    hyx_at[0] += 1

            hyx(1)
            turn_z(6)
            hyx(1)
            turn_z(7)
            pe.wait_ge(sem("zT_out"), 8)

            def inverse(n):
                pe.wait_ge(sem("uv_ready"), 2 * n + 2)
                for q in range(4):
                    i = 4 * n + q
                    take(6 + i % 2, "y_out", i + 1)
                    for odd in range(2):
                        parts = [(uv[:, 2 * (2 * odd + s) + f, q * P:(q + 1) * P], inv[:, 4 * s + 2 * odd + f, :])
                                 for s in range(2) for f in range(2)]
                        ins = product(bank[6 + i % 2][:, odd * NF:(odd + 1) * NF], parts)
                    ins.then_inc(sem("y_done"), 1)

            for n in range(2):
                for f in range(2):
                    i = 2 * n + f
                    x = lambda k, n=n: zT[:, k, n * 512:(n + 1) * 512]
                    transform("dft_done", "dft_read", i, x, x, f, 0)
                    hyx(HYX_AFTER[i])
                inverse(n)

            def output_half(n, p, n_pieces, name, out, k_ready, high_part, low_part):
                def inputs(q):
                    if n == 0:
                        pe.wait_ge(sem(k_ready), 2 * q + 2)

                project_tokens(p + n * n_pieces, n_pieces, 512, 4 * n, name, lambda m: (out, 4 * n + m + 1),
                               inputs, high_part, low_part, by_tile=2)

            for n in range(2):
                output_half(n, FIRST_HYO, 4, "hyo_done", "hyo_out", "y_low", hT_high, lambda k: x0c[:, k, :])

            turn_normed("n3", x_norm, 0)
            def up_reader(i):
                return ("image_out" if i % 2 == 0 else "hid_out", i // 2 + 1)

            first_tiles(FIRST_UP, hT_low, 4, "up_done", "n3", up_reader)
            for i in range(PIECES, PIECES + 8):
                split_tile(FIRST_UP + i, hT_low, (i + 4) % 8, "up_done", *up_reader(i))
            first = PIECES + 8
            with nc.tensor.Fori(0, 2 * KF - first, 8) as done:
                for t in range(8):
                    i = first + t
                    pe.wait_ge(sem("piece_low"), done + (FIRST_UP + i + 1))
                    if t % 2 == 0:
                        pe.wait_ge(sem("image_out"), done // 2 + ((i - 8) // 2 + 1))
                    else:
                        pe.wait_ge(sem("hid_out"), done // 2 + ((i - 8) // 2 + 1))
                    low, high = piece_parts(FIRST_UP + i)
                    product3(bank[t], [(high[:, k, :], low[:, k, :]) for k in range(KD)],
                             [(hT[:, k, :], hT_low[:, k, :]) for k in range(KD)]).then_inc(sem("up_done"), 1)
            for t in range(8):
                held[t] = up_reader(2 * KF - 8 + t)
            for n in range(2):
                output_half(n, FIRST_DOWN, KF // 2, "down_done", "down_out", "hid_low", hid_high, lambda k: hid[:, k, :])

        @block.scalar
        def _(act):
            def wait(name, count):
                act.wait_ge(sem(name), count)

            def copy(out, in_):
                return nc.scalar.activation(out, in_, ACT.Copy)

            def split_high(p, past=0):
                chunk_landed(act, pieces[p][0], 4 * past)
                if p == FIRST_HYZ:
                    wait(*chunk_used[C_FOUT])
                elif p >= PIECES and not FIRST_HYZ < p < FIRST_HYZ + PIECES:
                    name, count = piece_done(p - PIECES)
                    wait(name, 2 * past + count)
                low, high = piece_parts(p)
                copy(part(high), low).then_inc(sem("piece_high"), 1)

            squares = [0]

            def square(x, c, name, i, scratch=junk):
                if squares[0]:
                    wait("squares_done", squares[0])
                squares[0] += 1
                assert squares[0] == squares_at(name, i)
                nc.scalar.activation(scratch[:, 0:x.shape[1]], x, ACT.Square, accum_out=st(c)).then_inc(sem("squares_done"), 1)

            act.dma_start(small[:], small_d).then_inc(sem("small_in"), 16)
            act.dma_start(rowed, rowed_d).then_inc(sem("rowed_in"), 16)
            act.dma_start(pos_sb[:], pos_d).then_inc(sem("pos_in"), 16)
            act.dma_start(masks[:], masks_d.rearrange("p (a b) -> p a b", a=2)).then_inc(sem("masks_in"), 16)
            for m in range(TT):
                wait(f"x_in{m}", 16)
                square(x_sb[:, m, :], SS + m, "n1", m)
            wait("small_in", 16)
            nc.scalar.activation(st(CSILU, KD), small[:, SMALL["cond"]], ACT.Silu).then_inc(sem("cond_ready"), 1)
            for k in range(KD):
                wait("n1_turned", k + 1)
                nc.scalar.activation(n1_temp[:, k, :], bank[k % 4], ACT.Identity, scale=sm("norm_in", k)).then_inc(sem("n1_out"), 1)
            for p in range(4):
                split_high(p)
            for i, t in enumerate((sin_t, cos_t)):
                wait("angle_ready", i + 1)
                nc.scalar.activation(t, t, ACT.Sin).then_inc(sem("rope_table"), 1)

            def net_out(i):
                wait("net_angle", i + 1)
                nc.scalar.activation(net[0][0:FW, :] if i < 2 else h3T, net[1][0:FW, :], ACT.Sin).then_inc(sem("net_out"), 1)

            def input_out(i):
                wait("in_done", in_done_at(i))
                m = i % 4
                if i < 12:
                    copy(dv[:, m, :], in_bank(i)).then_inc(sem("in_out"), 1)
                else:
                    c = LAT_W * (i // 4 - 3)
                    copy(lat[:, m, c:c + LAT_W], in_bank(i)[:, 0:LAT_W]).then_inc(sem("in_out"), 1)

            def qk_out(i):
                wait("qk_turned", i + 1)
                copy((qT, kT)[i // 4][:, i % 4, :], bank[i % 4]).then_inc(sem("qk_out"), 1)

            for p in range(4, 16):
                split_high(p)
            for i in range(8, 12):
                input_out(i)
            for i in range(4):
                qk_out(i)
            for p in range(16, 20):
                split_high(p)
            for i in range(12, 16):
                input_out(i)
            for p in range(20, 24):
                split_high(p)
            for i in range(16, 20):
                input_out(i)
            wait("lambda_sums", 1)
            nc.scalar.activation(sums[:, 60:62], sums[:, 62:64], ACT.Exp).then_inc(sem("lambda_exps"), 1)
            wait("in_out", 12)
            for m in range(TT):
                square(lat[:, m, 0:Q_RANK], SS_L + m, "lat", 2 * m, cqT[:, 0, :])
                square(lat[:, m, Q_RANK:Q_RANK + KV_RANK], SS_L + 4 + m, "lat", 2 * m + 1, cqT[:, 0, :])
            for i in range(4, 8):
                qk_out(i)
            for m in range(TT):
                wait("dgate_done", tile_done(4, m))
                nc.scalar.activation(dgate[:, m, :], bank[4 + m], ACT.Silu).then_inc(sem("dgate_out"), 1)
            for i in range(1 + KQ + KKV):
                wait("lat_turned", i + 1)
                b = bank[i % 4]
                if i == 0:
                    ins = copy(krT, b)
                elif i <= KQ:
                    ins = nc.scalar.activation(cqT[:, i - 1, :], b, ACT.Identity, scale=sm("q_norm", i - 1))
                else:
                    ins = nc.scalar.activation(ckvT[:, i - 1 - KQ, :], b, ACT.Identity, scale=sm("kv_norm", i - 1 - KQ))
                ins.then_inc(sem("lat_out"), 1)
            for h in range(HEADS):
                wait("latq_done", TT + h + 1)
                copy(qn[:, h, :], bank[4 + h]).then_inc(sem("qn_out"), 1)
            for i in range(8):
                wait("latk_done", i + 1)
                copy((kn, mv)[i // 4][:, i % 4, :], bank[4 + i % 4]).then_inc(sem("latk_out"), 1)
            for b in range(2):
                wait("qr_turned", b + 1)
                copy(qrT[:, b, :], bank[b]).then_inc(sem("qrT_out"), 1)

            for p in range(FIRST_MGATE, FIRST_GATE):
                split_high(p)

            def exps(u):
                latent = u >= HEADS
                base = 32 * (u % 2)
                for a in range(1 if latent else 2):
                    wait("neg_max", scores_at(u) - (not latent and a == 0))
                    if a == 0 and u >= 2:
                        wait("p_turned", 4 * (u - 1))
                    if a == 1 and u >= 1:
                        wait("probs_ready", 4 * u)
                    for i in range(TT):
                        b, c = score_place(a, i)
                        n = (i + 1) * P
                        p = (probs2 if a else probs1[u % 2])[:, OFF[i]:OFF[i] + n]
                        nc.scalar.activation(p, bank[b][:, c:c + n], ACT.Exp, bias=sums[:, base + 4 * a + i:base + 4 * a + i + 1],
                                             scale=MLA_SCALE if latent else DIFF_SCALE,
                                             accum_out=sums[:, base + 8 + 4 * a + i:base + 9 + 4 * a + i]).then_inc(sem("exp_out"), 1)

            def fill_out(u):
                wait("fill_done", u + 1)
                if u == 4:
                    wait("mod_dve_done", MOD_DVE)
                copy(mgate[:, u, :] if u < 4 else sgd[:, u - 4, :], bank[5]).then_inc(sem("fill_out"), 1)

            def probs_out(u):
                for i in range(TT):
                    n = 4 * u + i
                    wait("p_turned", n + 1)
                    if n >= 2:
                        wait("pv_done", n - 1)
                    copy(pT[i % 2][:, 0:(i + 1) * P], bank[5 + i % 2][:, 0:(i + 1) * P]).then_inc(sem("pT_out"), 1)

            def output_out(u):
                wait("o_turned", u + 1)
                high, whole = (qn, dv) if u >= HEADS else (qT, kT)
                copy(whole[:, u % HEADS, :], bank[6])
                copy(part(high[:, u % HEADS, :]), bank[6]).then_inc(sem("oT_out"), 1)

            exps(0)
            fill_out(0)
            for u in range(UNITS):
                if u + 1 < UNITS:
                    exps(u + 1)
                    fill_out(u + 1)
                probs_out(u)
                if u == 3:
                    wait("fill_out", 4)
                    nc.scalar.activation(mgate, mgate, ACT.Silu).then_inc(sem("mgate_ready"), 1)
                if u:
                    output_out(u - 1)
                if u >= 2:
                    split_high(FIRST_GATE + u - 2)
            act.dma_start(early, early_d).then_inc(sem("early_in"), 16)
            split_high(FIRST_GATE + 6)
            split_high(FIRST_GATE + 7)
            wait("mod_pool_done", MOD_POOL)
            for i in range(12):
                if i - 2 in NET_AFTER:
                    net_out(NET_AFTER.index(i - 2))
                split_high(FIRST_GATE + 8 + i)
                wait("gate_done", i + 1)
                dst = sgd[:, 4 + i, :] if i < 4 else sgm[:, i - 4, :]
                nc.scalar.activation(dst, bank[i % 4], ACT.Sigmoid).then_inc(sem("gate_out"), 1)
                if i == 1:
                    output_out(UNITS - 1)
                if i == 2:
                    nc.scalar.activation(sgd[:, 0:4, :], sgd[:, 0:4, :], ACT.Sigmoid).then_inc(sem("sgd_ready"), 1)
            act.dma_start(norm_row, rows_d[0:1, :].partition_broadcast(P).rearrange("p a d -> p (a d)")).then_inc(sem("norm_row_in"), 16)
            wait("o_ready", UNITS)
            wait("mod_spilled", 16 * MOD_POOL // 2)
            act.dma_start(mod_back, mod_spill_d).then_inc(sem("mod_back_in"), 16)
            act.dma_start(deltas, deltas_d.partition_broadcast(P).rearrange("p a d -> p (a d)")).then_inc(sem("deltas_in"), 16)
            wait("gate_done", 12)
            for m in range(TT):
                act.dma_start(x_sb[:, m, :], x_d[m * P:(m + 1) * P, :]).then_inc(sem(f"x_in{m}"), 16)
            for p in range(FIRST_PD + 4, FIRST_PD + 8):
                split_high(p)
            wait("modc_done", 1)
            act.dma_start(at(75, 4096), tables_d).then_inc(sem("tables_in"), 16)
            for j in range(4):
                wait("modg_done", j + 1)
                copy(mod_g[:, j // 2, (j % 2) * 512:(j % 2) * 512 + 512], bank[(5, 6, 7, 4)[j]]).then_inc(sem("modg_out"), 1)
            act.dma_start(bias_row, rows_d[3:4, :]).then_inc(sem("bias_in"), 16)

            wait("deltas_in", 16)
            for m in range(TT + 1):
                if m < TT:
                    for i in (2 * m, 2 * m + 1):
                        if i >= 2:
                            wait("taps_scaled", i - 1)
                        n, t = i // 4, i % 4
                        nc.scalar.activation(decay[i % 2], deltas[:, n * 512:n * 512 + 512], ACT.Exp,
                                             scale=sm("minus_t", t)).then_inc(sem("decay_ready"), 1)
                    for i in (2 * m, 2 * m + 1):
                        wait("taps_scaled", i + 1)
                        if i:
                            wait("abs_step", i)
                        for d in range(2):
                            nc.scalar.activation(abs_tap[d], filt[2 * (i % 2) + d], ACT.Abs).then_inc(sem("abs_ready"), 1)
                    wait("wo_out", 2 * m + 2)
                    square(x_sb[:, m, :], SS + m, "x1", m)
                if m:
                    wait("x2_ready", m)
                    act.dma_start(spill_d[(m - 1) * P:m * P, :], x_sb[:, m - 1, :]).then_inc(sem("x_spilled"), 16)
                    square(x_sb[:, m - 1, :], SS2 + m - 1, "x2", m - 1)
            wait("taps_ready", 8)
            def kdft_copy(i):
                wait("kdft_done", 2 * i + 1)
                if i == 2:
                    wait("norm_done", 2)
                copy(hT[:, 2 * i, :], bank[KDFT_BANK[i] + 1]).then_inc(sem("kdft_copied"), 1)
                wait("kdft_done", 2 * i + 2)
                copy(hT[:, 2 * i + 1, :], bank[KDFT_BANK[i] + 3]).then_inc(sem("kdft_copied"), 1)

            def normed_out(tag, s, b0, dst):
                for k in range(KD):
                    wait(f"{tag}_turned", k + 1)
                    nc.scalar.activation(dst[:, k, :], bank[b0 + k % 4], ACT.Identity,
                                         scale=modc[:, (2 * s + 1) * KD + k:(2 * s + 1) * KD + k + 1],
                                         bias=modc[:, 2 * s * KD + k:2 * s * KD + k + 1]).then_inc(sem(f"{tag}_out"), 1)

            for p in range(PIECES):
                split_high(FIRST_HYZ + p)
            kdft_copy(0)
            kdft_copy(1)
            wait("modc_ready", 1)
            wait("x_spilled", 16 * TT)
            normed_out("n2", 0, 0, x_low)
            kdft_copy(2)
            kdft_copy(3)

            def hy_out(i, tile, b, place, name, done, conv_name):
                wait(done, i + 1)
                if conv_name:
                    wait(*conv_name)
                nc.scalar.activation(place[:, 1:SEQ + 1], bank[b], ACT.Identity, bias=sm("hy_b_in", tile)).then_inc(sem(name), 1)

            def z_out(c):
                wait("z_turned", c + 1)
                copy(zT[:, :, c * P:(c + 1) * P], bank[c % 4].rearrange("p (a b) -> p a b", a=4)).then_inc(sem("zT_out"), 1)

            wait("pads_ready", 1)
            for i in range(16):
                split_high(FIRST_HYZ + i + PIECES)
                hy_out(i, (8, 16)[i % 2] + i // 2, 4 + i % 4, padded[i % 2], "hyz_out", "hyz_done",
                       ("hyz_conv", i - 1) if i >= 2 else None)
                if i >= 4 and i % 2 == 1:
                    z_out((i - 4) // 2)

            def hyx_out(i):
                hy_out(i, i, 4 + i % 2, padded[0], "hyx_out", "hyx_done",
                       ("hyx_conv", i) if i >= 1 else ("hyz_conv", 16))

            hyx_out(0)
            split_high(FIRST_HYX + PIECES)
            z_out(6)
            hyx_out(1)
            split_high(FIRST_HYX + PIECES + 1)
            z_out(7)
            for i in range(4):
                wait("dft_done", 2 * i + 1)
                if i:
                    wait("uv_ready", i)
                copy(tmp[0], bank[1]).then_inc(sem("dft_copied"), 1)
                wait("dft_done", 2 * i + 2)
                copy(tmp[1], bank[3]).then_inc(sem("dft_copied"), 1)
                for t in hyx_tiles(i):
                    hyx_out(t)
                    split_high(FIRST_HYX + PIECES + t)
            for k in range(KD):
                wait("y_out", k + 1)
                copy(part(hT[:, k, :]), x0c[:, k, :]).then_inc(sem("y_high"), 1)
            wait("hyx_conv", 8)
            act.dma_start(row[:], rows_d[1:2, :].partition_broadcast(P).rearrange("p a d -> p (a d)")).then_inc(sem("b_out_in"), 16)
            for p in range(FIRST_HYO + PIECES, FIRST_UP + 2):
                split_high(p)
            for m in range(TT):
                wait("hyo_out", TT + m + 1)
                square(x_sb[:, m, :], SS + m, "x3", m)
            act.dma_start(row[:], rows_d[2:3, :].partition_broadcast(P).rearrange("p a d -> p (a d)")).then_inc(sem("final_g_in"), 16)
            split_high(FIRST_UP + 2)
            split_high(FIRST_UP + 3)
            normed_out("n3", 1, 0, hT_low)

            def hid_high_out(j):
                wait("hid_out", j + 1)
                if j >= 20:
                    wait("up_done", 2 * KF)
                copy(part(hid_high(j)), hid[:, j, :]).then_inc(sem("hid_high"), 1)

            wait("borders_ready", 1)

            def up_step(j, past=0):
                wait("up_done", 2 * past + (2 * j + 1))
                if j >= 2:
                    wait("conv_done", past + (j - 1))
                copy(image[j % 2][:, 1:ROWS + 1, 1:COLS + 1],
                     bank[(2 * j + 4) % 8].rearrange("p (r c) -> p r c", c=COLS)).then_inc(sem("image_out"), 1)
                split_high(FIRST_UP + 2 * j + 4, past)
                if j >= 2:
                    wait("hid_out", past + (j - 1))
                    copy(part(hid_highs)[:, past + (j - 2), :], hid[:, past + (j - 2), :]).then_inc(sem("hid_high"), 1)
                if j:
                    silu(j, past)
                split_high(FIRST_UP + 2 * j + 5, past)

            def silu(j, past=0):
                wait("conv_done", past + j)
                c = conv[(j - 1) % 2]
                nc.scalar.activation(c, c, ACT.Silu).then_inc(sem("silu_out"), 1)

            up_step(0)
            up_step(1)
            with nc.scalar.Fori(0, 13, 4) as past:
                for t in range(4):
                    up_step(2 + t, past)
            for j in range(18, KF):
                up_step(j)
            hid_high_out(KF - 2)
            silu(KF)
            hid_high_out(KF - 1)
            for p in range(FIRST_DOWN + 4, len(pieces)):
                split_high(p)
            for m in range(TT):
                wait("down_out", 4 + m + 1)
                square(x_sb[:, m, :], SS_L + m, "x4", m, x4_squares)

        @block.gpsimd
        def _(pool):
            steps = [0]

            def wait(name, count):
                pool.wait_ge(sem(name), count)

            def link(ins):
                steps[0] += 1
                ins.then_inc(sem("pool_step"), 1)
                pool.wait_ge(sem("pool_step"), steps[0])

            def rsqrt(dst, src, n, width, name):
                link(nc.gpsimd.tensor_scalar(st(dst, n), st(src, n), 1.0 / width, NORM_EPS, ALU.mult, ALU.add))
                nc.gpsimd.tensor_tensor(st(dst, n), st(dst, n), st(MHALF, n), ALU.pow).then_inc(sem(name), 1)

            link(nc.gpsimd.memset(st(MHALF, 4), -0.5))
            nc.gpsimd.memset(st(ONE), 1.0).then_inc(sem("one_ready"), 1)
            nc.gpsimd.memset(mod_g[:], 0.0).then_inc(sem("mod_g_clear"), 1)
            for m in range(TT):
                wait("squares_done", squares_at("n1", m))
                rsqrt(RS + m, SS + m, 1, D, "roots")
            wait("mod_g_clear", 1)
            pool.dma_start(mod_g[0:1, :, :].rearrange("p a b -> p (a b)"), mod_b_d).then_inc(sem("mod_b_in"), 16)
            C = MOD_POOL_COLS

            def load_pool(j):
                pool.dma_start(modw_pool[j % 2], mod_d[:, j * 1024:(j + 1) * 1024].rearrange("p (k c) -> p k c", k=KD)).then_inc(sem(f"modw_pool_in{j % 2}"), 16)

            def load_dve(j):
                if j:
                    wait("mod_dve_done", j)
                a = MOD_POOL * 1024 + j * 2048
                pool.dma_start(modw_dve, mod_d[:, a:a + 2048].rearrange("p (k c) -> p k c", k=KD)).then_inc(sem("modw_dve_in"), 16)

            def latent_roots():
                wait("squares_done", squares_at("lat", 7))
                rsqrt(RS_L, SS_L, 4, Q_RANK, "roots")
                rsqrt(RS_L + 4, SS_L + 4, 4, KV_RANK, "roots")

            def head_roots(h):
                wait("o_ss", h + 1)
                rsqrt(RS_H + 4 * (h % 2), SS_H + 4 * (h % 2), 4, P, "roots")

            load_pool(0)
            load_dve(0)
            load_pool(1)
            wait("cond_ready", 1)
            cb = st(CSILU, KD).unsqueeze(2).broadcast_to([P, KD, C])
            for j in range(MOD_POOL):
                w = modw_pool[j % 2]
                wait(f"modw_pool_in{j % 2}", 16 * (j // 2 + 1))
                link(nc.gpsimd.tensor_tensor(w, w, cb, ALU.mult))
                for n in (4, 2):
                    link(nc.gpsimd.tensor_tensor(w[:, 0:n, :], w[:, 0:n, :], w[:, n:2 * n, :], ALU.add))
                if j % 2 == 0 and j:
                    wait("mod_spilled", 16 * j // 2)
                nc.gpsimd.tensor_tensor(mod_part[:, j % 2 * C:(j % 2 + 1) * C], w[:, 0, :], w[:, 1, :],
                                        ALU.add).then_inc(sem("mod_pool_done"), 1)
                wait("mod_pool_done", j + 1)
                if j % 2:
                    pool.dma_start(mod_spill_d[:, (j - 1) * C:(j + 1) * C], mod_part[:]).then_inc(sem("mod_spilled"), 16)
                if j + 2 < MOD_POOL:
                    load_pool(j + 2)
                if j == ROOTS_AFTER[0]:
                    latent_roots()
                for h in range(HEADS):
                    if j == ROOTS_AFTER[1 + h]:
                        head_roots(h)
                if j in LOADS_AFTER:
                    load_dve(LOADS_AFTER.index(j) + 1)
            wait("o_turned", UNITS)
            nc.gpsimd.memset(ones_sq, 1.0).then_inc(sem("ones_ready"), 1)
            for m in range(TT + 1):
                if m < TT:
                    for i in (2 * m, 2 * m + 1):
                        n, t = i // 4, i % 4
                        wait("taps_scaled", i + 1)
                        h0, h1 = filt[2 * (i % 2)], filt[2 * (i % 2) + 1]
                        nc.gpsimd.tensor_tensor(taps(0, n)[:, t, :], h0, h1, ALU.add).then_inc(sem("taps_step"), 1)
                        nc.gpsimd.tensor_tensor(taps(1, n)[:, t, :], h0, h1, ALU.subtract).then_inc(sem("taps_ready"), 1)
                    wait("squares_done", squares_at("x1", m))
                    rsqrt(RS + m, SS + m, 1, D, "x_rs")
                if m:
                    wait("squares_done", squares_at("x2", m - 1))
                    rsqrt(RS2 + m - 1, SS2 + m - 1, 1, D, "x2_rs")
            def subtract(low, high):
                return nc.gpsimd.tensor_tensor(part(low), low, part(high), ALU.subtract)

            def split_low(p, past=0):
                wait("piece_high", past + (p + 1))
                subtract(*piece_parts(p)).then_inc(sem("piece_low"), 1)

            def hid_low_out(j):
                wait("hid_high", j + 1)
                subtract(hid[:, j, :], hid_high(j)).then_inc(sem("hid_low"), 1)

            for p in range(FIRST_HYZ, FIRST_HYX + PIECES + 2):
                split_low(p)
            for i in range(4):
                n, f = i // 2, i % 2
                kr, ks = km[:, f, n * 512:n * 512 + 512], km[:, 2 + f, n * 512:n * 512 + 512]
                wait("dft_read", i + 1)
                if i:
                    wait("uv_ready", i)
                link(nc.gpsimd.tensor_tensor(tmp[5], tmp[2], kr, ALU.mult))
                link(nc.gpsimd.tensor_tensor(tmp[6], tmp[3], ks, ALU.mult))
                link(nc.gpsimd.tensor_tensor(tmp[5], tmp[5], tmp[6], ALU.subtract))
                nc.gpsimd.tensor_tensor(tmp[6], tmp[2], ks, ALU.mult).then_inc(sem("w_ready"), 1)
                for t in hyx_tiles(i):
                    split_low(FIRST_HYX + PIECES + t)
            for k in range(KD):
                wait("y_high", k + 1)
                subtract(x0c[:, k, :], hT[:, k, :]).then_inc(sem("y_low"), 1)
            for p in range(FIRST_HYO + PIECES, FIRST_UP + 2):
                split_low(p)
            for m in range(TT):
                wait("squares_done", squares_at("x3", m))
                rsqrt(RS + m, SS + m, 1, D, "x_rs")

            split_low(FIRST_UP + 2)
            split_low(FIRST_UP + 3)

            def up_step(j, past=0):
                split_low(FIRST_UP + 2 * j + 4, 2 * past)
                if j >= 2:
                    wait("hid_high", past + (j - 1))
                    low = hid[:, past + (j - 2), :]
                    nc.gpsimd.tensor_tensor(part(hid)[:, past + (j - 2), :], low, part(hid_highs)[:, past + (j - 2), :],
                                            ALU.subtract).then_inc(sem("hid_low"), 1)
                split_low(FIRST_UP + 2 * j + 5, 2 * past)

            up_step(0)
            up_step(1)
            with nc.gpsimd.Fori(0, 13, 4) as past:
                for t in range(4):
                    up_step(2 + t, past)
            for j in range(18, KF):
                up_step(j)
            hid_low_out(KF - 2)
            hid_low_out(KF - 1)
            for p in range(FIRST_DOWN + 4, len(pieces)):
                split_low(p)
            for m in range(TT):
                wait("squares_done", squares_at("x4", m))
                rsqrt(RS_L + m, SS_L + m, 1, D, "x_rs")

        @block.vector
        def _(dve):
            steps = [0]
            V = nc.vector

            def wait(name, count):
                dve.wait_ge(sem(name), count)

            def link(ins):
                steps[0] += 1
                ins.then_inc(sem("dve_step"), 1)
                dve.wait_ge(sem("dve_step"), steps[0])

            def split_low(p):
                wait("piece_high", p + 1)
                low, high = piece_parts(p)
                V.tensor_tensor(part(low), low, part(high), ALU.subtract).then_inc(sem("piece_low"), 1)

            def wrap(r, a, k, quarter):
                link(V.tensor_scalar(k, a, 1.0 / TWO_PI, 0.25 * quarter, ALU.mult, ALU.add))
                link(V.tensor_scalar(k, k, ROUNDER, None, ALU.add))
                link(V.tensor_scalar(k, k, ROUNDER, None, ALU.subtract))
                link(V.scalar_tensor_tensor(out=r, in0=k, scalar=-PI_1, in1=a, op0=ALU.mult, op1=ALU.add))
                link(V.scalar_tensor_tensor(out=r, in0=k, scalar=-PI_2, in1=r, op0=ALU.mult, op1=ALU.add))
                link(V.scalar_tensor_tensor(out=r, in0=k, scalar=-PI_3, in1=r, op0=ALU.mult, op1=ALU.add))
                if quarter:
                    link(V.tensor_scalar(r, r, math.pi / 2, None, ALU.add))
                return V.tensor_scalar(r, r, PI_BELOW, -PI_BELOW, ALU.min, ALU.max)

            for m in range(TT):
                wait("roots", m + 1)
                V.tensor_scalar(x_sb[:, m, :], x_sb[:, m, :], st(RS + m), None, ALU.mult).then_inc(sem("n1_scaled"), 1)

            for k in range(KD):
                wait("n1_out", k + 1)
                V.tensor_copy(part(hT[:, k, :]), n1_temp[:, k, :]).then_inc(sem("input_split"), 1)
            for k in range(KD):
                wait("input_split", k + 1)
                wait("n1_turned", KD)
                V.tensor_tensor(part(x_low[:, k, :]), n1_temp[:, k, :], part(hT[:, k, :]), ALU.subtract).then_inc(sem("input_split"), 1)
                if k % 2:
                    split_low(k // 2)
            wait("input_split", 2 * KD)

            wait("rowed_in", 16)
            wait("pos_in", 16)
            ang = nsin_t
            posf = sums[:, 0:TT]
            link(V.tensor_copy(posf, pos_sb[:]))
            for m in range(TT):
                ins = V.tensor_scalar(ang[:, m * HALF:(m + 1) * HALF], rowed[:, ROWED["inv_freq"]], posf[:, m:m + 1], None, ALU.mult)
            link(ins)
            for i, t in enumerate((sin_t, cos_t)):
                wrap(t, ang, rope_tmp[:, 0:128], i).then_inc(sem("angle_ready"), 1)
            wait("rope_table", 1)
            wait("angle_ready", 2)
            link(V.tensor_scalar(nsin_t, sin_t, -1.0, None, ALU.mult))
            lam = rowed[:, ROWED["lam"]].rearrange("p (a b c) -> p a b c", a=2, b=2)
            prod = rope_tmp[:, 0:128].rearrange("p (a c) -> p a c", a=2)
            link(V.tensor_tensor(prod, lam[:, :, 0, :], lam[:, :, 1, :], ALU.mult))
            V.tensor_reduce(sums[:, 62:64], prod, AX.X, ALU.add).then_inc(sem("lambda_sums"), 1)

            def net_layer(i):
                wait("net_done", i + 1)
                if i:
                    wait("net_out", i)
                fb = early[0:FW, EARLY["f_b"]][:, i:i + 1]
                a, k, r = net[2][0:FW, :], net[3][0:FW, :], net[1][0:FW, :]
                V.tensor_scalar(a, bank[4][0:FW, :], fb, early[0:FW, EARLY["freq"]], ALU.add, ALU.mult).then_inc(sem("net_read"), 1)
                wait("net_read", i + 1)
                wrap(r, a, k, 0).then_inc(sem("net_angle"), 1)

            def mod_chunk(j):
                C = MOD_DVE_COLS
                wait("modw_dve_in", 16 * (j + 1))
                acc = mod_g[:].rearrange("p a b -> p (a b)")[:, j * C:(j + 1) * C]
                w = modw_dve
                for k in range(KD):
                    ins = V.scalar_tensor_tensor(out=acc, in0=w[:, k, :], scalar=st(CSILU + k), in1=acc, op0=ALU.mult, op1=ALU.add)
                    if k < KD - 1:
                        link(ins)
                ins.then_inc(sem("mod_dve_done"), 1)

            def table(t, m, groups, halves):
                v = t[:, m * HALF:(m + 1) * HALF]
                return v.unsqueeze(1).broadcast_to([P, groups * halves, HALF])

            def rope_tile(out, src, m, groups):
                o3 = out.rearrange("p (g c) -> p g c", c=HALF)
                s3 = src.rearrange("p (g c) -> p g c", c=HALF)
                t3 = rope_tmp[:, 0:groups * 64].rearrange("p (g two c) -> p two g c", two=2, c=HALF)
                s4 = src.rearrange("p (g two c) -> p two g c", two=2, c=HALF)
                link(V.tensor_tensor(o3, s3, table(cos_t, m, groups, 2), ALU.mult))
                link(V.tensor_tensor(t3[:, 0], s4[:, 1], table(nsin_t, m, groups, 1), ALU.mult))
                link(V.tensor_tensor(t3[:, 1], s4[:, 0], table(sin_t, m, groups, 1), ALU.mult))
                return V.tensor_tensor(out, out, rope_tmp[:, 0:groups * 64], ALU.add)

            wait("rope_table", 2)
            for p in range(4, 8):
                split_low(p)
            wait("mod_b_in", 16)
            wait("cond_ready", 1)
            mod_chunk(0)
            for i in range(8):
                wait("in_done", in_done_at(i))
                rope_tile(roped[i // 4][:, i % 4, :], in_bank(i), i % 4, 8).then_inc(sem("rope_out"), 1)
                split_low(8 + i)
                if i % 4 == 3:
                    mod_chunk(1 + i // 4)
            for p in range(16, 20):
                split_low(p)
            mod_chunk(3)
            for p in range(20, 24):
                split_low(p)
            mod_chunk(4)
            wait("lambda_exps", 1)
            link(V.tensor_scalar(st(NLAM), sums[:, 61:62], sums[:, 60:61], LAMBDA_INIT, ALU.subtract, ALU.subtract))
            wait("in_out", 12)
            wait("qk_turned", 8)
            for m in range(TT):
                link(rope_tile(kr2[:, m, 0:64], lat[:, m, 640:704], m, 1))
                ins = V.tensor_copy(kr2[:, m, 64:128], kr2[:, m, 0:64])
            ins.then_inc(sem("kr_ready"), 1)
            wait("roots", TT + 2)
            for s, (a, n) in enumerate(((0, Q_RANK), (Q_RANK, KV_RANK))):
                for m in range(TT):
                    ins = V.tensor_scalar(lat[:, m, a:a + n], lat[:, m, a:a + n], st(RS_L + 4 * s + m), None, ALU.mult)
                ins.then_inc(sem("lat_scaled"), 1)
            mod_chunk(5)
            for m in range(TT):
                wait("latq_done", m + 1)
                rope_tile(qr[:, m, :], bank[4 + m][:, 0:256], m, 4).then_inc(sem("qr_out"), 1)
            wait("dgate_out", TT)
            sub = rowed[:, ROWED["subln"]].unsqueeze(1).broadcast_to([P, HEADS, P])
            for m in range(TT):
                g = dgate[:, m, :].rearrange("p (h c) -> p h c", h=HEADS)
                V.scalar_tensor_tensor(out=g, in0=g, scalar=1.0 - LAMBDA_INIT, in1=sub, op0=ALU.mult,
                                       op1=ALU.mult).then_inc(sem("dgate_ready"), 1)
            for p in range(FIRST_MGATE, FIRST_GATE):
                split_low(p)

            def maxima(u):
                latent = u >= HEADS
                base, maps = 32 * (u % 2), 1 if latent else 2
                wait("scores_done", scores_at(u))

                def maximum(a, i):
                    b, c = score_place(a, i)
                    o = base + 16 + 4 * a + i
                    return V.tensor_reduce(sums[:, o:o + 1], bank[b][:, c:c + (i + 1) * P], AX.X, ALU.max)

                def negate(a):
                    V.tensor_scalar(sums[:, base + 4 * a:base + 4 * a + 4], sums[:, base + 16 + 4 * a:base + 20 + 4 * a],
                                    -(MLA_SCALE if latent else DIFF_SCALE), None, ALU.mult).then_inc(sem("neg_max"), 1)

                for i in range(TT):
                    ins = maximum(0, i)
                if not latent:
                    ins = maximum(1, 1)
                link(ins)
                negate(0)
                if not latent:
                    for i in (0, 2, 3):
                        ins = maximum(1, i)
                    link(ins)
                    negate(1)

            def combine(u):
                base = 32 * (u % 2)
                wait("exp_out", exps_before(u) + 4)
                r1, ratio = sums[:, base + 24:base + 28], sums[:, base + 28:base + 32]
                if u >= HEADS:
                    for i in range(TT):
                        V.reciprocal(r1[:, i:i + 1], sums[:, base + 8 + i:base + 9 + i]).then_inc(sem("probs_ready"), 1)
                    return
                weighted = sums[:, base + 16:base + 20]
                V.reciprocal(r1, sums[:, base + 8:base + 12])
                link(V.tensor_scalar(weighted, sums[:, base + 8:base + 12], st(NLAM), None, ALU.mult))
                wait("exp_out", exps_before(u + 1))
                link(V.reciprocal(ratio, sums[:, base + 12:base + 16]))
                link(V.tensor_tensor(ratio, ratio, weighted, ALU.mult))
                for i in range(TT):
                    s = slice(OFF[i], OFF[i] + (i + 1) * P)
                    V.scalar_tensor_tensor(out=probs1[u % 2][:, s], in0=probs2[:, s], scalar=ratio[:, i:i + 1],
                                           in1=probs1[u % 2][:, s], op0=ALU.mult, op1=ALU.add).then_inc(sem("probs_ready"), 1)

            def output(u):
                base = 32 * (u % 2)
                o = o_tok[u % 2]
                wait("pv_done", 4 * u + 4)
                if u >= 2:
                    wait("o_turned", u - 1)
                r1 = sums[:, base + 24:base + 28].unsqueeze(2).broadcast_to([P, TT, P])
                V.tensor_tensor(o, bank[7].rearrange("p (a b) -> p a b", a=TT), r1, ALU.mult).then_inc(sem("o_read"), 1)
                wait("o_read", u + 1)
                if u < HEADS:
                    link(V.tensor_tensor(o_sq, o, o, ALU.mult))
                    c = SS_H + 4 * (u % 2)
                    V.tensor_reduce(st(c, 4), o_sq, AX.X, ALU.add).then_inc(sem("o_ss"), 1)

            def gate_output(u):
                h, o = u % HEADS, o_tok[u % 2]
                if u < HEADS:
                    wait("roots", TT + 2 + u + 1)
                    r = st(RS_H + 4 * (u % 2), 4).unsqueeze(2).broadcast_to([P, TT, P])
                    link(V.tensor_tensor(o, o, r, ALU.mult))
                    g = dgate
                else:
                    wait("mgate_ready", 1)
                    g = mgate
                V.tensor_tensor(o, o, g[:, :, h * P:(h + 1) * P], ALU.mult).then_inc(sem("o_ready"), 1)

            def split_output(u):
                high, low = ((qn, dv) if u >= HEADS else (qT, kT))
                high, low = high[:, u % HEADS, :], low[:, u % HEADS, :]
                wait("oT_out", u + 1)
                V.tensor_tensor(part(low), low, part(high), ALU.subtract).then_inc(sem("oT_low"), 1)

            maxima(0)
            combine(0)
            mod_chunk(6)
            for u in range(UNITS):
                if u + 1 < UNITS:
                    maxima(u + 1)
                if u:
                    gate_output(u - 1)
                if u + 1 < UNITS:
                    combine(u + 1)
                output(u)
                if u >= 2:
                    split_output(u - 2)
                    split_low(FIRST_GATE + u - 2)
                elif u == 1:
                    mod_chunk(7)
            gate_output(UNITS - 1)
            split_output(UNITS - 2)
            for p in range(FIRST_GATE + 6, FIRST_PD + 4):
                split_low(p)
                if p == FIRST_GATE + 8:
                    split_output(UNITS - 1)
                if p - FIRST_GATE - 8 in NET_AFTER:
                    net_layer(NET_AFTER.index(p - FIRST_GATE - 8))

            wait("gate_out", 12)
            wait("sgd_ready", 1)
            for d in range(KD):
                wait("merge_done", d + 1)
                V.tensor_tensor(sgd[:, d, :], sgd[:, d, :], bank[d], ALU.mult).then_inc(sem("merge_out"), 1)
                if d % 2:
                    split_low(FIRST_PD + 4 + d // 2)
            for d in range(KD):
                wait("merge_done", KD + d + 1)
                wait("merge_out", KD + d)
                link(V.tensor_tensor(sgm[:, d, :], sgm[:, d, :], bank[d], ALU.mult))
                V.tensor_tensor(sgd[:, d, :], sgd[:, d, :], sgm[:, d, :], ALU.add).then_inc(sem("merge_out"), 1)

            wait("modc_done", 1)
            V.tensor_tensor(modc[:], bank[4][:, 0:4 * KD], small[:, SMALL["mod_b"]], ALU.add).then_inc(sem("modc_read"), 1)
            wait("modc_read", 1)
            for s, name in enumerate(("norm_g1", "norm_g2")):
                c = modc[:, (2 * s + 1) * KD:(2 * s + 2) * KD]
                ins = V.scalar_tensor_tensor(out=c, in0=c, scalar=1.0, in1=small[:, SMALL[name]], op0=ALU.add, op1=ALU.mult)
            ins.then_inc(sem("modc_ready"), 1)

            def add_abs(i):
                a = abs_sum[i // 4]
                wait("abs_ready", 2 * i + 2)
                link(V.tensor_tensor(a, a, abs_tap[0], ALU.add))
                V.tensor_tensor(a, a, abs_tap[1], ALU.add).then_inc(sem("abs_step"), 1)
                wait("abs_step", i + 1)

            def bias_tap(n):
                s = slice(n * 512, n * 512 + 512)
                wait("norm_done", n + 1)
                V.tensor_copy(norm_half[n], bank[3][0:1, :]).then_inc(sem("norm_read"), 1)
                wait("norm_read", n + 1)
                link(V.tensor_tensor(bias_row[:, s], bias_row[:, s], norm_half[n], ALU.mult))
                wait("taps_ready", 4 * n + 4)
                tap0 = taps(0, n)[0:1, 0, :]
                V.tensor_tensor(tap0, tap0, bias_row[:, s], ALU.add).then_inc(sem("bias_in_taps"), 1)

            wait("norm_row_in", 16)
            link(V.memset(abs_sum[0], 0.0))
            link(V.memset(abs_sum[1], 0.0))
            for m in range(TT + 2):
                if m == TT - 1:
                    wait("bias_in", 16)
                    bias_tap(0)
                if m < TT:
                    wait(f"x_in{m}", 32)
                    for i in (2 * m, 2 * m + 1):
                        s = slice((i % 2) * 512, (i % 2) * 512 + 512)
                        wait("wo_done", i + 1)
                        V.tensor_tensor(x_sb[:, m, s], x_sb[:, m, s], bank[i % 3], ALU.add).then_inc(sem("wo_out"), 1)
                        n, t = i // 4, i % 4
                        wait("taps_done", i + 1)
                        wait("decay_ready", i + 1)
                        if i >= 2:
                            wait("taps_ready", i - 1)
                        h0, h1 = filt[2 * (i % 2)], filt[2 * (i % 2) + 1]
                        b = 4 + 2 * (i % 2)
                        V.tensor_tensor(h0, bank[b], decay[i % 2], ALU.mult)
                        ins = V.tensor_tensor(h1, bank[b + 1], decay[i % 2], ALU.mult)
                        if t == 0:
                            link(ins)
                            ins = V.memset(h1[0:1, :], 0.0)
                        ins.then_inc(sem("taps_scaled"), 1)
                        if i:
                            add_abs(i - 1)
                elif m == TT:
                    add_abs(7)
                if 1 <= m <= TT:
                    wait("x_rs", m)
                    V.scalar_tensor_tensor(out=x_sb[:, m - 1, :], in0=x_sb[:, m - 1, :], scalar=st(RS + m - 1), in1=norm_row,
                                           op0=ALU.mult, op1=ALU.mult).then_inc(sem("x2_ready"), 1)
                if m >= 2:
                    wait("x2_rs", m - 1)
                    wait("x2_ready", m - 1)
                    V.tensor_scalar(x_norm[:, m - 2, :], x_sb[:, m - 2, :], st(RS2 + m - 2), None, ALU.mult).then_inc(sem("n2_scaled"), 1)
            def split_input(tag, x, ks):
                for k in ks:
                    wait(f"{tag}_out", k + 1)
                    V.tensor_copy(part(hT[:, k, :]), x[:, k, :]).then_inc(sem("input_split"), 1)
                for k in ks:
                    wait("input_split", split_at(tag, k, 0))
                    V.tensor_tensor(part(x[:, k, :]), x[:, k, :], part(hT[:, k, :]), ALU.subtract).then_inc(sem("input_split"), 1)

            for i in range(4):
                if i == 2:
                    bias_tap(1)
                    wait("kdft_read", 2)
                    split_input("n2", x_low, range(4))
                n, f = i // 2, i % 2
                b0 = KDFT_BANK[i]
                s = slice(n * 512, n * 512 + 512)
                wait("kdft_copied", 2 * i + 1)
                o_cos, o_sin = hT[:, 2 * i, :], hT[:, 2 * i + 1, :]
                V.tensor_tensor(kp[:, f, s], bank[b0], o_cos, ALU.add)
                V.tensor_tensor(km[:, f, s], bank[b0], o_cos, ALU.subtract)
                wait("kdft_copied", 2 * i + 2)
                V.tensor_tensor(kp[:, 2 + f, s], bank[b0 + 2], o_sin, ALU.add)
                V.tensor_tensor(km[:, 2 + f, s], bank[b0 + 2], o_sin, ALU.subtract).then_inc(sem("kdft_read"), 1)
                if i == 2:
                    wait("rnorm_done", 1)
                    V.reciprocal(st(RNORM, KD), bank[3][:, 0:KD]).then_inc(sem("rnorm_read"), 1)
                    wait("rnorm_read", 1)
                    link(V.tensor_scalar(st(RNORM, KD), st(RNORM, KD), 2.0 / (2 * SEQ), None, ALU.mult))

            wait("kdft_read", 4)
            split_input("n2", x_low, range(4, KD))

            wait("taps_done", 8)
            wait("squares_done", squares_at("x2", 3))
            for p in padded:
                V.memset(p[:, 0:1], 0.0)
                ins = V.memset(p[:, SEQ + 1:SEQ + 2], 0.0)
            ins.then_inc(sem("pads_ready"), 1)

            def short_conv(out, p, tile):
                w = lambda t: sm("hy_sc_w", 24 * t + tile)
                link(V.tensor_scalar(out, p[:, 0:SEQ], w(0), sm("hy_sc_b", tile), ALU.mult, ALU.add))
                link(V.scalar_tensor_tensor(out=out, in0=p[:, 1:SEQ + 1], scalar=w(1), in1=out, op0=ALU.mult, op1=ALU.add))
                return V.scalar_tensor_tensor(out=out, in0=p[:, 2:SEQ + 2], scalar=w(2), in1=out, op0=ALU.mult, op1=ALU.add)

            wait("pads_ready", 1)
            for i in range(16):
                c = i // 2
                wait("hyz_out", i + 1)
                if i % 2 == 0 and c:
                    wait("z_ready", c)
                short_conv((x1c, vc)[i % 2], padded[i % 2], (8, 16)[i % 2] + c).then_inc(sem("hyz_conv"), 1)
                if i % 2:
                    wait("hyz_conv", i + 1)
                    if c >= 2:
                        wait("z_turned", c - 1)
                    V.tensor_tensor(z_buf[c % 2], x1c, vc, ALU.mult).then_inc(sem("z_ready"), 1)

            def hyx_conv(i):
                wait("hyx_out", i + 1)
                short_conv(x0c[:, i, :], padded[0], i).then_inc(sem("hyx_conv"), 1)

            def inverse_out(n):
                for q in range(4):
                    i = 4 * n + q
                    wait("y_done", i + 1)
                    x = x0c[:, i, :].rearrange("p (t two) -> p two t", two=2)
                    y = bank[6 + i % 2].rearrange("p (two t) -> p two t", two=2)
                    V.scalar_tensor_tensor(out=x, in0=y, scalar=st(RNORM + i), in1=x, op0=ALU.mult,
                                           op1=ALU.mult).then_inc(sem("y_out"), 1)

            hyx_conv(0)
            hyx_conv(1)
            for i in range(4):
                n, f = i // 2, i % 2
                s = slice(n * 512, n * 512 + 512)
                kr, ks = kp[:, f, s], kp[:, 2 + f, s]
                ur, us, vr, vs = (uv[:, 2 * c + f, :] for c in range(4))
                e_cos, e_sin = bank[0], bank[2]
                sr, ss, dr, ds, yr, wr, ws = tmp
                wait("dft_copied", 2 * i + 1)
                link(V.tensor_tensor(dr, e_cos, sr, ALU.subtract))
                link(V.tensor_tensor(sr, e_cos, sr, ALU.add))
                wait("dft_copied", 2 * i + 2)
                link(V.tensor_tensor(ds, e_sin, ss, ALU.subtract))
                V.tensor_tensor(ss, e_sin, ss, ALU.add).then_inc(sem("dft_read"), 1)
                wait("dft_read", i + 1)
                if n:
                    wait("y_done", 4)
                V.tensor_tensor(yr, sr, kr, ALU.mult)
                link(V.tensor_tensor(ur, ss, ks, ALU.mult))
                V.tensor_tensor(us, sr, ks, ALU.mult)
                link(V.tensor_tensor(yr, yr, ur, ALU.subtract))
                link(V.tensor_tensor(sr, ss, kr, ALU.mult))
                V.tensor_tensor(sr, sr, us, ALU.add)
                link(V.tensor_tensor(ss, ds, km[:, f, s], ALU.mult))
                wait("w_ready", i + 1)
                link(V.tensor_tensor(ws, ws, ss, ALU.add))
                V.tensor_tensor(ur, yr, wr, ALU.add)
                V.tensor_tensor(vr, yr, wr, ALU.subtract)
                V.tensor_tensor(us, sr, ws, ALU.add)
                V.tensor_tensor(vs, sr, ws, ALU.subtract).then_inc(sem("uv_ready"), 1)
                for t in hyx_tiles(i):
                    hyx_conv(t)
                if i % 2:
                    wait("hyx_conv", 2 * i + 2)
                    wait("dve_step", steps[0])
                    inverse_out(n)
            wait("b_out_in", 16)
            for i in range(2 * TT + 1):
                if i < 2 * TT:
                    n, m = i // TT, i % TT
                    s = slice(n * 512, n * 512 + 512)
                    t = tmp[i % 2]
                    if n == 0:
                        wait(f"x_in{m}", 48)
                    wait("hyo_done", 16 * n + tile_done(4, m, 2))
                    link(V.tensor_tensor(t, bank[i], row[:, s], ALU.add))
                    link(V.tensor_tensor(t, t, mod_g[:, 0, s], ALU.mult))
                    V.tensor_tensor(x_sb[:, m, s], x_sb[:, m, s], t, ALU.add).then_inc(sem("hyo_out"), 1)
                if i > TT:
                    m = i - TT - 1
                    wait("x_rs", TT + m + 1)
                    wait("hyo_out", i)
                    V.tensor_scalar(x_norm[:, m, :], x_sb[:, m, :], st(RS + m), None, ALU.mult).then_inc(sem("n3_scaled"), 1)

            split_input("n3", hT_low, range(KD))

            for im in image:
                V.memset(im[:, 0, :], 0.0)
                V.memset(im[:, ROWS + 1, :], 0.0)
                V.memset(im[:, 1:ROWS + 1, 0:1], 0.0)
                ins = V.memset(im[:, 1:ROWS + 1, COLS + 1:COLS + 2], 0.0)
            ins.then_inc(sem("borders_ready"), 1)

            def conv_step(j, past=0):
                wait("image_out", past + (j + 1))
                if j >= 2:
                    wait("hid_out", past + (j - 1))
                out = conv[j % 2].rearrange("p (r c) -> p r c", c=COLS)
                for t in range(9):
                    src = image[j % 2][:, t // 3:t // 3 + ROWS, t % 3:t % 3 + COLS]
                    w = small[:, bass.ds(past + (SMALL["conv_w"].start + t * KF + j), 1)]
                    if t == 0:
                        b = small[:, bass.ds(past + (SMALL["conv_b"].start + j), 1)]
                        ins = V.tensor_scalar(out, src, w, b, ALU.mult, ALU.add)
                    else:
                        dve.wait_ge(sem("tap_added"), 8 * past + (8 * j + t))
                        ins = V.scalar_tensor_tensor(out=out, in0=src, scalar=w, in1=out, op0=ALU.mult, op1=ALU.add)
                    ins.then_inc(sem("tap_added" if t < 8 else "conv_done"), 1)

            def gate_step(j, past=0):
                wait("silu_out", past + (j + 1))
                wait("up_done", 2 * past + (2 * j + 2))
                V.tensor_tensor(hid[:, past + j, :], conv[j % 2], bank[(2 * j + 5) % 8], ALU.mult).then_inc(sem("hid_out"), 1)

            conv_step(0)
            conv_step(1)
            gate_step(0)
            with nc.vector.Fori(0, KF - 5, 4) as past:
                for t in range(4):
                    conv_step(2 + t, past)
                    gate_step(1 + t, past)
            gate_step(KF - 1)
            for i in range(2 * TT + 1):
                if i < 2 * TT:
                    n, m = i // TT, i % TT
                    wait("down_done", n * TT * KF // 2 + tile_done(KF // 2, m, 2))
                    s = slice(n * 512, n * 512 + 512)
                    t = conv[m % 2]
                    link(V.tensor_tensor(t, bank[i], mod_g[:, 1, s], ALU.mult))
                    V.tensor_tensor(x_sb[:, m, s], x_sb[:, m, s], t, ALU.add).then_inc(sem("down_out"), 1)
                if i == TT:
                    wait("final_g_in", 16)
                if i > TT:
                    m = i - TT - 1
                    wait("x_rs", 2 * TT + m + 1)
                    wait("down_out", i)
                    V.scalar_tensor_tensor(out=out_tok[m], in0=x_sb[:, m, :], scalar=st(RS_L + m), in1=row[:],
                                           op0=ALU.mult, op1=ALU.mult).then_inc(sem("y_ready"), 1)


def _times():
    return np.concatenate([np.arange(0, SEQ, 2), np.arange(1, SEQ, 2)])


def _filter_constants():
    t = np.linspace(0.0, 1.0, SEQ, dtype=np.float32)
    w = (2.0 * math.pi * np.arange(SEQ, dtype=np.float32) / SEQ).astype(np.float32)
    bands = np.linspace(1e-4, BANDS - 1, BANDS, dtype=np.float32)
    angle = (bands[:, None] * w[None, :]).astype(np.float32).astype(np.float64)
    pos = np.concatenate([t[None, :], np.cos(angle), -np.sin(angle)]).astype(np.float32)
    deltas = np.abs(np.linspace(math.log(1e-2) / 1.5, math.log(1e-2) / 0.3, D, dtype=np.float32))
    order = _times()
    return pos[:, order], -t[order].reshape(TT, P).T, deltas[None, :].astype(np.float32)


def _transform_tables():
    t = _times().astype(np.int64)
    k = np.arange(NF, dtype=np.int64)
    angle = np.pi * ((2 * k[None, :] + 1) * t[:, None] % (4 * SEQ)) / (2 * SEQ)
    tables = []
    for f in (np.cos, np.sin):
        tables.append(f(angle).reshape(4, P, NF).transpose(1, 0, 2).reshape(P, 4 * NF))
    for f in (np.cos, np.sin):
        by_f = f(angle).T
        tables.append(by_f.reshape(2, P, 2, NF).transpose(1, 2, 0, 3).reshape(P, 4 * NF))
    return np.concatenate(tables, axis=1).astype(np.float32)


def _by_feature(v, n):
    return v.reshape(n, P).T


def kernel(**inputs):
    import concourse.bacc as _bacc
    from concourse.bass_utils import run_bass_kernel_spmd as _run
    import ml_dtypes

    a = {k: np.asarray(v) for k, v in inputs.items()}
    f32 = np.float32
    w_in = a["w_in"][0]
    pos_emb, minus_t, deltas = _filter_constants()

    stream = np.zeros((N_CHUNKS, P, SLOT), f32)

    def put(c, w):
        n, width = w.shape[0] // P, w.shape[1]
        stream[c, :, 0:n * width] = w.reshape(n, P, width).transpose(1, 0, 2).reshape(P, n * width)

    put(C_DQ, w_in[:, 0:512])
    put(C_DK, w_in[:, 512:1024])
    put(C_DV, w_in[:, 1024:1536])
    put(C_DGATE, w_in[:, 1536:2048])
    put(C_LAT0, w_in[:, 2048:2400])
    put(C_LAT1, w_in[:, 2400:2752])
    put(C_MGATE, w_in[:, 2752:3264])
    for i, c in enumerate((C_GD0, C_GD1, C_GM0, C_GM1)):
        put(c, w_in[:, 3264 + 512 * i:3776 + 512 * i])
    uq = a["w_uq"][0].reshape(Q_RANK, HEADS, 192)
    put(C_UQ, np.concatenate([uq[:, :, 0:128].reshape(Q_RANK, 512), uq[:, :, 128:].reshape(Q_RANK, 256)], axis=1))
    ukv = a["w_ukv"][0].reshape(KV_RANK, HEADS, 256)
    put(C_UKV, np.concatenate([ukv[:, :, 0:128].reshape(KV_RANK, 512), ukv[:, :, 128:].reshape(KV_RANK, 512)], axis=1))
    put(C_PD, a["w_proj_diff"][0])
    put(C_PM, a["w_proj_mla"][0])
    for n in range(2):
        put(C_WO0 + n, a["w_out"][0][:, 512 * n:512 * n + 512])
        put(C_HYO + n, a["hy_w_out_2"][0][:, 512 * n:512 * n + 512])
    stream[C_FOUT, 0:FW, 0:2 * D] = a["hy_f_wout_2"][0]
    hy = a["hy_w_in_2"][0]
    for c in range(4):
        tiles = [8 + 2 * c, 16 + 2 * c, 9 + 2 * c, 17 + 2 * c]
        put(C_HYZ0 + c, np.concatenate([hy[:, t * P:(t + 1) * P] for t in tiles], axis=1))
    for c in range(2):
        put(C_HYX0 + c, hy[:, 512 * c:512 * c + 512])
    up = a["ffn_w_up_2"][0]
    for c in range(KF // 2):
        cols = []
        for j in (2 * c, 2 * c + 1):
            cols += [up[:, FFN + j * P:FFN + (j + 1) * P], up[:, j * P:(j + 1) * P]]
        put(C_UP + c, np.concatenate(cols, axis=1))
    down = a["ffn_w_down_2"][0]
    for n in range(2):
        k0 = 0
        for q, k in enumerate(DOWN_K):
            put(C_DOWN + 3 * n + q, down[k0 * P:(k0 + k) * P, 512 * n:512 * n + 512])
            k0 += k

    def mod_part(w, width):
        n = w.shape[1] // width
        return w.reshape(KD, P, n, width).transpose(1, 2, 0, 3).reshape(P, n * KD * width)

    by_use = np.concatenate([np.arange(i * D, (i + 1) * D) for i in (0, 1, 3, 4, 2, 5)])
    mod_w = a["mod_w_2"][0][:, by_use]
    mod = np.concatenate([mod_part(mod_w[:, 0:4 * D], MOD_POOL_COLS), mod_part(mod_w[:, 4 * D:], MOD_DVE_COLS)], axis=1)

    small = np.zeros((P, N_SMALL), f32)
    for name, v, n in (("norm_in", a["norm_in"][0], KD), ("norm_g1", a["norm_g_2"][0, 0], KD),
                       ("norm_g2", a["norm_g_2"][0, 1], KD), ("q_norm", a["mla_q_norm"][0], KQ),
                       ("kv_norm", a["mla_kv_norm"][0], KKV), ("hy_b_in", a["hy_b_in_2"][0], 24),
                       ("hy_sc_w", a["hy_sc_w_2"][0].reshape(-1), 72), ("hy_sc_b", a["hy_sc_b_2"][0], 24),
                       ("conv_w", a["ffn_conv_w_2"][0].reshape(-1), 9 * KF), ("conv_b", a["ffn_conv_b_2"][0], KF),
                       ("cond", a["c_2"][0], KD), ("mod_b", a["mod_b_2"][0, by_use[0:4 * D]], 4 * KD)):
        small[:, SMALL[name]] = _by_feature(v, n)
    small[:, SMALL["minus_t"]] = minus_t
    small[:, SMALL["ident"]] = np.eye(P, dtype=f32)
    early = np.zeros((P, N_EARLY), f32)
    early[0:EMB, EARLY["pos_emb"]] = pos_emb
    early[0:EMB, EARLY["f_w1"]] = a["hy_f_w1_2"][0]
    early[0:FW, EARLY["f_w2"]] = a["hy_f_w2_2"][0]
    early[0:FW, EARLY["f_w3"]] = a["hy_f_w3_2"][0]
    for i in range(3):
        early[0:FW, EARLY["f_b"].start + i] = a[f"hy_f_b{i + 1}_2"][0]
    early[0:FW, EARLY["freq"].start] = a["hy_freq_2"][0]
    rowed = np.zeros((P, N_ROWED), f32)
    rowed[:, ROWED["inv_freq"]] = (10000.0 ** (-np.arange(0, 64, 2, dtype=f32) / 64)).astype(f32)[None, :]
    rowed[:, ROWED["lam"]] = np.concatenate([a["diff_lambda_q1"][0], a["diff_lambda_k1"][0],
                                             a["diff_lambda_q2"][0], a["diff_lambda_k2"][0]])[None, :]
    rowed[:, ROWED["subln"]] = a["diff_subln"][0][None, :]
    masks = np.zeros((P, 2, P), f32)
    masks[:, 0, :] = np.eye(P)
    masks[:, 1, :] = np.where(np.arange(P)[None, :] > np.arange(P)[:, None], MASKED, 0.0)
    rows = np.stack([a["norm_final"], a["hy_b_out_2"][0], a["final_g_2"], a["hy_bias_2"][0]])

    arrays = {
        "x_in": a["x"][0], "pos_in": np.ascontiguousarray(a["positions"][0].reshape(TT, P).T.astype(np.int32)),
        "weights_in": stream, "mod_w_in": mod, "mod_b_in": a["mod_b_2"][:, by_use[4 * D:]], "small_in": small, "early_in": early,
        "rowed_in": rowed, "masks_in": masks.reshape(P, 2 * P).astype(ml_dtypes.bfloat16),
        "tables_in": _transform_tables(), "deltas_in": deltas, "rows_in": rows,
    }
    arrays = {k: np.ascontiguousarray(v) for k, v in arrays.items()}
    nc = _bacc.Bacc("TRN2", target_bir_lowering=False, num_devices=1)
    args = [nc.dram_tensor(k, v.shape, mybir.dt.from_np(v.dtype), kind="ExternalInput").ap() for k, v in arrays.items()]
    out = nc.dram_tensor("y_out", (SEQ, D), F32, kind="ExternalOutput").ap()
    spill = nc.dram_tensor("x_spill", (SEQ, D), F32, kind="Internal").ap()
    mod_spill = nc.dram_tensor("mod_spill", (P, 4 * D), F32, kind="Internal").ap()
    build_program(nc, *args, spill, mod_spill, out)
    r = _run(nc, [arrays], core_ids=[0])
    return r.results[0]["y_out"].reshape(1, SEQ, D)
```
